# Optimizing a Trainium2 kernel written in Bass

```python
import jax, jax.numpy as jnp
from jax import lax
import numpy as np

D_MODEL = 1024
BATCH = 1
SEQ = 256
DEPTH = 2

GRID_W = 64
CTX_LEN = 256
N_MOD = 6
EPS = 1e-6
N_EVEN = (DEPTH + 1) // 2
N_ODD = DEPTH // 2
MLA_HEADS = 8
MLA_NOPE = 64
MLA_ROPE = 32
MLA_V = 64
MLA_Q_RANK = 256
MLA_KV_RANK = 128
MLA_SCALE = (MLA_NOPE + MLA_ROPE) ** -0.5
CONV_CH = 512
CONV_WIDTH = 31
AB_IN = MLA_Q_RANK + MLA_KV_RANK + MLA_ROPE + 2 * CONV_CH
AB_MIX = MLA_HEADS * MLA_V + CONV_CH
ROPE_BASE = 10000.0
Q_BLOCK = 128
HG_HEADS = 8
HG_DK = 128
HG_DV = D_MODEL // HG_HEADS
HG_F = HG_HEADS * HG_DK
HG_V = HG_HEADS * HG_DV
HG_IN = 3 * HG_F + 2 * HG_V
HG_CHUNK = 64
PEER_HEADS = 8
PEER_NKEYS = 128
PEER_EXPERTS = PEER_NKEYS * PEER_NKEYS
PEER_QDIM = 256
PEER_HALF = PEER_QDIM // 2
PEER_TOPK = 16
PEER_BLOCK = 128

kernel_name = 'hybrid_mla_conformer_hgrn2_peer_block'

def rms_norm(x, g):
    xf = x.astype(jnp.float32)
    y = xf * lax.rsqrt(jnp.mean(xf * xf, axis=-1, keepdims=True) + EPS)
    return (y * g.astype(jnp.float32)).astype(x.dtype)

def layer_norm(x, g, b):
    xf = x.astype(jnp.float32)
    mu = jnp.mean(xf, axis=-1, keepdims=True)
    xc = xf - mu
    y = xc * lax.rsqrt(jnp.mean(xc * xc, axis=-1, keepdims=True) + EPS)
    return (y * g.astype(jnp.float32) + b.astype(jnp.float32)).astype(x.dtype)

def modulate(h, shift, scale):
    return h * (1 + scale) + shift

def axial_rope_tables(n_tokens):
    rows = n_tokens // GRID_W
    row = jnp.repeat(jnp.arange(rows, dtype=jnp.float32), GRID_W)
    col = jnp.tile(jnp.arange(GRID_W, dtype=jnp.float32), rows)
    axis_dim = MLA_ROPE // 2
    inv = ROPE_BASE ** (-jnp.arange(0, axis_dim, 2, dtype=jnp.float32) / axis_dim)
    ang = jnp.concatenate([row[:, None] * inv, col[:, None] * inv], axis=-1)
    return jnp.cos(ang), jnp.sin(ang)

def apply_rope(x, cos, sin):
    xp = x.astype(jnp.float32).reshape(x.shape[:-1] + (x.shape[-1] // 2, 2))
    x0, x1 = xp[..., 0], xp[..., 1]
    out = jnp.stack([x0 * cos - x1 * sin, x0 * sin + x1 * cos], axis=-1)
    return out.reshape(x.shape).astype(x.dtype)

def mla_queries(cq, q_g, w_uq):
    B, T = cq.shape[:2]
    return (rms_norm(cq, q_g) @ w_uq).reshape(B, T, MLA_HEADS, MLA_NOPE + MLA_ROPE)

def mla_keys_values(ckv, k_rope, kv_g, w_ukv):
    B, T = ckv.shape[:2]
    kv = (rms_norm(ckv, kv_g) @ w_ukv).reshape(B, T, MLA_HEADS, MLA_NOPE + MLA_V)
    k = jnp.concatenate([kv[..., :MLA_NOPE], jnp.broadcast_to(k_rope[:, :, None, :], (B, T, MLA_HEADS, MLA_ROPE))], axis=-1)
    return k, kv[..., MLA_NOPE:]

def attend(q, k, v):
    s = jnp.einsum('bqhd,bkhd->bhqk', q, k).astype(jnp.float32) * MLA_SCALE
    p = jax.nn.softmax(s, axis=-1).astype(v.dtype)
    return jnp.einsum('bhqk,bkhd->bqhd', p, v)

def blocked_attention(q, k, v):
    B, T, H, dq = q.shape
    nb = T // Q_BLOCK
    qb = q.reshape(B, nb, Q_BLOCK, H, dq).transpose(1, 0, 2, 3, 4)
    ob = lax.map(lambda qi: attend(qi, k, v), qb)
    return ob.transpose(1, 0, 2, 3, 4).reshape(B, T, H, v.shape[-1])

def conformer_conv(u, conv_w, conv_b, ln_g, ln_b):
    a, gt = jnp.split(u, 2, axis=-1)
    y = a * jax.nn.sigmoid(gt)
    y = lax.conv_general_dilated(y, conv_w[:, None, :], window_strides=(1,),
                                 padding=[(CONV_WIDTH // 2, CONV_WIDTH // 2)],
                                 dimension_numbers=('NWC', 'WIO', 'NWC'),
                                 feature_group_count=CONV_CH) + conv_b
    return jax.nn.silu(layer_norm(y, ln_g, ln_b))

def mla_conv_mixer(h, hc, need_ctx_out, w_in, q_g, w_uq, kv_g, w_ukv, conv_w, conv_b, ln_g, ln_b, w_out):
    B, T = h.shape[:2]
    splits = [MLA_Q_RANK, MLA_Q_RANK + MLA_KV_RANK, MLA_Q_RANK + MLA_KV_RANK + MLA_ROPE]
    cq, ckv, kr, cu = jnp.split(h @ w_in, splits, axis=-1)
    cqc, ckvc, krc, cuc = jnp.split(hc @ w_in, splits, axis=-1)
    cos, sin = axial_rope_tables(T)
    q = mla_queries(cq, q_g, w_uq)
    q = jnp.concatenate([q[..., :MLA_NOPE], apply_rope(q[..., MLA_NOPE:], cos[:, None], sin[:, None])], axis=-1)
    k, v = mla_keys_values(ckv, apply_rope(kr, cos, sin), kv_g, w_ukv)
    kc, vc = mla_keys_values(ckvc, krc, kv_g, w_ukv)
    o = blocked_attention(q, jnp.concatenate([kc, k], axis=1), jnp.concatenate([vc, v], axis=1))
    y = jnp.concatenate([o.reshape(B, T, -1), conformer_conv(cu, conv_w, conv_b, ln_g, ln_b)], axis=-1) @ w_out
    if not need_ctx_out:
        return y, None
    oc = attend(mla_queries(cqc, q_g, w_uq), kc, vc)
    yc = jnp.concatenate([oc.reshape(B, hc.shape[1], -1), conformer_conv(cuc, conv_w, conv_b, ln_g, ln_b)], axis=-1) @ w_out
    return y, yc

def hgrn_lower_bounds(lb_param):
    p = jax.nn.softmax(lb_param.astype(jnp.float32), axis=0)
    cum = jnp.cumsum(p, axis=0)
    return cum - cum[0]

def gla_chunked(q, k, v, logf, s0):
    B, T, H, DK = q.shape
    DV = v.shape[-1]
    C = HG_CHUNK
    n = T // C
    q, k, v, logf = [a.reshape(B, n, C, H, a.shape[-1]) for a in (q, k, v, logf)]
    b = jnp.cumsum(logf, axis=2)
    b_last = b[:, :, -1:]
    q_in = q * jnp.exp(b)
    k_in = k * jnp.exp(-b)
    k_out = k * jnp.exp(b_last - b)
    mask = jnp.tril(jnp.ones((C, C), dtype=bool))
    a = jnp.where(mask, jnp.einsum('bnthk,bnshk->bnhts', q_in, k_in), 0.0)
    o_intra = jnp.einsum('bnhts,bnshv->bnthv', a, v)
    ds = jnp.einsum('bnshk,bnshv->bnhkv', k_out, v)
    decay = jnp.exp(b_last[:, :, 0])

    def step(s, inp):
        d, dsn = inp
        return d[..., None] * s + dsn, s

    s_final, s_prev = lax.scan(step, s0, (jnp.moveaxis(decay, 1, 0), jnp.moveaxis(ds, 1, 0)))
    s_prev = jnp.moveaxis(s_prev, 0, 1)
    o_inter = jnp.einsum('bnthk,bnhkv->bnthv', q_in, s_prev)
    return (o_intra + o_inter).reshape(B, T, H, DV), s_final

def hgrn_mixer(h, hc, layer_idx, need_ctx_out, w_in, lb_param, norm_g, w_out):
    lb = hgrn_lower_bounds(lb_param)[layer_idx]

    def heads(a, d):
        return a.reshape(a.shape[:2] + (HG_HEADS, d))

    def prep(hh):
        p = (hh @ w_in).astype(jnp.float32)
        q, zf, zb, i, g = jnp.split(p, [HG_F, 2 * HG_F, 3 * HG_F, 3 * HG_F + HG_V], axis=-1)
        ff = lb[0] + (1.0 - lb[0]) * jax.nn.sigmoid(zf)
        fb = lb[1] + (1.0 - lb[1]) * jax.nn.sigmoid(zb)
        fwd = (heads(jnp.log(ff), HG_DK), heads(1.0 - ff, HG_DK))
        bwd = (heads(jnp.log(fb), HG_DK), heads(1.0 - fb, HG_DK))
        return heads(q, HG_DK), heads(i, HG_DV), g, fwd, bwd

    def flip(a):
        return jnp.flip(a, axis=1)

    def readout(o, g, dtype):
        on = rms_norm(o, jnp.ones((HG_DV,), jnp.float32)).reshape(o.shape[:2] + (HG_V,))
        return ((on * norm_g * jax.nn.silu(g)).astype(dtype)) @ w_out

    B = h.shape[0]
    s0 = jnp.zeros((B, HG_HEADS, HG_DK, HG_DV), jnp.float32)
    qc, ic, gc, (lfc, kfc), (lbc, kbc) = prep(hc)
    oc_f, sc_f = gla_chunked(qc, kfc, ic, lfc, s0)
    oc_b, sc_b = gla_chunked(flip(qc), flip(kbc), flip(ic), flip(lbc), s0)
    q, i, g, (lf, kf), (lbk, kb) = prep(h)
    o_f, _ = gla_chunked(q, kf, i, lf, sc_f)
    o_b, _ = gla_chunked(flip(q), flip(kb), flip(i), flip(lbk), sc_b)
    y = readout(o_f + flip(o_b), g, h.dtype)
    if not need_ctx_out:
        return y, None
    return y, readout(oc_f + flip(oc_b), gc, hc.dtype)

def peer_ffn(h, w_q, sub_keys, u, v):
    shp = h.shape
    x = h.reshape(-1, shp[-1])
    n = x.shape[0]
    q = (x @ w_q).reshape(n, PEER_HEADS, 2, PEER_HALF)
    s = jnp.einsum('nhpd,hpkd->nhpk', q, sub_keys).astype(jnp.float32)
    sv, si = lax.top_k(s, PEER_TOPK)
    cand = (sv[:, :, 0, :, None] + sv[:, :, 1, None, :]).reshape(n, PEER_HEADS, PEER_TOPK * PEER_TOPK)
    cidx = (si[:, :, 0, :, None] * PEER_NKEYS + si[:, :, 1, None, :]).reshape(n, PEER_HEADS, PEER_TOPK * PEER_TOPK)
    top_s, pos = lax.top_k(cand, PEER_TOPK)
    eidx = jnp.take_along_axis(cidx, pos, axis=-1)
    gate = jax.nn.softmax(top_s, axis=-1).astype(x.dtype)
    nb = n // PEER_BLOCK

    def block(args):
        xb, eb, gb = args
        act = jax.nn.gelu(jnp.einsum('nd,nhkd->nhk', xb, u[eb]), approximate=False)
        return jnp.einsum('nhk,nhkd->nd', gb * act, v[eb])

    y = lax.map(block, (x.reshape(nb, PEER_BLOCK, shp[-1]),
                        eidx.reshape(nb, PEER_BLOCK, PEER_HEADS, PEER_TOPK),
                        gate.reshape(nb, PEER_BLOCK, PEER_HEADS, PEER_TOPK)))
    return y.reshape(shp)

def setup_inputs(seed: int = 0) -> dict:
    key = jax.random.key(seed)
    ks = iter(jax.random.split(key, 32))

    def nrm(shape, scale):
        return jax.random.normal(next(ks), shape, jnp.float32) * scale

    def gain(shape):
        return 1.0 + nrm(shape, 0.02)

    d = D_MODEL
    return {
        'x': nrm((BATCH, SEQ, d), 1.0),
        'c': nrm((BATCH, d), 1.0),
        'ctx': nrm((BATCH, CTX_LEN, d), 1.0),
        'c_ctx': nrm((d,), 1.0),
        'ada_w': nrm((DEPTH, d, N_MOD * d), 0.5 * d ** -0.5),
        'ada_b': nrm((DEPTH, N_MOD * d), 0.02),
        'norm1_g': gain((DEPTH, d)),
        'norm2_g': gain((DEPTH, d)),
        'ab_w_in': nrm((N_EVEN, d, AB_IN), d ** -0.5),
        'mla_q_norm_g': gain((N_EVEN, MLA_Q_RANK)),
        'mla_w_uq': nrm((N_EVEN, MLA_Q_RANK, MLA_HEADS * (MLA_NOPE + MLA_ROPE)), MLA_Q_RANK ** -0.5),
        'mla_kv_norm_g': gain((N_EVEN, MLA_KV_RANK)),
        'mla_w_ukv': nrm((N_EVEN, MLA_KV_RANK, MLA_HEADS * (MLA_NOPE + MLA_V)), MLA_KV_RANK ** -0.5),
        'conv_w': nrm((N_EVEN, CONV_WIDTH, CONV_CH), CONV_WIDTH ** -0.5),
        'conv_b': nrm((N_EVEN, CONV_CH), 0.02),
        'conv_ln_g': gain((N_EVEN, CONV_CH)),
        'conv_ln_b': nrm((N_EVEN, CONV_CH), 0.02),
        'ab_w_out': nrm((N_EVEN, AB_MIX, d), AB_MIX ** -0.5),
        'hg_w_in': nrm((N_ODD, d, HG_IN), d ** -0.5),
        'hg_lower_bound': nrm((DEPTH, 2, HG_F), 0.1),
        'hg_norm_g': gain((N_ODD, HG_V)),
        'hg_w_out': nrm((N_ODD, HG_V, d), HG_V ** -0.5),
        'peer_w_q': nrm((DEPTH, d, PEER_HEADS * PEER_QDIM), d ** -0.5),
        'peer_sub_keys': nrm((DEPTH, PEER_HEADS, 2, PEER_NKEYS, PEER_HALF), PEER_HALF ** -0.5),
        'peer_u': nrm((DEPTH, PEER_EXPERTS, d), d ** -0.5),
        'peer_v': nrm((DEPTH, PEER_EXPERTS, d), 0.25),
        'final_norm_g': gain((d,)),
    }

def reference(x, c, ctx, c_ctx, ada_w, ada_b, norm1_g, norm2_g, ab_w_in, mla_q_norm_g, mla_w_uq,
              mla_kv_norm_g, mla_w_ukv, conv_w, conv_b, conv_ln_g, conv_ln_b, ab_w_out, hg_w_in,
              hg_lower_bound, hg_norm_g, hg_w_out, peer_w_q, peer_sub_keys, peer_u, peer_v, final_norm_g):
    xc = ctx
    sc = jax.nn.silu(c)
    scc = jax.nn.silu(c_ctx)
    for l in range(DEPTH):
        need_ctx = l < DEPTH - 1
        mod = jnp.split((sc @ ada_w[l] + ada_b[l])[:, None, :], N_MOD, axis=-1)
        modc = jnp.split(scc @ ada_w[l] + ada_b[l], N_MOD, axis=-1)
        h = modulate(rms_norm(x, norm1_g[l]), mod[0], mod[1])
        hc = modulate(rms_norm(xc, norm1_g[l]), modc[0], modc[1])
        if l % 2 == 0:
            e = l // 2
            y, yc = mla_conv_mixer(h, hc, need_ctx, ab_w_in[e], mla_q_norm_g[e], mla_w_uq[e], mla_kv_norm_g[e],
                                   mla_w_ukv[e], conv_w[e], conv_b[e], conv_ln_g[e], conv_ln_b[e], ab_w_out[e])
        else:
            o = l // 2
            y, yc = hgrn_mixer(h, hc, l, need_ctx, hg_w_in[o], hg_lower_bound, hg_norm_g[o], hg_w_out[o])
        x = x + mod[2] * y
        h2 = modulate(rms_norm(x, norm2_g[l]), mod[3], mod[4])
        x = x + mod[5] * peer_ffn(h2, peer_w_q[l], peer_sub_keys[l], peer_u[l], peer_v[l])
        if need_ctx:
            xc = xc + modc[2] * yc
            hc2 = modulate(rms_norm(xc, norm2_g[l]), modc[3], modc[4])
            xc = xc + modc[5] * peer_ffn(hc2, peer_w_q[l], peer_sub_keys[l], peer_u[l], peer_v[l])
    return rms_norm(x, final_norm_g)


_drawn_inputs = setup_inputs


def setup_inputs(seed=0):
    import zlib

    import numpy as np

    out = dict(_drawn_inputs(seed))
    spreads = {}
    factors = {'ctx': 3.041,
     'norm1_g': 5.707,
     'norm2_g': 6.083,
     'mla_q_norm_g': 8.0,
     'mla_kv_norm_g': 8.0,
     'conv_b': 8.0,
     'conv_ln_g': 8.0,
     'conv_ln_b': 8.0,
     'hg_lower_bound': 3.781,
     'hg_norm_g': 8.0,
     'final_norm_g': 2.8}
    for name, (base, spread) in spreads.items():
        noise = np.random.default_rng([zlib.crc32(name.encode()), seed]).standard_normal(out[name].shape)
        drawn = base * np.exp(spread * noise) if base else spread * noise
        out[name] = __import__('jax').numpy.asarray(drawn.astype(out[name].dtype))
    for name, factor in factors.items():
        out[name] = (out[name] * factor).astype(out[name].dtype)
    return out
```

```python
import concourse.bass as bass
from concourse import mybir
from contextlib import ExitStack

FP32 = mybir.dt.float32
U32 = mybir.dt.uint32
ALU = mybir.AluOpType
ACT = mybir.ActivationFunctionType
AX = mybir.AxisListType.X

P = 128
D = 1024
KT = D // P
T = 256
N2 = 2 * T
EPS = 1e-6
MOD_TILES = 6 * KT
HEADS = 8
NOPE, ROPE, VDIM = 64, 32, 64
QK = NOPE + ROPE
MLA_SCALE = QK ** -0.5
CONV_T = 4
TAPS = 31
HALO = TAPS // 2
CHUNK = 64
TOPK = 16
RING = 4
SLOTS = 8
NEG = -3.0e38

C_ID, C_MASK, C_IOTA, C_COS, C_SIN, C_END = 0, 128, 384, 400, 656, 912


def wait_apart(eng, sem, value):
    if not isinstance(value, int):
        value = eng.to_reg(value)
        eng.wait_ge(sem, 1)
    eng.wait_ge(sem, value)


class Chain:

    def __init__(self, eng, sem, base=0):
        self.eng, self.sem, self.base, self.n = eng, sem, base, 0

    def __call__(self, ins):
        self.n += 1
        ins.then_inc(self.sem, 1)
        self.eng.wait_ge(self.sem, self.base + self.n)

    def apart(self, ins):
        self.n += 1
        ins.then_inc(self.sem, 1)
        wait_apart(self.eng, self.sem, self.base + self.n)


def build(nc, t, out, stop=None):
    with ExitStack() as whole:
        def sem(name):
            return whole.enter_context(nc.semaphore(name))

        def sb(name, shape, dt=FP32, ctx=whole):
            return ctx.enter_context(nc.sbuf_tensor(name, shape, dt))

        def ps(name, shape, ctx):
            return ctx.enter_context(nc.psum_tensor(name, shape, FP32))

        xT = sb("xT", [P, KT, N2])
        cst = sb("cst", [P, C_END])
        ones = sb("ones", [P, P])
        vecs = sb("vecs", [P, 128])
        modT = sb("modT", [P, 2, 6, KT, 2])
        gainT = sb("gainT", [P, 2, 2, KT, 2])
        wring = sb("wring", [P, RING, KT * P])
        ident = cst[:, C_ID:C_ID + P]

        V_N1, V_N2, V_FIN, V_QG, V_KVG, V_CB, V_LNG, V_LNB, V_HGN = 0, 16, 32, 40, 42, 43, 47, 51, 55

        w_loaded = [sem(f"w_loaded{j}") for j in range(RING)]
        acc_ready = sem("acc_ready")
        acc_free = sem("acc_free")
        lin = [("w_in", 12), ("w_out", 8), ("peer_q0", 16),
               ("hg_zz", 16), ("hg_qg", 16), ("hg_out", 8), ("peer_q1", 16)]
        first = {}
        g = 0
        for name, n in lin:
            first[name] = g
            g += n
        total_tiles = g

        def load_tile(sp, name, i, j, g):
            if not (isinstance(g, int) and g < RING):
                sp.wait_ge(acc_ready, g - (RING - 1))
            src = t[name][i] if isinstance(i, int) else \
                t[name][bass.ds(i, 1), :, :].rearrange("a p n -> p (a n)")
            sp.dma_start(wring[:, j, :], src).then_inc(w_loaded[j], 16)

        state = {"which": -1}

        def lin_loads(sp, which):
            name, n = lin[which]
            state["which"] = which
            g0 = first[name]
            if n > RING:
                with sp.Fori(0, n // RING - 1) as it:
                    for j in range(RING):
                        load_tile(sp, name, it * RING + (RING + j), j, it * RING + (g0 + RING + j))
            if which + 1 < len(lin):
                for j in range(RING):
                    load_tile(sp, lin[which + 1][0], j, j, g0 + n + j)

        def lin_matmuls(pe, which, psum, rhs, n_cols):
            name, n = lin[which]
            g0 = first[name]
            with pe.Fori(0, n // RING) as it:
                for j in range(RING):
                    pe.wait_ge(w_loaded[j], it * 16 + (g0 // RING + 1) * 16)
                    pe.wait_ge(acc_free, it * RING + (g0 + j + 1))
                    for k in range(KT):
                        last = nc.tensor.matmul(psum[:, j, 0:n_cols], wring[:, j, k * P:(k + 1) * P],
                                                rhs(k), start=(k == 0), stop=(k == KT - 1))
                    last.then_inc(acc_ready, 1)

        def lin_evac(eng, which, one):
            name, n = lin[which]
            g0 = first[name]
            with eng.Fori(0, n // RING) as it:
                for j in range(RING):
                    eng.wait_ge(acc_ready, it * RING + (g0 + j + 1))
                    one(it * RING + j, j).then_inc(acc_free, 1)

        def lin_done(eng, which):
            name, n = lin[which]
            eng.wait_ge(acc_free, RING + first[name] + n)

        s_xT, s_const, s_cond, s_sc, s_mod = sem("s_xT"), sem("s_const"), sem("s_cond"), sem("s_sc"), sem("s_mod")
        a_loaded = [sem(f"a_loaded{j}") for j in range(RING)]
        a_ready = sem("a_ready")
        a_free = sem("a_free")
        a_turned = sem("a_turned")
        GROUPS = 2 * 6 * D // 512
        with ExitStack() as c:
            scT = sb("scT", [P, KT, 2], ctx=c)
            adab = sb("adab", [P, 96], ctx=c)
            aw = sb("aw", [P, RING, KT * 512], ctx=c)
            rows = sb("rows", [P, RING, 512], ctx=c)
            pm = ps("pm", [P, RING, 512], c)
            pt = ps("pt", [P, 4 * (GROUPS + 1), 2], c)
            block = c.enter_context(nc.Block())

            @block.sync
            def _(sp):
                sp.dma_start(scT[:], t["cT"]).then_inc(s_cond, 16)
                sp.dma_start(aw[:, 0, :], t["ada_w"][0]).then_inc(a_loaded[0], 16)
                sp.dma_start(cst[:], t["consts"]).then_inc(s_const, 16)
                sp.dma_start(vecs[:, 0:63], t["vecs"]).then_inc(s_const, 16)
                sp.dma_start(adab[:], t["ada_b"]).then_inc(s_const, 16)
                for j in range(1, RING):
                    sp.dma_start(aw[:, j, :], t["ada_w"][j]).then_inc(a_loaded[j], 16)
                sp.dma_start(xT[:], t["xT"]).then_inc(s_xT, 16)
                with sp.Fori(0, GROUPS // RING - 1) as it:
                    for j in range(RING):
                        sp.wait_ge(a_ready, it * RING + (j + 1))
                        sp.dma_start(aw[:, j, :], t["ada_w"][bass.ds(it * RING + (RING + j), 1), :, :]
                                     .rearrange("a p n -> p (a n)")).then_inc(a_loaded[j], 16)
                for j in range(RING):
                    load_tile(sp, lin[0][0], j, j, j)
                sp.wait_ge(s_xT, 16)

            @block.gpsimd
            def _(pool):
                nc.gpsimd.memset(ones[:], 1.0)

            @block.scalar
            def _(act):
                act.wait_ge(s_cond, 16)
                nc.scalar.activation(scT[:], scT[:], ACT.Silu).then_inc(s_sc, 1)

            @block.tensor
            def _(pe):
                def turn(j, n):
                    for q in range(4):
                        last = nc.tensor.matmul(pt[:, bass.ds(n * 4 + q, 1), :].rearrange("p a c -> p (a c)"),
                                                rows[:, j, q * P:(q + 1) * P], ident[:, 0:2], start=True, stop=True)
                    last.then_inc(a_turned, 1)

                pe.wait_ge(s_sc, 1)
                pe.wait_ge(s_const, 48)
                pe.wait_ge(s_mod, 1)
                with pe.Fori(0, GROUPS // RING) as it:
                    for j in range(RING):
                        pe.wait_ge(a_loaded[j], it * 16 + 16)
                        pe.wait_ge(a_free, it * RING + (j + 1))
                        for k in range(KT):
                            last = nc.tensor.matmul(pm[0:2, j, :], scT[:, k, :], aw[:, j, k * 512:(k + 1) * 512],
                                                    start=(k == 0), stop=(k == KT - 1))
                        last.then_inc(a_ready, 1)
                        pe.wait_ge(a_free, it * RING + (RING + j))
                        turn((j - 1) % RING, it * RING + j)
                pe.wait_ge(a_free, RING + GROUPS)
                turn(RING - 1, GROUPS)

            @block.vector
            def _(dve):
                chain = Chain(dve, s_mod)
                chain(nc.vector.memset(rows[:], 0.0))
                dve.sem_inc(a_free, RING)
                dve.sem_inc(a_turned, RING - 1)
                dve.sem_inc(acc_free, RING)
                with dve.Fori(0, GROUPS // RING) as it:
                    for j in range(RING):
                        dve.wait_ge(a_ready, it * RING + (j + 1))
                        dve.wait_ge(a_turned, it * RING + (j + 1))
                        nc.vector.tensor_copy(rows[0:2, j, :], pm[0:2, j, :]).then_inc(a_free, 1)
                dve.wait_ge(a_turned, RING - 1 + GROUPS + 1)
                dve.wait_ge(s_const, 48)
                mod_flat = modT[:].rearrange("p l m k c -> p (l m k) c")
                chain(nc.vector.tensor_tensor(mod_flat, pt[:, 4:, :],
                                              adab[:].unsqueeze(2).broadcast_to([P, 96, 2]), ALU.add))
                for l in range(2):
                    for w in range(2):
                        gain = vecs[:, (V_N1, V_N2)[w] + 8 * l:][:, 0:8].unsqueeze(2).broadcast_to([P, KT, 2])
                        chain(nc.vector.scalar_tensor_tensor(
                            out=gainT[:, l, w], in0=modT[:, l, 3 * w + 1], scalar=1.0, in1=gain,
                            op0=ALU.add, op1=ALU.mult))

        def done(name):
            if stop == name:
                with nc.Block() as block:
                    @block.sync
                    def _(sp):
                        nxt = lin[state["which"]] if state["which"] >= 0 else ("w_in", -0)
                        if state["which"] < 0:
                            nxt = ("w_in", 0)
                        for j in range(RING):
                            sp.wait_ge(w_loaded[j], (first[nxt[0]] + nxt[1] + RING) // RING * 16)
            return stop == name

        if done("mod"):
            return

        def norm_phase(tag, src, dst, cols, l, w):
            sq_ready, sum_ready, rs_ready, y_ready = (sem(f"{tag}_{x}") for x in ("sq", "sum", "rs", "y"))
            s_done = sem(f"{tag}_done")
            with ExitStack() as c:
                sq = sb(f"{tag}_sqb", [P, KT, cols], ctx=c)
                rs = sb(f"{tag}_rsb", [P, cols], ctx=c)
                pn = ps(f"{tag}_pn", [P, 512], c)
                block = c.enter_context(nc.Block())

                def affine(eng, k):
                    for c2 in range(cols // T):
                        part = dst[:, k, c2 * T:(c2 + 1) * T]
                        if l is None:
                            a, b = vecs[:, V_FIN + k:V_FIN + k + 1], 0.0
                        else:
                            a, b = gainT[:, l, w, k, c2:c2 + 1], modT[:, l, 3 * w, k, c2:c2 + 1]
                        if eng is nc.scalar:
                            last = eng.activation(part, part, ACT.Identity, scale=a, bias=b)
                        elif l is None:
                            last = eng.tensor_scalar(part, part, a, None, ALU.mult)
                        else:
                            last = eng.tensor_scalar(part, part, a, b, ALU.mult, ALU.add)
                    return last

                @block.scalar
                def _(act):
                    for k in range(KT):
                        nc.scalar.activation(sq[:, k], src[:, k, 0:cols], ACT.Square).then_inc(sq_ready, 1)
                    act.wait_ge(rs_ready, 1)
                    nc.scalar.activation(rs[:], rs[:], ACT.Sqrt).then_inc(s_done, 1)
                    for k in range(0, KT, 2):
                        act.wait_ge(y_ready, k + 1)
                        affine(nc.scalar, k).then_inc(s_done, 1)

                @block.tensor
                def _(pe):
                    for k in range(KT):
                        pe.wait_ge(sq_ready, k + 1)
                        last = nc.tensor.matmul(pn[:, 0:cols], ones[:], sq[:, k], start=(k == 0), stop=(k == KT - 1))
                    last.then_inc(sum_ready, 1)

                @block.vector
                def _(dve):
                    dve.wait_ge(sum_ready, 1)
                    nc.vector.tensor_scalar(rs[:], pn[:, 0:cols], 1.0 / D, EPS, ALU.mult, ALU.add).then_inc(rs_ready, 1)
                    dve.wait_ge(s_done, 1)
                    nc.vector.reciprocal(rs[:], rs[:]).then_inc(rs_ready, 1)
                    dve.wait_ge(rs_ready, 2)
                    for k in range(KT):
                        nc.vector.tensor_tensor(dst[:, k, 0:cols], src[:, k, 0:cols], rs[:], ALU.mult).then_inc(y_ready, 1)
                        if k >= 1 and (k - 1) % 2 == 1:
                            dve.wait_ge(y_ready, k)
                            affine(nc.vector, k - 1)
                    dve.wait_ge(y_ready, KT)
                    affine(nc.vector, KT - 1)

        def residual_evac(which, psum, cols, l, part):
            def one(i, j):
                for c2 in range(cols // T):
                    span = slice(c2 * T, (c2 + 1) * T)
                    last = nc.vector.scalar_tensor_tensor(
                        out=xT[:, bass.ds(i, 1), span], in0=psum[:, j:j + 1, span],
                        scalar=modT[:, l, part, bass.ds(i, 1), c2:c2 + 1].rearrange("p a c -> p (a c)"),
                        in1=xT[:, bass.ds(i, 1), span], op0=ALU.mult, op1=ALU.add)
                return last
            return one

        with ExitStack() as c0:
            mix = sb("mix", [P, KT, N2], ctx=c0)
            with ExitStack() as c1:
                cT = sb("cT", [P, 12, N2], ctx=c1)
                with ExitStack() as c:
                    hT = sb("hT0", [P, KT, N2], ctx=c)
                    norm_phase("n0", xT, hT, N2, 0, 0)
                    if done("n0"):
                        return
                    pl = ps("pl0", [P, RING, 512], c)
                    block = c.enter_context(nc.Block())

                    @block.sync
                    def _(sp):
                        lin_loads(sp, 0)

                    @block.tensor
                    def _(pe):
                        lin_matmuls(pe, 0, pl, lambda k: hT[:, k, :], N2)

                    @block.scalar
                    def _(act):
                        lin_evac(act, 0, lambda i, j: nc.scalar.copy(cT[:, bass.ds(i, 1), :], pl[:, j:j + 1, :]))
                if done("w_in"):
                    return
                mla_phase(nc, t, sem, sb, ps, cT, mix, cst, vecs, ones, ident,
                          (V_QG, V_KVG, V_CB, V_LNG, V_LNB), done)
                if done("mla") or done("proj"):
                    return
            with ExitStack() as c:
                pl = ps("pl1", [P, RING, 512], c)
                block = c.enter_context(nc.Block())

                @block.sync
                def _(sp):
                    lin_loads(sp, 1)

                @block.tensor
                def _(pe):
                    lin_matmuls(pe, 1, pl, lambda k: mix[:, k, :], N2)

                @block.vector
                def _(dve):
                    lin_evac(dve, 1, residual_evac(1, pl, N2, 0, 2))
        if done("l0mix"):
            return

        u_loaded = [sem(f"u_loaded{j}") for j in range(SLOTS)]
        v_loaded = [sem(f"v_loaded{j}") for j in range(SLOTS)]
        peer_base = {"steps": 0}

        def peer_layer(l, cols):
            peer_phase(nc, t, sem, sb, ps, xT, modT, cst, ident, l, cols, norm_phase, lin_loads,
                       lin_matmuls, lin_evac, lin_done, {0: 2, 1: 6}[l], u_loaded, v_loaded, peer_base, done)

        peer_layer(0, N2)
        if done("peer_p0") or done("peer0"):
            return

        hgrn_phase(nc, t, sem, sb, ps, xT, modT, cst, vecs, ones, ident, norm_phase, lin_loads,
                   lin_matmuls, lin_evac, lin_done, residual_evac, V_HGN, done)
        if done("hgrn_p") or done("hgrn"):
            return
        peer_layer(1, T)

        s_out = sem("s_out")
        with ExitStack() as c:
            yT = sb("yT", [P, KT, T], ctx=c)
            norm_phase("nf", xT, yT, T, None, None)
            block = c.enter_context(nc.Block())

            @block.sync
            def _(sp):
                sp.dma_start(out, yT[:]).then_inc(s_out, 16)
                sp.wait_ge(s_out, 16)


def mla_phase(nc, t, sem, sb, ps, cT, mix, cst, vecs, ones, ident, cols, done):
    V_QG, V_KVG, V_CB, V_LNG, V_LNB = cols
    rope_rows = slice(NOPE, QK)
    with ExitStack() as c:
        Q = sb("Q", [QK, HEADS, N2], ctx=c)
        K = sb("K", [QK, HEADS, N2], ctx=c)
        V = sb("V", [P, 4, HEADS * VDIM], ctx=c)
        gated = sb("gated", [P, CONV_T, 2, T + 2 * HALO], ctx=c)
        convw = sb("convw", [P, CONV_T, TAPS], ctx=c)
        s_w = sem("mla_w")
        s_act, s_pe, s_dve, s_pool = sem("mla_act"), sem("mla_pe"), sem("mla_dve"), sem("mla_pool")
        s_q, s_qe, s_k, s_ke, s_v, s_ve = (sem(f"mla_{x}") for x in ("q", "qe", "k", "ke", "v", "ve"))

        with ExitStack() as c2:
            wuq = sb("wuq", [P, 2, HEADS * P], ctx=c2)
            wuk = sb("wuk", [P, HEADS * NOPE], ctx=c2)
            wuv = sb("wuv", [P, HEADS * VDIM], ctx=c2)
            lat = sb("lat", [P, 3, N2], ctx=c2)
            rs = sb("lat_rs", [P, 2, N2], ctx=c2)
            QS = sb("QS", [QK, HEADS, T], ctx=c2)
            KS = sb("KS", [QK, N2], ctx=c2)
            KR = sb("KR", [QK, N2], ctx=c2)
            pn = ps("mla_pn", [P, 2, 512], c2)
            pq = ps("mla_pq", [P, 3, 512], c2)
            pk = ps("mla_pk", [P, 3, 512], c2)
            block = c2.enter_context(nc.Block())

            @block.sync
            def _(sp):
                sp.dma_start(wuq[:], t["w_uq"]).then_inc(s_w, 16)
                sp.dma_start(wuk[:], t["w_uk"]).then_inc(s_w, 16)
                sp.dma_start(wuv[:], t["w_uv"]).then_inc(s_w, 16)
                sp.dma_start(convw[:], t["conv_w"]).then_inc(s_w, 16)

            @block.gpsimd
            def _(pool):
                nc.gpsimd.memset(gated[:], 0.0).then_inc(s_pool, 1)

            @block.scalar
            def _(act):
                nc.scalar.activation(lat[:], cT[:, 0:3, :], ACT.Square).then_inc(s_act, 1)
                nc.scalar.copy(KS[rope_rows, 0:T], cT[QK:P, 3, 0:T]).then_inc(s_act, 1)
                act.wait_ge(s_dve, 2)
                nc.scalar.activation(rs[:], rs[:], ACT.Sqrt).then_inc(s_act, 1)
                for h in range(HEADS):
                    act.wait_ge(s_q, h + 1)
                    nc.scalar.copy(Q[:, h, :], pq[0:QK, h % 3, :])
                    nc.scalar.copy(QS[rope_rows, h, :], pq[QK:P, h % 3, 0:T]).then_inc(s_qe, 1)
                for m in range(4):
                    act.wait_ge(s_v, m + 1)
                    nc.scalar.copy(V[:, m, :], pq[:, (HEADS + m) % 3, :]).then_inc(s_qe, 1)

            @block.tensor
            def _(pe):
                pe.wait_ge(s_act, 1)
                for k in range(2):
                    nc.tensor.matmul(pn[:, 0, :], ones[:], lat[:, k, :], start=(k == 0), stop=(k == 1))
                nc.tensor.matmul(pn[:, 1, :], ones[:], lat[:, 2, :], start=True, stop=True).then_inc(s_pe, 1)
                pe.wait_ge(s_w, 64)
                pe.wait_ge(s_dve, 6)
                for h in range(HEADS):
                    if h >= 3:
                        pe.wait_ge(s_qe, h - 2)
                    for k in range(2):
                        last = nc.tensor.matmul(pq[:, h % 3, :], wuq[:, k, h * P:(h + 1) * P], lat[:, k, :],
                                                start=(k == 0), stop=(k == 1))
                    last.then_inc(s_q, 1)
                    if h >= 3:
                        pe.wait_ge(s_ke, h - 2)
                    nc.tensor.matmul(pk[0:NOPE, h % 3, :], wuk[:, h * NOPE:(h + 1) * NOPE], lat[:, 2, :],
                                     start=True, stop=True).then_inc(s_k, 1)
                for m in range(4):
                    pe.wait_ge(s_qe, HEADS + m - 2)
                    nc.tensor.matmul(pq[:, (HEADS + m) % 3, :], lat[:, 2, m * P:(m + 1) * P], wuv[:],
                                     start=True, stop=True).then_inc(s_v, 1)

            @block.vector
            def _(dve):
                chain = Chain(dve, s_dve)
                dve.wait_ge(s_pe, 1)
                chain(nc.vector.tensor_scalar(rs[:, 0], pn[:, 0], 1.0 / 256, EPS, ALU.mult, ALU.add))
                chain(nc.vector.tensor_scalar(rs[:, 1], pn[:, 1], 1.0 / 128, EPS, ALU.mult, ALU.add))
                dve.wait_ge(s_act, 3)
                chain(nc.vector.reciprocal(rs[:], rs[:]))
                for k in range(3):
                    chain(nc.vector.scalar_tensor_tensor(
                        out=lat[:, k], in0=cT[:, k], scalar=vecs[:, V_QG + k:V_QG + k + 1],
                        in1=rs[:, k // 2], op0=ALU.mult, op1=ALU.mult))
                cos, sin = cst[rope_rows, C_COS:C_COS + T], cst[rope_rows, C_SIN:C_SIN + T]
                kr = cT[rope_rows, 3, 0:T]
                chain(nc.vector.tensor_tensor(KR[rope_rows, 0:T], kr, cos, ALU.mult))
                chain(nc.vector.tensor_tensor(KS[rope_rows, 0:T], KS[rope_rows, 0:T], sin, ALU.mult))
                chain(nc.vector.tensor_tensor(KR[rope_rows, 0:T], KR[rope_rows, 0:T], KS[rope_rows, 0:T], ALU.add))
                chain(nc.vector.tensor_copy(KR[rope_rows, T:N2], cT[rope_rows, 3, T:N2]))
                nc.vector.tensor_copy(K[rope_rows], KR[rope_rows, :].unsqueeze(1).broadcast_to([ROPE, HEADS, N2]))
                for h in range(HEADS):
                    dve.wait_ge(s_k, h + 1)
                    nc.vector.tensor_copy(K[0:NOPE, h, :], pk[0:NOPE, h % 3, :]).then_inc(s_ke, 1)
                dve.wait_ge(s_qe, HEADS)
                bc = [ROPE, HEADS, T]
                qx = Q[rope_rows, :, 0:T]
                chain(nc.vector.tensor_tensor(qx, qx, cos.unsqueeze(1).broadcast_to(bc), ALU.mult))
                chain(nc.vector.tensor_tensor(QS[rope_rows], QS[rope_rows], sin.unsqueeze(1).broadcast_to(bc), ALU.mult))
                chain(nc.vector.tensor_tensor(qx, qx, QS[rope_rows], ALU.add))
        if done("proj"):
            return

        O = sb("O", [P, 4, HEADS * VDIM], ctx=c)
        conv = sb("conv", [P, CONV_T, 2, T], ctx=c)
        with ExitStack() as c2:
            prob = sb("prob", [P, 2, N2], ctx=c2)
            probT = sb("probT", [P, 2, 4, P], ctx=c2)
            sg = sb("sg", [P, CONV_T, 2, T], ctx=c2)
            nmx = sb("nmx", [P, 2], ctx=c2)
            den = sb("den", [P, 2], ctx=c2)
            rden = sb("rden", [P, 2], ctx=c2)
            pS = ps("pS", [P, 2, 512], c2)
            pT = ps("pT", [P, 2, 4, P], c2)
            pO = ps("pO", [P, 2, 512], c2)
            at = {x: sem(f"att_{x}") for x in ("s", "mx", "nmx", "exp", "t", "copied", "o", "rd", "norm", "sg", "gated", "conv")}
            block = c2.enter_context(nc.Block())
            units = [(m, h) for m in range(4) for h in range(HEADS)]

            def keys(m):
                return (0, 4) if m < 2 else (2, 4)

            @block.tensor
            def _(pe):
                for u in range(len(units) + 2):
                    if u < len(units):
                        m, h = units[u]
                        lo, hi = keys(m)
                        if u >= 2:
                            pe.wait_ge(at["exp"], u - 1)
                        nc.tensor.matmul(pS[:, u % 2, lo * P:hi * P], Q[:, h, m * P:(m + 1) * P],
                                         K[:, h, lo * P:hi * P], start=True, stop=True).then_inc(at["s"], 1)
                    if 1 <= u <= len(units):
                        v = u - 1
                        lo, hi = keys(units[v][0])
                        pe.wait_ge(at["exp"], v + 1)
                        if v >= 2:
                            pe.wait_ge(at["copied"], v - 1)
                        for j in range(lo, hi):
                            last = nc.tensor.transpose(pT[:, v % 2, j, :], prob[:, v % 2, j * P:(j + 1) * P], ident)
                        last.then_inc(at["t"], 1)
                    if u >= 2:
                        v = u - 2
                        m, h = units[v]
                        lo, hi = keys(m)
                        pe.wait_ge(at["copied"], v + 1)
                        if v >= 2:
                            pe.wait_ge(at["norm"], v - 1)
                        for j in range(lo, hi):
                            last = nc.tensor.matmul(pO[:, v % 2, 0:VDIM], probT[:, v % 2, j, :],
                                                    V[:, j, h * VDIM:(h + 1) * VDIM], start=(j == lo), stop=(j == hi - 1))
                        last.then_inc(at["o"], 1)

            @block.scalar
            def _(act):
                nc.scalar.activation(sg[:].rearrange("p a b n -> p (a b n)"),
                                     cT[:, 8:12, :].rearrange("p a n -> p (a n)"), ACT.Sigmoid).then_inc(at["sg"], 1)
                for u in range(len(units) + 1):
                    if u < len(units):
                        lo, hi = keys(units[u][0])
                        act.wait_ge(at["nmx"], u + 1)
                        if u >= 2:
                            act.wait_ge(at["t"], u - 1)
                            act.wait_ge(at["rd"], u - 1)
                        nc.scalar.activation(prob[:, u % 2, lo * P:hi * P], pS[:, u % 2, lo * P:hi * P], ACT.Exp,
                                             bias=nmx[:, u % 2:u % 2 + 1], scale=MLA_SCALE,
                                             accum_out=den[:, u % 2:u % 2 + 1]).then_inc(at["exp"], 1)
                    if u >= 1:
                        v = u - 1
                        lo, hi = keys(units[v][0])
                        act.wait_ge(at["t"], v + 1)
                        if v >= 2:
                            act.wait_ge(at["o"], v - 1)
                        nc.scalar.copy(probT[:, v % 2, lo:hi, :], pT[:, v % 2, lo:hi, :]).then_inc(at["copied"], 1)

            @block.vector
            def _(dve):
                dve.wait_ge(at["sg"], 1)
                for i in range(CONV_T):
                    nc.vector.tensor_tensor(gated[:, i, :, HALO:HALO + T],
                                            cT[:, 4 + i, :].rearrange("p (s n) -> p s n", s=2),
                                            sg[:, i], ALU.mult).then_inc(at["gated"], 1)
                dve.wait_ge(at["gated"], CONV_T)
                for u in range(len(units) + 2):
                    if u < len(units):
                        lo, hi = keys(units[u][0])
                        dve.wait_ge(at["s"], u + 1)
                        if u >= 2:
                            dve.wait_ge(at["exp"], u - 1)
                        nc.vector.reduce_max(nmx[:, u % 2:u % 2 + 1], pS[:, u % 2, lo * P:hi * P], AX).then_inc(at["mx"], 1)
                        dve.wait_ge(at["mx"], u + 1)
                        nc.vector.tensor_scalar(nmx[:, u % 2:u % 2 + 1], nmx[:, u % 2:u % 2 + 1],
                                                -MLA_SCALE, None, ALU.mult).then_inc(at["nmx"], 1)
                    if u < TAPS:
                        for i in range(CONV_T):
                            src, w = gated[:, i, :, u:u + T], convw[:, i, u:u + 1]
                            if u == 0:
                                nc.vector.tensor_scalar(conv[:, i], src, w, vecs[:, V_CB + i:V_CB + i + 1],
                                                        ALU.mult, ALU.add).then_inc(at["conv"], 1)
                            else:
                                dve.wait_ge(at["conv"], CONV_T * (u - 1) + i + 1)
                                nc.vector.scalar_tensor_tensor(out=conv[:, i], in0=src, scalar=w, in1=conv[:, i],
                                                               op0=ALU.mult, op1=ALU.add).then_inc(at["conv"], 1)
                    if u >= 2:
                        v = u - 2
                        m, h = units[v]
                        dve.wait_ge(at["exp"], v + 1)
                        nc.vector.reciprocal(rden[:, v % 2:v % 2 + 1], den[:, v % 2:v % 2 + 1]).then_inc(at["rd"], 1)
                        dve.wait_ge(at["o"], v + 1)
                        dve.wait_ge(at["rd"], v + 1)
                        nc.vector.tensor_scalar(O[:, m, h * VDIM:(h + 1) * VDIM], pO[:, v % 2, 0:VDIM],
                                                rden[:, v % 2:v % 2 + 1], None, ALU.mult).then_inc(at["norm"], 1)
        if done("att"):
            return

        with ExitStack() as c2:
            sq = sb("conv_sq", [P, CONV_T, N2], ctx=c2)
            rs = sb("conv_rs", [P, N2], ctx=c2)
            pOT = ps("pOT", [P, 4, 512], c2)
            pL = ps("pL", [P, 2, 512], c2)
            ot, ln_pe, ln_dve, ln_act = sem("ot"), sem("ln_pe"), sem("ln_dve"), sem("ln_act")
            cv = conv[:].rearrange("p c s n -> p c (s n)")
            block = c2.enter_context(nc.Block())

            @block.tensor
            def _(pe):
                for i in range(CONV_T):
                    last = nc.tensor.matmul(pL[:, 0], ones[:], cv[:, i], start=(i == 0), stop=(i == CONV_T - 1))
                last.then_inc(ln_pe, 1)
                for k in range(4):
                    for m in range(4):
                        last = nc.tensor.transpose(pOT[:, k, m * P:(m + 1) * P], O[:, m, k * P:(k + 1) * P], ident)
                    last.then_inc(ot, 1)
                for i in range(CONV_T):
                    pe.wait_ge(ln_act, i + 1)
                    last = nc.tensor.matmul(pL[:, 1], ones[:], sq[:, i], start=(i == 0), stop=(i == CONV_T - 1))
                last.then_inc(ln_pe, 1)

            @block.vector
            def _(dve):
                chain = Chain(dve, ln_dve)
                dve.wait_ge(ln_pe, 1)
                for i in range(CONV_T):
                    chain(nc.vector.scalar_tensor_tensor(out=cv[:, i], in0=pL[:, 0], scalar=-1.0 / 512,
                                                         in1=cv[:, i], op0=ALU.mult, op1=ALU.add))
                dve.wait_ge(ln_pe, 2)
                chain(nc.vector.tensor_scalar(rs[:], pL[:, 1], 1.0 / 512, EPS, ALU.mult, ALU.add))
                dve.wait_ge(ln_act, CONV_T + 1)
                chain(nc.vector.reciprocal(rs[:], rs[:]))
                for i in range(CONV_T):
                    chain(nc.vector.tensor_tensor(cv[:, i], cv[:, i], rs[:], ALU.mult))
                for k in range(4):
                    dve.wait_ge(ot, k + 1)
                    nc.vector.tensor_copy(mix[:, k, :], pOT[:, k, :])

            @block.scalar
            def _(act):
                for i in range(CONV_T):
                    act.wait_ge(ln_dve, i + 1)
                    nc.scalar.activation(sq[:, i], cv[:, i], ACT.Square).then_inc(ln_act, 1)
                act.wait_ge(ln_dve, CONV_T + 1)
                nc.scalar.activation(rs[:], rs[:], ACT.Sqrt).then_inc(ln_act, 1)
                for i in range(CONV_T):
                    act.wait_ge(ln_dve, CONV_T + 3 + i)
                    nc.scalar.activation(mix[:, 4 + i, :], cv[:, i], ACT.Silu, scale=vecs[:, V_LNG + i:V_LNG + i + 1],
                                         bias=vecs[:, V_LNB + i:V_LNB + i + 1])


def peer_phase(nc, t, sem, sb, ps, xT, modT, cst, ident, l, cols, norm_phase, lin_loads, lin_matmuls,
               lin_evac, lin_done, which, u_loaded, v_loaded, base, done):
    blocks = cols // P
    steps = blocks * HEADS
    pairs = HEADS // 2
    with ExitStack() as c:
        H2 = sb(f"H2_{l}", [P, blocks, D], ctx=c)
        S = sb(f"S_{l}", [P, steps + 1, 2 * P], ctx=c)
        Y = sb(f"Y_{l}", [P, blocks + 1, D], ctx=c)

        with ExitStack() as c2:
            hT = sb(f"h2T_{l}", [P, KT, cols], ctx=c2)
            qT = sb(f"qT_{l}", [P, 2 * HEADS, cols], ctx=c2)
            keys = sb(f"keys_{l}", [P, 2 * HEADS, P], ctx=c2)
            norm_phase(f"np{l}", xT, hT, cols, l, 1)
            pl = ps(f"pq_{l}", [P, RING, 512], c2)
            ptr = ps(f"ptr_{l}", [P, 4, 512], c2)
            s_keys, s_tr, s_tre, s_sc, s_sce = (sem(f"p{l}_{x}") for x in ("keys", "tr", "tre", "sc", "sce"))
            block = c2.enter_context(nc.Block())

            @block.sync
            def _(sp):
                sp.dma_start(keys[:], t[f"keys{l}"]).then_inc(s_keys, 16)
                lin_loads(sp, which)

            @block.gpsimd
            def _(pool):
                nc.gpsimd.memset(S[:, steps, :], 0.0)
                nc.gpsimd.memset(Y[:], 0.0)

            @block.tensor
            def _(pe):
                for n in range(2 * blocks):
                    b, half = n // 2, n % 2
                    if n >= 4:
                        pe.wait_ge(s_tre, n - 3)
                    for k in range(4):
                        last = nc.tensor.transpose(ptr[:, n % 4, k * P:(k + 1) * P],
                                                   hT[:, 4 * half + k, b * P:(b + 1) * P], ident)
                    last.then_inc(s_tr, 1)
                lin_matmuls(pe, which, pl, lambda k: hT[:, k, :], cols)
                pe.wait_ge(s_keys, 16)
                lin_done(pe, which)
                for n in range(4 * blocks):
                    b, h2 = n // 4, n % 4
                    pe.wait_ge(s_tre, 2 * blocks)
                    if n >= 4:
                        pe.wait_ge(s_sce, n - 3)
                    for j in range(4):
                        last = nc.tensor.matmul(ptr[:, n % 4, j * P:(j + 1) * P], qT[:, 4 * h2 + j, b * P:(b + 1) * P],
                                                keys[:, 4 * h2 + j, :], start=True, stop=True)
                    last.then_inc(s_sc, 1)

            @block.scalar
            def _(act):
                lin_evac(act, which, lambda i, j: nc.scalar.copy(qT[:, bass.ds(i, 1), :], pl[:, j:j + 1, 0:cols]))

            @block.vector
            def _(dve):
                for n in range(2 * blocks):
                    dve.wait_ge(s_tr, n + 1)
                    nc.vector.tensor_copy(H2[:, n // 2, (n % 2) * 512:(n % 2 + 1) * 512], ptr[:, n % 4, :]).then_inc(s_tre, 1)
                for n in range(4 * blocks):
                    dve.wait_ge(s_sc, n + 1)
                    nc.vector.tensor_copy(S[:, 2 * n:2 * n + 2, :].rearrange("p s k -> p (s k)"),
                                          ptr[:, n % 4, :]).then_inc(s_sce, 1)
        if done(f"peer_p{l}"):
            return

        with ExitStack() as c2:
            U = [sb(f"U{l}_{j}", [P, D], ctx=c2) for j in range(SLOTS)]
            Vr = [sb(f"V{l}_{j}", [P, D], ctx=c2) for j in range(SLOTS)]
            diag = sb(f"diag{l}", [P, TOPK, P], ctx=c2)
            junk = sb(f"junk{l}", [P, 2, D], ctx=c2)
            raw = sb(f"raw{l}", [P, 2, P], ctx=c2)
            rest = sb(f"rest{l}", [P, 2, P], ctx=c2)
            sv = sb(f"sv{l}", [P, 2, TOPK], ctx=c2)
            si = sb(f"si{l}", [P, 2, TOPK], U32, ctx=c2)
            sif = sb(f"sif{l}", [P, 2, TOPK], ctx=c2)
            cand = sb(f"cand{l}", [P, TOPK, TOPK], ctx=c2)
            cand2 = sb(f"cand2{l}", [P, TOPK, TOPK], ctx=c2)
            top = [sb(f"top{l}_{e}", [P, TOPK], ctx=c2) for e in range(2)]
            pos = sb(f"pos{l}", [P, TOPK], U32, ctx=c2)
            pij = sb(f"pij{l}", [P, 2, TOPK], U32, ctx=c2)
            pf = sb(f"pf{l}", [P, 2, TOPK], ctx=c2)
            hot = sb(f"hot{l}", [P, 2, TOPK, TOPK], ctx=c2)
            e2 = sb(f"e2{l}", [P, 2, TOPK], ctx=c2)
            idx = [sb(f"idx{l}_{e}", [P, TOPK], U32, ctx=c2) for e in range(2)]
            mine = [sb(f"mine{l}_{e}", [P, TOPK], U32, ctx=c2) for e in range(2)]
            nmax = [sb(f"nmax{l}_{e}", [P, 1], ctx=c2) for e in range(2)]
            ex = [sb(f"ex{l}_{e}", [P, TOPK], ctx=c2) for e in range(2)]
            den = [sb(f"pden{l}_{e}", [P, 1], ctx=c2) for e in range(2)]
            rden = sb(f"prden{l}", [P, 1], ctx=c2)
            dots = sb(f"dots{l}", [P, TOPK], ctx=c2)
            act_t = sb(f"actt{l}", [P, TOPK], ctx=c2)
            coef = sb(f"coef{l}", [P, TOPK], ctx=c2)
            pY = ps(f"pY{l}", [P, D], c2)
            iota = cst[:, C_IOTA:C_IOTA + TOPK]
            s_idx, s_dot, s_gelu, s_coef, s_diag, s_y, s_u, s_v, s_exp, s_ch, s_taken = (
                sem(f"p{l}_{x}") for x in ("idx", "dot", "gelu", "coef", "diag", "y", "ufree", "vfree", "exp", "chain", "taken"))
            TOPK_LINKS, STEP_LINKS = 25, 27
            block = c2.enter_context(nc.Block())

            def topk(chain, s, e):
                v = nc.vector
                chain.apart(v.tensor_copy(raw[:].rearrange("p h k -> p (h k)"),
                                    S[:, bass.ds(s, 1), :].rearrange("p a n -> p (a n)")))
                for h in range(2):
                    chain.apart(v.max(out=sv[:, h, 0:8], in_=raw[:, h]))
                    chain.apart(v.max_index(out=si[:, h, 0:8], in_max=sv[:, h, 0:8], in_values=raw[:, h]))
                    chain.apart(v.match_replace(out=rest[:, h], in_to_replace=sv[:, h, 0:8], in_values=raw[:, h], imm_value=NEG))
                    chain.apart(v.max(out=sv[:, h, 8:16], in_=rest[:, h]))
                    chain.apart(v.max_index(out=si[:, h, 8:16], in_max=sv[:, h, 8:16], in_values=rest[:, h]))
                chain.apart(v.tensor_tensor(cand[:], sv[:, 0, :].unsqueeze(2).broadcast_to([P, TOPK, TOPK]),
                                      sv[:, 1, :].unsqueeze(1).broadcast_to([P, TOPK, TOPK]), ALU.add))
                cf, cf2 = (x[:].rearrange("p a b -> p (a b)") for x in (cand, cand2))
                chain.apart(v.max(out=top[e][:, 0:8], in_=cf))
                chain.apart(v.max_index(out=pos[:, 0:8], in_max=top[e][:, 0:8], in_values=cf))
                chain.apart(v.match_replace(out=cf2, in_to_replace=top[e][:, 0:8], in_values=cf, imm_value=NEG))
                chain.apart(v.max(out=top[e][:, 8:16], in_=cf2))
                chain.apart(v.max_index(out=pos[:, 8:16], in_max=top[e][:, 8:16], in_values=cf2))
                chain(v.tensor_scalar(nmax[e][:], top[e][:, 0:1], -1.0, None, ALU.mult))
                chain(v.tensor_scalar(pij[:, 0], pos[:], 4, None, ALU.logical_shift_right))
                chain(v.tensor_scalar(pij[:, 1], pos[:], TOPK - 1, None, ALU.bitwise_and))
                chain(v.tensor_copy(pf[:], pij[:]))
                chain(v.tensor_copy(sif[:], si[:]))
                q4 = [P, 2, TOPK, TOPK]
                chain(v.tensor_tensor(hot[:], pf[:].unsqueeze(3).broadcast_to(q4),
                                      iota.unsqueeze(1).unsqueeze(1).broadcast_to(q4), ALU.is_equal))
                chain(v.tensor_tensor(hot[:], hot[:], sif[:].unsqueeze(2).broadcast_to(q4), ALU.mult))
                chain(v.tensor_reduce(e2[:], hot[:], AX, ALU.add))
                v.scalar_tensor_tensor(out=idx[e][:], in0=e2[:, 0], scalar=float(P), in1=e2[:, 1],
                                       op0=ALU.mult, op1=ALU.add).then_inc(s_idx, 1)

            def dots_of(dve, b, s):
                for k in range(TOPK):
                    j = k % SLOTS
                    dve.wait_ge(u_loaded[j], (base["steps"] + s) * 32 + (k // SLOTS + 1) * 16)
                    dve.wait_ge(s_u, s * TOPK + (SLOTS + k - 1))
                    nc.vector.scalar_tensor_tensor(
                        out=junk[:, k % 2], in0=U[j][:], scalar=1.0, in1=H2[:, bass.ds(b, 1), :].rearrange("p a n -> p (a n)"),
                        op0=ALU.mult, op1=ALU.mult, accum_out=dots[:, k:k + 1]).then_inc(s_u, 1)

            def step(dve, chain, b, p, s, e):
                dve.wait_ge(s_taken, s + 1)
                topk(chain, s + 1, 1 - e)
                dots_of(dve, b, s)
                dve.wait_ge(s_y, s + 1)
                yb = Y[:, bass.ds(b + 1 if e else (s + (HEADS - 1)) // HEADS, 1), :].rearrange("p a n -> p (a n)")
                chain(nc.vector.tensor_tensor(yb, yb, pY[:], ALU.add))
                dve.wait_ge(s_exp, s + 1)
                chain(nc.vector.reciprocal(rden[:], den[e][:]))
                dve.wait_ge(s_gelu, s + 1)
                nc.vector.scalar_tensor_tensor(out=coef[:], in0=act_t[:], scalar=rden[:, 0:1], in1=ex[e][:],
                                               op0=ALU.mult, op1=ALU.mult).then_inc(s_coef, 1)

            @block.vector
            def _(dve):
                chain = Chain(dve, s_ch)
                dve.sem_inc(s_u, SLOTS)
                chain(nc.vector.memset(pY[:, 0:512], 0.0))
                chain(nc.vector.memset(pY[:, 512:D], 0.0))
                topk(chain, 0, 0)
                assert chain.n == 2 + TOPK_LINKS, chain.n
                dve.sem_inc(s_y, 1)
                with dve.Fori(0, blocks) as b:
                    with dve.Fori(0, pairs) as p:
                        for e in range(2):
                            s = b * HEADS + p * 2 + e
                            chain = Chain(dve, s_ch, s * STEP_LINKS + (2 + TOPK_LINKS))
                            step(dve, chain, b, p, s, e)
                            assert chain.n == STEP_LINKS, chain.n
                dve.wait_ge(s_y, steps + 1)
                nc.vector.tensor_tensor(Y[:, blocks, :], Y[:, blocks, :], pY[:], ALU.add)

            @block.gpsimd
            def _(pool):
                pool.sem_inc(s_taken, 1)
                with pool.Fori(0, steps // 2) as p:
                    for e in range(2):
                        s = p * 2 + e
                        wait_apart(pool, s_idx, s + 1)
                        nc.gpsimd.tensor_copy(mine[e][:], idx[e][:]).then_inc(s_taken, 1)
                        wait_apart(pool, s_taken, s + 2)
                        for k in range(TOPK):
                            wait_apart(pool, s_u, s * TOPK + (k + 1))
                            nc.gpsimd.indirect_dma_start(
                                out=U[k % SLOTS][:], out_offset=None, in_=t[f"u{l}"],
                                in_offset=bass.IndirectOffsetOnAxis(ap=mine[e][:, k:k + 1], axis=0)
                            ).then_inc(u_loaded[k % SLOTS], 16)
                        for k in range(TOPK):
                            wait_apart(pool, s_v, s * TOPK + (k + 1))
                            nc.gpsimd.indirect_dma_start(
                                out=Vr[k % SLOTS][:], out_offset=None, in_=t[f"v{l}"],
                                in_offset=bass.IndirectOffsetOnAxis(ap=mine[e][:, k:k + 1], axis=0)
                            ).then_inc(v_loaded[k % SLOTS], 16)

            @block.scalar
            def _(act):
                def exponentials(s, e):
                    act.wait_ge(s_idx, s + 1)
                    nc.scalar.activation(ex[e][:], top[e][:], ACT.Exp, bias=nmax[e][:], accum_out=den[e][:]).then_inc(s_exp, 1)
                exponentials(0, 0)
                with act.Fori(0, steps // 2) as p:
                    for e in range(2):
                        s = p * 2 + e
                        exponentials(s + 1, 1 - e)
                        act.wait_ge(s_u, s * TOPK + (TOPK + SLOTS))
                        nc.scalar.activation(act_t[:], dots[:], ACT.Gelu).then_inc(s_gelu, 1)
                        act.wait_ge(s_coef, s + 1)
                        for k in range(TOPK):
                            nc.scalar.activation(diag[:, k, :], ident, ACT.Copy, scale=coef[:, k:k + 1]).then_inc(s_diag, 1)

            @block.tensor
            def _(pe):
                pe.sem_inc(s_v, SLOTS)
                with pe.Fori(0, steps // 2) as p:
                    for e in range(2):
                        s = p * 2 + e
                        for k in range(TOPK):
                            j = k % SLOTS
                            pe.wait_ge(s_diag, s * TOPK + (k + 1))
                            pe.wait_ge(v_loaded[j], (base["steps"] + s) * 32 + (k // SLOTS + 1) * 16)
                            for half in range(2):
                                last = nc.tensor.matmul(pY[:, half * 512:(half + 1) * 512], diag[:, k, :],
                                                        Vr[j][:, half * 512:(half + 1) * 512],
                                                        start=(k == 0), stop=(k == TOPK - 1))
                            last.then_inc(s_v, 1)
                        pe.wait_ge(s_v, s * TOPK + (TOPK + SLOTS))
                        pe.sem_inc(s_y, 1)

        with ExitStack() as c2:
            pt = ps(f"pt{l}", [P, 4, 512], c2)
            s_t, s_r = sem(f"p{l}_t"), sem(f"p{l}_r")
            block = c2.enter_context(nc.Block())

            @block.tensor
            def _(pe):
                for k in range(KT):
                    if k >= 4:
                        pe.wait_ge(s_r, k - 3)
                    for b in range(blocks):
                        last = nc.tensor.transpose(pt[:, k % 4, b * P:(b + 1) * P], Y[:, b + 1, k * P:(k + 1) * P], ident)
                    last.then_inc(s_t, 1)

            @block.vector
            def _(dve):
                for k in range(KT):
                    dve.wait_ge(s_t, k + 1)
                    for c2_ in range(cols // T):
                        span = slice(c2_ * T, (c2_ + 1) * T)
                        last = nc.vector.scalar_tensor_tensor(out=xT[:, k, span], in0=pt[:, k % 4, span],
                                                              scalar=modT[:, l, 5, k, c2_:c2_ + 1], in1=xT[:, k, span],
                                                              op0=ALU.mult, op1=ALU.add)
                    last.then_inc(s_r, 1)
    base["steps"] += steps


def hgrn_phase(nc, t, sem, sb, ps, xT, modT, cst, vecs, ones, ident, norm_phase, lin_loads, lin_matmuls,
               lin_evac, lin_done, residual_evac, V_HGN, done):
    CTX_CHUNKS = N2 // CHUNK // 2
    ORDER = ([4, 5, 6, 7, 0, 1, 2, 3], [7, 6, 5, 4, 3, 2, 1, 0])
    with ExitStack() as c:
        QG = sb("QG", [P, 2 * HEADS, T], ctx=c)
        OT = sb("OT", [P, HEADS, T], ctx=c)
        with ExitStack() as c1:
            F = sb("F", [P, 2 * HEADS, N2], ctx=c1)
            KK = sb("KK", [P, 2 * HEADS, N2], ctx=c1)
            VI = sb("VI", [P, 4, D], ctx=c1)

            with ExitStack() as c2:
                hT = sb("h1T", [P, KT, N2], ctx=c2)
                norm_phase("n1", xT, hT, N2, 1, 0)
                wi = sb("wi", [P, KT, D], ctx=c2)
                lb = sb("lb", [P, 2, 2 * KT], ctx=c2)
                mx = sb("lbmx", [P, 2 * KT], ctx=c2)
                low = sb("low", [P, 2 * KT], ctx=c2)
                room = sb("room", [P, 2 * KT], ctx=c2)
                pl = ps("plh", [P, RING, 512], c2)
                pi = ps("pi", [P, 2, 512], c2)
                s_w, s_lb, s_e, s_i, s_ie = (sem(f"hg_{x}") for x in ("w", "lb", "e", "i", "ie"))
                block = c2.enter_context(nc.Block())

                @block.sync
                def _(sp):
                    sp.dma_start(lb[:].rearrange("p l k -> p (l k)"),
                                 t["hg_lb"].rearrange("p l d k -> p (l d k)")).then_inc(s_w, 16)
                    sp.dma_start(wi[:], t["hg_i"]).then_inc(s_w, 16)
                    lin_loads(sp, 3)
                    lin_loads(sp, 4)

                @block.tensor
                def _(pe):
                    lin_matmuls(pe, 3, pl, lambda k: hT[:, k, :], N2)
                    lin_matmuls(pe, 4, pl, lambda k: hT[:, k, 0:T], T)
                    pe.wait_ge(s_w, 32)
                    for n in range(8):
                        if n >= 2:
                            pe.wait_ge(s_ie, n - 1)
                        for k in range(KT):
                            last = nc.tensor.matmul(pi[:, n % 2, :], hT[:, k, (n // 2) * P:(n // 2 + 1) * P],
                                                    wi[:, k, (n % 2) * 512:(n % 2 + 1) * 512],
                                                    start=(k == 0), stop=(k == KT - 1))
                        last.then_inc(s_i, 1)

                @block.scalar
                def _(act):
                    act.wait_ge(s_lb, 2)
                    nc.scalar.activation(lb[:], lb[:], ACT.Exp).then_inc(s_e, 1)
                    lin_evac(act, 3, lambda i, j: nc.scalar.activation(F[:, bass.ds(i, 1), :], pl[:, j:j + 1, :], ACT.Sigmoid))
                    lin_evac(act, 4, lambda i, j: nc.scalar.copy(QG[:, bass.ds(i, 1), :], pl[:, j:j + 1, 0:T]))

                @block.vector
                def _(dve):
                    chain = Chain(dve, s_lb)
                    v = nc.vector
                    dve.wait_ge(s_w, 32)
                    chain(v.tensor_tensor(mx[:], lb[:, 0], lb[:, 1], ALU.max))
                    chain(v.tensor_tensor(lb[:], lb[:], mx[:].unsqueeze(1).broadcast_to([P, 2, 2 * KT]), ALU.subtract))
                    dve.wait_ge(s_e, 1)
                    chain(v.tensor_tensor(mx[:], lb[:, 0], lb[:, 1], ALU.add))
                    chain(v.reciprocal(mx[:], mx[:]))
                    chain(v.tensor_tensor(lb[:], lb[:], mx[:].unsqueeze(1).broadcast_to([P, 2, 2 * KT]), ALU.mult))
                    chain(v.tensor_tensor(low[:], lb[:, 0], lb[:, 1], ALU.add))
                    chain(v.tensor_tensor(low[:], low[:], lb[:, 0], ALU.subtract))
                    chain(v.tensor_scalar(room[:], low[:], -1.0, 1.0, ALU.mult, ALU.add))
                    lin_done(dve, 3)
                    for i in range(2 * HEADS):
                        chain(v.tensor_scalar(F[:, i], F[:, i], room[:, i:i + 1], low[:, i:i + 1], ALU.mult, ALU.add))
                        v.tensor_scalar(KK[:, i], F[:, i], -1.0, 1.0, ALU.mult, ALU.add)
                    for n in range(8):
                        dve.wait_ge(s_i, n + 1)
                        v.tensor_copy(VI[:, n // 2, (n % 2) * 512:(n % 2 + 1) * 512], pi[:, n % 2, :]).then_inc(s_ie, 1)
            if done("hgrn_p"):
                return

            with ExitStack() as c2:
                two = range(2)
                starts = sb("starts", [P, N2], ctx=c2)
                lf = [sb(f"lf{d}", [P, N2], ctx=c2) for d in two]
                bs = [sb(f"bs{d}", [P, N2], ctx=c2) for d in two]
                bd = [sb(f"bd{d}", [P, N2], ctx=c2) for d in two]
                eb = [sb(f"eb{d}", [P, T], ctx=c2) for d in two]
                enb = [sb(f"enb{d}", [P, T], ctx=c2) for d in two]
                ebd = [sb(f"ebd{d}", [P, N2], ctx=c2) for d in two]
                dec = [sb(f"dec{d}", [P, 8], ctx=c2) for d in two]
                qin = [sb(f"qin{d}", [P, T], ctx=c2) for d in two]
                kin = [sb(f"kin{d}", [P, T], ctx=c2) for d in two]
                kout = [sb(f"kout{d}", [P, N2], ctx=c2) for d in two]
                koT = [sb(f"koT{d}", [P, 4, P], ctx=c2) for d in two]
                AM = [sb(f"AM{d}", [P, 2, P], ctx=c2) for d in two]
                ST = [sb(f"ST{d}", [P, 7, P], ctx=c2) for d in two]
                vh = sb("vh", [P, 4, P], ctx=c2)
                pK = [ps(f"pK{d}", [P, 4, P], c2) for d in two]
                pA = ps("pA", [P, 2, 2, P], c2)
                pD = [[ps(f"pD{d}{x}", [P, 4, P], c2) for x in two] for d in two]
                pO = ps("pOh", [P, 512], c2)
                names2 = ("ln", "scan", "ex", "prod", "pt", "kot", "pa", "am", "ds", "st")
                s = {x: sem(f"gla_{x}") for x in names2 + ("o", "oc", "vst", "c", "init")}
                LINKS = 2 * 3 + 2 * 6
                block = c2.enter_context(nc.Block())

                def now(h, d):
                    return h * 2 + (d + 3)

                def before(h, d):
                    return h * 2 + (d + 1)

                def head(x, h):
                    return x[:, bass.ds(h, 1), :].rearrange("p a n -> p (a n)")

                def last_col(x, d):
                    return x[:].rearrange("p (c n) -> p c n", n=CHUNK)[:, :, (CHUNK - 1) * (1 - d):(CHUNK - 1) * (1 - d) + 1]

                @block.gpsimd
                def _(pool):
                    pool.sem_inc(s["vst"], 1)
                    with pool.Fori(0, HEADS) as h:
                        pool.wait_ge(s["o"], h + 1)
                        nc.gpsimd.tensor_copy(vh[:], VI[:, :, bass.ds(h * P, P)]).then_inc(s["vst"], 1)

                @block.scalar
                def _(act):
                    for x in ("ln", "ex", "kot"):
                        act.sem_inc(s[x], 2)
                    act.sem_inc(s["oc"], 1)
                    with act.Fori(0, HEADS) as h:
                        for d in two:
                            act.wait_ge(s["scan"], before(h, d))
                            nc.scalar.activation(lf[d][:], head(F, h + d * HEADS), ACT.Ln).then_inc(s["ln"], 1)
                        for d in two:
                            act.wait_ge(s["scan"], now(h, d))
                            act.wait_ge(s["st"], before(h, d))
                            nc.scalar.activation(eb[d][:], bs[d][:, 0:T], ACT.Exp)
                            nc.scalar.activation(enb[d][:], bs[d][:, 0:T], ACT.Exp, scale=-1.0)
                            nc.scalar.activation(dec[d][:].unsqueeze(2), last_col(bs[d], d), ACT.Exp)
                            nc.scalar.activation(ebd[d][:], bd[d][:], ACT.Exp).then_inc(s["ex"], 1)
                        for d in two:
                            act.wait_ge(s["pt"], now(h, d))
                            act.wait_ge(s["ds"], before(h, d))
                            nc.scalar.copy(koT[d][:], pK[d][:]).then_inc(s["kot"], 1)
                        act.wait_ge(s["o"], h + 2)
                        nc.scalar.copy(head(OT, h), pO[:, 0:T]).then_inc(s["oc"], 1)

                @block.vector
                def _(dve):
                    v = nc.vector
                    init = Chain(dve, s["init"])
                    init(v.memset(starts[:], 1.0))
                    init(v.memset(starts[:].rearrange("p (c n) -> p c n", n=CHUNK)[:, :, 0:1], 0.0))
                    for d in two:
                        init(v.memset(AM[d][:], 0.0))
                    for x in ("scan", "prod", "am", "st"):
                        dve.sem_inc(s[x], 2)
                    masks = cst[:, C_MASK:C_MASK + 2 * P].rearrange("p (d n) -> p d n", d=2).bitcast(U32)
                    with dve.Fori(0, HEADS) as h:
                        chain = Chain(dve, s["c"], h * LINKS)
                        for d in two:
                            dve.wait_ge(s["ln"], now(h, d))
                            dve.wait_ge(s["ex"], before(h, d))
                            way = slice(None) if d == 0 else slice(None, None, -1)
                            chain(v.tensor_tensor_scan(bs[d][:, way], starts[:], lf[d][:, way], 0.0, ALU.mult, ALU.add))
                            v.tensor_tensor(bd[d][:].rearrange("p (c n) -> p c n", n=CHUNK),
                                            last_col(bs[d], d).broadcast_to([P, 8, CHUNK]),
                                            bs[d][:].rearrange("p (c n) -> p c n", n=CHUNK),
                                            ALU.subtract).then_inc(s["scan"], 1)
                        for d in two:
                            dve.wait_ge(s["ex"], now(h, d))
                            dve.wait_ge(s["o"], h + 1)
                            chain(v.tensor_tensor(kout[d][:], head(KK, h + d * HEADS), ebd[d][:], ALU.mult))
                            chain(v.tensor_tensor(qin[d][:], head(QG, h), eb[d][:], ALU.mult))
                            v.tensor_tensor(kin[d][:], head(KK, h + d * HEADS)[:, 0:T], enb[d][:],
                                            ALU.mult).then_inc(s["prod"], 1)
                        for d in two:
                            wait_apart(dve, s["pa"], now(h, 1))
                            v.copy_predicated(AM[d][:], masks[:, d, :].unsqueeze(1).broadcast_to([P, 2, P]),
                                              pA[:, d]).then_inc(s["am"], 1)
                        for d in two:
                            dve.wait_ge(s["ds"], now(h, d))
                            for i in range(7):
                                ch = ORDER[d][i]
                                own = pD[d][ch % 2][:, ch // 2, :]
                                if i == 0:
                                    ins = v.tensor_copy(ST[d][:, 0], own)
                                else:
                                    ins = v.scalar_tensor_tensor(out=ST[d][:, i], in0=ST[d][:, i - 1],
                                                                 scalar=dec[d][:, ch:ch + 1], in1=own,
                                                                 op0=ALU.mult, op1=ALU.add)
                                chain(ins) if i < 6 else ins.then_inc(s["st"], 1)
                        assert chain.n == LINKS, chain.n

                @block.tensor
                def _(pe):
                    for x in ("pt", "pa", "ds"):
                        pe.sem_inc(s[x], 2)
                    pe.sem_inc(s["o"], 1)
                    with pe.Fori(0, HEADS) as h:
                        for d in two:
                            pe.wait_ge(s["prod"], now(h, d))
                            pe.wait_ge(s["kot"], before(h, d))
                            for m in range(4):
                                last = nc.tensor.transpose(pK[d][:, m, :], kout[d][:, m * P:(m + 1) * P], ident)
                            last.then_inc(s["pt"], 1)
                        for d in two:
                            pe.wait_ge(s["am"], before(h, 1))
                            for m in two:
                                last = nc.tensor.matmul(pA[:, d, m, :], kin[d][:, m * P:(m + 1) * P],
                                                        qin[d][:, m * P:(m + 1) * P], start=True, stop=True)
                            last.then_inc(s["pa"], 1)
                        pe.wait_ge(s["vst"], h + 2)
                        for d in two:
                            pe.wait_ge(s["kot"], now(h, d))
                            pe.wait_ge(s["st"], before(h, d))
                            for i in range(7):
                                ch = ORDER[d][i]
                                rows = slice(CHUNK * (ch % 2), CHUNK * (ch % 2 + 1))
                                last = nc.tensor.matmul(pD[d][ch % 2][:, ch // 2, :], koT[d][rows, ch // 2, :],
                                                        vh[rows, ch // 2, :], start=True, stop=True)
                            last.then_inc(s["ds"], 1)
                        pe.wait_ge(s["oc"], h + 1)
                        for d in two:
                            pe.wait_ge(s["am"], now(h, d))
                            for m in two:
                                nc.tensor.matmul(pO[:, m * P:(m + 1) * P], vh[:, m, :], AM[d][:, m, :],
                                                 start=(d == 0 and m == 0), stop=False, skip_group_check=True)
                        for d in two:
                            pe.wait_ge(s["st"], now(h, d))
                            for i in range(4):
                                ch = ORDER[d][CTX_CHUNKS + i]
                                cols = slice(ch * CHUNK, (ch + 1) * CHUNK)
                                last = nc.tensor.matmul(pO[:, cols], ST[d][:, 3 + i, :], qin[d][:, cols],
                                                        start=False, stop=(d == 1 and i == 3), skip_group_check=True)
                        last.then_inc(s["o"], 1)
        if done("gla"):
            return

        with ExitStack() as c1:
            sq = sb("osq", [P, HEADS, T], ctx=c1)
            rs = sb("ors", [P, HEADS, T], ctx=c1)
            pR = ps("pR", [P, HEADS, T], c1)
            pl = ps("plo", [P, RING, 512], c1)
            r_act, r_pe, r_dve = sem("r_act"), sem("r_pe"), sem("r_dve")
            block = c1.enter_context(nc.Block())

            @block.sync
            def _(sp):
                lin_loads(sp, 5)

            @block.scalar
            def _(act):
                for h in range(HEADS):
                    nc.scalar.activation(sq[:, h], OT[:, h], ACT.Square).then_inc(r_act, 1)
                nc.scalar.activation(QG[:, HEADS:], QG[:, HEADS:], ACT.Silu).then_inc(r_act, 1)
                act.wait_ge(r_dve, 1)
                nc.scalar.activation(rs[:], rs[:], ACT.Sqrt).then_inc(r_act, 1)

            @block.vector
            def _(dve):
                chain = Chain(dve, r_dve)
                dve.wait_ge(r_pe, 1)
                chain(nc.vector.tensor_scalar(rs[:], pR[:], 1.0 / P, EPS, ALU.mult, ALU.add))
                dve.wait_ge(r_act, HEADS + 2)
                chain(nc.vector.reciprocal(rs[:], rs[:]))
                chain(nc.vector.tensor_tensor(rs[:], rs[:], OT[:], ALU.mult))
                for h in range(HEADS):
                    chain(nc.vector.scalar_tensor_tensor(out=OT[:, h], in0=rs[:, h], scalar=vecs[:, V_HGN + h:V_HGN + h + 1],
                                                         in1=QG[:, HEADS + h], op0=ALU.mult, op1=ALU.mult))
                lin_evac(dve, 5, residual_evac(5, pl, T, 1, 2))

            @block.tensor
            def _(pe):
                for h in range(HEADS):
                    pe.wait_ge(r_act, h + 1)
                    last = nc.tensor.matmul(pR[:, h], ones[:], sq[:, h], start=True, stop=True)
                last.then_inc(r_pe, 1)
                pe.wait_ge(r_dve, 3 + HEADS)
                lin_matmuls(pe, 5, pl, lambda k: OT[:, k, :], T)

def host_arrays(a):
    import numpy as np
    f = {k: np.asarray(v) for k, v in a.items()}

    def tiles(w):
        K, N = w.shape
        return np.ascontiguousarray(w.reshape(K // P, P, N // P, P).transpose(2, 1, 0, 3).reshape(N // P, P, -1))

    def cols(v):
        return v.reshape(-1, P).T

    def swapped(w):
        return w.reshape(w.shape[0], -1, 2)[:, :, ::-1].reshape(w.shape)

    o = {}
    o["xT"] = np.concatenate([f["x"][0], f["ctx"][0]], axis=0).T.reshape(KT, P, N2).transpose(1, 0, 2)
    o["cT"] = np.stack([f["c"][0], f["c_ctx"]], axis=1).reshape(KT, P, 2).transpose(1, 0, 2)
    o["ada_w"] = f["ada_w"].reshape(2, KT, P, 12, 512).transpose(0, 3, 2, 1, 4).reshape(24, P, KT * 512)
    o["ada_b"] = cols(f["ada_b"].reshape(-1))
    w = f["ab_w_in"][0]
    kr = w[:, 384:416]
    o["w_in"] = tiles(np.concatenate([w[:, :384], w[:, 320:384], kr, swapped(kr), w[:, 416:]], axis=1))
    wq = f["mla_w_uq"][0].reshape(256, HEADS, QK)
    rope = wq[:, :, NOPE:]
    wq = np.concatenate([wq, rope.reshape(256, HEADS, ROPE // 2, 2)[..., ::-1].reshape(256, HEADS, ROPE)], axis=2)
    o["w_uq"] = wq.reshape(2, P, HEADS * P).transpose(1, 0, 2)
    wkv = f["mla_w_ukv"][0].reshape(P, HEADS, NOPE + VDIM)
    o["w_uk"] = wkv[:, :, :NOPE].reshape(P, -1)
    o["w_uv"] = wkv[:, :, NOPE:].reshape(P, -1)
    o["conv_w"] = f["conv_w"][0].reshape(TAPS, CONV_T, P).transpose(2, 1, 0)
    o["w_out"] = tiles(f["ab_w_out"][0])
    hg = f["hg_w_in"][0]
    o["hg_zz"] = tiles(hg[:, 1024:3072])
    o["hg_qg"] = tiles(np.concatenate([hg[:, 0:1024], hg[:, 4096:5120]], axis=1))
    o["hg_i"] = hg[:, 3072:4096].reshape(KT, P, D).transpose(1, 0, 2)
    o["hg_out"] = tiles(f["hg_w_out"][0])
    o["hg_lb"] = f["hg_lower_bound"].reshape(2, 2, KT, P).transpose(3, 0, 1, 2)
    for l in range(2):
        o[f"peer_q{l}"] = tiles(f["peer_w_q"][l])
        o[f"keys{l}"] = f["peer_sub_keys"][l].reshape(16, P, P).transpose(2, 0, 1)
        o[f"u{l}"] = f["peer_u"][l]
        o[f"v{l}"] = f["peer_v"][l]
    o["vecs"] = np.concatenate([cols(f[k].reshape(-1)) for k in (
        "norm1_g", "norm2_g", "final_norm_g", "mla_q_norm_g", "mla_kv_norm_g", "conv_b",
        "conv_ln_g", "conv_ln_b", "hg_norm_g")], axis=1)

    cst = np.zeros((P, C_END), np.float32)
    cst[:, C_ID:C_ID + P] = np.eye(P)
    s, q = np.arange(P)[:, None], np.arange(P)[None, :]
    same = s // CHUNK == q // CHUNK
    cst[:, C_MASK:C_MASK + P] = same & (s <= q)
    cst[:, C_MASK + P:C_MASK + 2 * P] = same & (s >= q)
    cst[:, C_IOTA:C_IOTA + TOPK] = np.arange(TOPK)
    tok = np.arange(T)
    inv = 10000.0 ** (-np.arange(0, ROPE // 2, 2, dtype=np.float64) / (ROPE // 2))
    ang = np.concatenate([(tok // 64)[:, None] * inv, (tok % 64)[:, None] * inv], axis=1).T
    cst[NOPE:QK, C_COS:C_COS + T] = np.repeat(np.cos(ang), 2, axis=0)
    sign = np.tile([-1.0, 1.0], ROPE // 2)[:, None]
    cst[NOPE:QK, C_SIN:C_SIN + T] = np.repeat(np.sin(ang), 2, axis=0) * sign
    o["consts"] = cst
    return {k: np.ascontiguousarray(v) for k, v in o.items()}


def kernel(**inputs):
    import numpy as np
    import concourse.bacc as bacc
    from concourse.bass_utils import run_bass_kernel_spmd

    arrays = host_arrays(inputs)
    nc = bacc.Bacc("TRN2", target_bir_lowering=False, num_devices=1)
    t = {k: nc.dram_tensor(k + "_dram", v.shape, mybir.dt.from_np(v.dtype), kind="ExternalInput").ap()
         for k, v in arrays.items()}
    out = nc.dram_tensor("out_dram", (P, KT, T), FP32, kind="ExternalOutput").ap()
    build(nc, t, out)
    r = run_bass_kernel_spmd(nc, [{k + "_dram": v for k, v in arrays.items()}], core_ids=[0])
    y = r.results[0]["out_dram"]
    return np.ascontiguousarray(np.asarray(y).transpose(2, 1, 0).reshape(1, T, D))
```

```python
import concourse.bass as bass
from concourse import mybir
from contextlib import ExitStack

FP32 = mybir.dt.float32
U32 = mybir.dt.uint32
ALU = mybir.AluOpType
ACT = mybir.ActivationFunctionType
AX = mybir.AxisListType.X

P = 128
D = 1024
KT = D // P
T = 256
N2 = 2 * T
EPS = 1e-6
MOD_TILES = 6 * KT
HEADS = 8
NOPE, ROPE, VDIM = 64, 32, 64
QK = NOPE + ROPE
MLA_SCALE = QK ** -0.5
CONV_T = 4
TAPS = 31
HALO = TAPS // 2
CHUNK = 64
TOPK = 16
RING = 4
SLOTS = 8
NEG = -3.0e38

C_ID, C_MASK, C_IOTA, C_COS, C_SIN, C_END = 0, 128, 384, 400, 656, 912


def wait_apart(eng, sem, value):
    if not isinstance(value, int):
        value = eng.to_reg(value)
        eng.wait_ge(sem, 1)
    eng.wait_ge(sem, value)


class Chain:

    def __init__(self, eng, sem, base=0):
        self.eng, self.sem, self.base, self.n = eng, sem, base, 0

    def __call__(self, ins):
        self.n += 1
        ins.then_inc(self.sem, 1)
        self.eng.wait_ge(self.sem, self.base + self.n)

    def apart(self, ins):
        self.n += 1
        ins.then_inc(self.sem, 1)
        wait_apart(self.eng, self.sem, self.base + self.n)


def build(nc, t, out, stop=None):
    with ExitStack() as whole:
        def sem(name):
            return whole.enter_context(nc.semaphore(name))

        def sb(name, shape, dt=FP32, ctx=whole):
            return ctx.enter_context(nc.sbuf_tensor(name, shape, dt))

        def ps(name, shape, ctx):
            return ctx.enter_context(nc.psum_tensor(name, shape, FP32))

        xT = sb("xT", [P, KT, N2])
        cst = sb("cst", [P, C_END])
        ones = sb("ones", [P, P])
        vecs = sb("vecs", [P, 128])
        modT = sb("modT", [P, 2, 6, KT, 2])
        gainT = sb("gainT", [P, 2, 2, KT, 2])
        wring = sb("wring", [P, RING, KT * P])
        ident = cst[:, C_ID:C_ID + P]

        V_N1, V_N2, V_FIN, V_QG, V_KVG, V_CB, V_LNG, V_LNB, V_HGN = 0, 16, 32, 40, 42, 43, 47, 51, 55

        w_loaded = [sem(f"w_loaded{j}") for j in range(RING)]
        acc_ready = sem("acc_ready")
        acc_free = sem("acc_free")
        lin = [("w_in", 12), ("w_out", 8), ("peer_q0", 16),
               ("hg_zz", 16), ("hg_qg", 16), ("hg_out", 8), ("peer_q1", 16)]
        first = {}
        g = 0
        for name, n in lin:
            first[name] = g
            g += n
        total_tiles = g

        def load_tile(sp, name, i, j, g):
            if not (isinstance(g, int) and g < RING):
                sp.wait_ge(acc_ready, g - (RING - 1))
            src = t[name][i] if isinstance(i, int) else \
                t[name][bass.ds(i, 1), :, :].rearrange("a p n -> p (a n)")
            sp.dma_start(wring[:, j, :], src).then_inc(w_loaded[j], 16)

        state = {"which": -1}

        def lin_loads(sp, which):
            name, n = lin[which]
            state["which"] = which
            g0 = first[name]
            if n > RING:
                with sp.Fori(0, n // RING - 1) as it:
                    for j in range(RING):
                        load_tile(sp, name, it * RING + (RING + j), j, it * RING + (g0 + RING + j))
            if which + 1 < len(lin):
                for j in range(RING):
                    load_tile(sp, lin[which + 1][0], j, j, g0 + n + j)

        def lin_matmuls(pe, which, psum, rhs, n_cols):
            name, n = lin[which]
            g0 = first[name]
            with pe.Fori(0, n // RING) as it:
                for j in range(RING):
                    pe.wait_ge(w_loaded[j], it * 16 + (g0 // RING + 1) * 16)
                    pe.wait_ge(acc_free, it * RING + (g0 + j + 1))
                    for k in range(KT):
                        last = nc.tensor.matmul(psum[:, j, 0:n_cols], wring[:, j, k * P:(k + 1) * P],
                                                rhs(k), start=(k == 0), stop=(k == KT - 1))
                    last.then_inc(acc_ready, 1)

        def lin_evac(eng, which, one):
            name, n = lin[which]
            g0 = first[name]
            with eng.Fori(0, n // RING) as it:
                for j in range(RING):
                    eng.wait_ge(acc_ready, it * RING + (g0 + j + 1))
                    one(it * RING + j, j).then_inc(acc_free, 1)

        def lin_done(eng, which, tiles=None):
            name, n = lin[which]
            eng.wait_ge(acc_free, RING + first[name] + (tiles or n))

        s_xT, s_const, s_cond, s_sc, s_mod = sem("s_xT"), sem("s_const"), sem("s_cond"), sem("s_sc"), sem("s_mod")
        a_loaded = [sem(f"a_loaded{j}") for j in range(RING)]
        a_ready = sem("a_ready")
        a_free = sem("a_free")
        a_turned = sem("a_turned")
        GROUPS = 6 * D // 512
        cond = ExitStack()
        scT = sb("scT", [P, KT, 2], ctx=cond)
        adab = sb("adab", [P, 2, MOD_TILES], ctx=cond)

        def mod_finish(chain, l, columns):
            chain(nc.vector.tensor_tensor(modT[:, l].rearrange("p m k c -> p (m k) c"), columns,
                                          adab[:, l].unsqueeze(2).broadcast_to([P, MOD_TILES, 2]), ALU.add))
            for w in range(2):
                gain = vecs[:, (V_N1, V_N2)[w] + 8 * l:][:, 0:8].unsqueeze(2).broadcast_to([P, KT, 2])
                chain(nc.vector.scalar_tensor_tensor(
                    out=gainT[:, l, w], in0=modT[:, l, 3 * w + 1], scalar=1.0, in1=gain,
                    op0=ALU.add, op1=ALU.mult))

        with ExitStack() as c:
            aw = sb("aw", [P, RING, KT * 512], ctx=c)
            rows = sb("rows", [P, RING, 512], ctx=c)
            pm = ps("pm", [P, RING, 512], c)
            pt = ps("pt", [P, 4 * (GROUPS + 1), 2], c)
            block = c.enter_context(nc.Block())

            @block.sync
            def _(sp):
                sp.dma_start(scT[:], t["cT"]).then_inc(s_cond, 16)
                sp.dma_start(aw[:, 0, :], t["ada_w"][0]).then_inc(a_loaded[0], 16)
                sp.dma_start(cst[:], t["consts"]).then_inc(s_const, 16)
                sp.dma_start(vecs[:, 0:63], t["vecs"]).then_inc(s_const, 16)
                sp.dma_start(adab[:].rearrange("p l n -> p (l n)"), t["ada_b"]).then_inc(s_const, 16)
                for j in range(1, RING):
                    sp.dma_start(aw[:, j, :], t["ada_w"][j]).then_inc(a_loaded[j], 16)
                sp.dma_start(xT[:], t["xT"]).then_inc(s_xT, 16)
                with sp.Fori(0, GROUPS // RING - 1) as it:
                    for j in range(RING):
                        sp.wait_ge(a_ready, it * RING + (j + 1))
                        sp.dma_start(aw[:, j, :], t["ada_w"][bass.ds(it * RING + (RING + j), 1), :, :]
                                     .rearrange("a p n -> p (a n)")).then_inc(a_loaded[j], 16)
                for j in range(RING):
                    load_tile(sp, lin[0][0], j, j, j)
                sp.wait_ge(s_xT, 16)

            @block.gpsimd
            def _(pool):
                nc.gpsimd.memset(ones[:], 1.0)

            @block.scalar
            def _(act):
                act.wait_ge(s_cond, 16)
                nc.scalar.activation(scT[:], scT[:], ACT.Silu).then_inc(s_sc, 1)

            @block.tensor
            def _(pe):
                def turn(j, n):
                    for q in range(4):
                        last = nc.tensor.matmul(pt[:, bass.ds(n * 4 + q, 1), :].rearrange("p a c -> p (a c)"),
                                                rows[:, j, q * P:(q + 1) * P], ident[:, 0:2], start=True, stop=True)
                    last.then_inc(a_turned, 1)

                pe.wait_ge(s_sc, 1)
                pe.wait_ge(s_const, 48)
                pe.wait_ge(s_mod, 1)
                with pe.Fori(0, GROUPS // RING) as it:
                    for j in range(RING):
                        pe.wait_ge(a_loaded[j], it * 16 + 16)
                        pe.wait_ge(a_free, it * RING + (j + 1))
                        for k in range(KT):
                            last = nc.tensor.matmul(pm[0:2, j, :], scT[:, k, :], aw[:, j, k * 512:(k + 1) * 512],
                                                    start=(k == 0), stop=(k == KT - 1))
                        last.then_inc(a_ready, 1)
                        pe.wait_ge(a_free, it * RING + (RING + j))
                        turn((j - 1) % RING, it * RING + j)
                pe.wait_ge(a_free, RING + GROUPS)
                turn(RING - 1, GROUPS)

            @block.vector
            def _(dve):
                chain = Chain(dve, s_mod)
                chain(nc.vector.memset(rows[:], 0.0))
                dve.sem_inc(a_free, RING)
                dve.sem_inc(a_turned, RING - 1)
                dve.sem_inc(acc_free, RING)
                with dve.Fori(0, GROUPS // RING) as it:
                    for j in range(RING):
                        dve.wait_ge(a_ready, it * RING + (j + 1))
                        dve.wait_ge(a_turned, it * RING + (j + 1))
                        nc.vector.tensor_copy(rows[0:2, j, :], pm[0:2, j, :]).then_inc(a_free, 1)
                dve.wait_ge(a_turned, RING - 1 + GROUPS + 1)
                dve.wait_ge(s_const, 48)
                mod_finish(chain, 0, pt[:, 4:, :])

        def done(name):
            if stop == name:
                with nc.Block() as block:
                    @block.sync
                    def _(sp):
                        nxt = lin[state["which"]] if state["which"] >= 0 else ("w_in", -0)
                        if state["which"] < 0:
                            nxt = ("w_in", 0)
                        for j in range(RING):
                            sp.wait_ge(w_loaded[j], (first[nxt[0]] + nxt[1] + RING) // RING * 16)
            return stop == name

        if done("mod"):
            return

        def norm_phase(tag, src, dst, cols, l, w):
            sq_ready, sum_ready, rs_ready, y_ready = (sem(f"{tag}_{x}") for x in ("sq", "sum", "rs", "y"))
            s_done = sem(f"{tag}_done")
            with ExitStack() as c:
                sq = sb(f"{tag}_sqb", [P, KT, cols], ctx=c)
                rs = sb(f"{tag}_rsb", [P, cols], ctx=c)
                pn = ps(f"{tag}_pn", [P, 512], c)
                block = c.enter_context(nc.Block())

                def affine(eng, k):
                    for c2 in range(cols // T):
                        part = dst[:, k, c2 * T:(c2 + 1) * T]
                        if l is None:
                            a, b = vecs[:, V_FIN + k:V_FIN + k + 1], 0.0
                        else:
                            a, b = gainT[:, l, w, k, c2:c2 + 1], modT[:, l, 3 * w, k, c2:c2 + 1]
                        if eng is nc.scalar:
                            last = eng.activation(part, part, ACT.Identity, scale=a, bias=b)
                        elif l is None:
                            last = eng.tensor_scalar(part, part, a, None, ALU.mult)
                        else:
                            last = eng.tensor_scalar(part, part, a, b, ALU.mult, ALU.add)
                    return last

                @block.scalar
                def _(act):
                    for k in range(KT):
                        nc.scalar.activation(sq[:, k], src[:, k, 0:cols], ACT.Square).then_inc(sq_ready, 1)
                    act.wait_ge(rs_ready, 1)
                    nc.scalar.activation(rs[:], rs[:], ACT.Sqrt).then_inc(s_done, 1)
                    for k in range(0, KT, 2):
                        act.wait_ge(y_ready, k + 1)
                        affine(nc.scalar, k).then_inc(s_done, 1)

                @block.tensor
                def _(pe):
                    for k in range(KT):
                        pe.wait_ge(sq_ready, k + 1)
                        last = nc.tensor.matmul(pn[:, 0:cols], ones[:], sq[:, k], start=(k == 0), stop=(k == KT - 1))
                    last.then_inc(sum_ready, 1)

                @block.vector
                def _(dve):
                    dve.wait_ge(sum_ready, 1)
                    nc.vector.tensor_scalar(rs[:], pn[:, 0:cols], 1.0 / D, EPS, ALU.mult, ALU.add).then_inc(rs_ready, 1)
                    dve.wait_ge(s_done, 1)
                    nc.vector.reciprocal(rs[:], rs[:]).then_inc(rs_ready, 1)
                    dve.wait_ge(rs_ready, 2)
                    for k in range(KT):
                        nc.vector.tensor_tensor(dst[:, k, 0:cols], src[:, k, 0:cols], rs[:], ALU.mult).then_inc(y_ready, 1)
                        if k >= 1 and (k - 1) % 2 == 1:
                            dve.wait_ge(y_ready, k)
                            affine(nc.vector, k - 1)
                    dve.wait_ge(y_ready, KT)
                    affine(nc.vector, KT - 1)

        def residual_evac(which, psum, cols, l, part):
            def one(i, j):
                for c2 in range(cols // T):
                    span = slice(c2 * T, (c2 + 1) * T)
                    last = nc.vector.scalar_tensor_tensor(
                        out=xT[:, bass.ds(i, 1), span], in0=psum[:, j:j + 1, span],
                        scalar=modT[:, l, part, bass.ds(i, 1), c2:c2 + 1].rearrange("p a c -> p (a c)"),
                        in1=xT[:, bass.ds(i, 1), span], op0=ALU.mult, op1=ALU.add)
                return last
            return one

        with ExitStack() as c0:
            mix = sb("mix", [P, KT, N2], ctx=c0)
            with ExitStack() as c1:
                cT = sb("cT", [P, 12, N2], ctx=c1)
                with ExitStack() as c:
                    hT = sb("hT0", [P, KT, N2], ctx=c)
                    norm_phase("n0", xT, hT, N2, 0, 0)
                    if done("n0"):
                        return
                    pl = ps("pl0", [P, RING, 512], c)
                    block = c.enter_context(nc.Block())

                    @block.sync
                    def _(sp):
                        lin_loads(sp, 0)

                    @block.tensor
                    def _(pe):
                        lin_matmuls(pe, 0, pl, lambda k: hT[:, k, :], N2)

                    @block.scalar
                    def _(act):
                        lin_evac(act, 0, lambda i, j: nc.scalar.copy(cT[:, bass.ds(i, 1), :], pl[:, j:j + 1, :]))
                if done("w_in"):
                    return
                mla_phase(nc, t, sem, sb, ps, cT, mix, cst, vecs, ones, ident,
                          (V_QG, V_KVG, V_CB, V_LNG, V_LNB), scT, mod_finish, done)
                if done("mla") or done("proj"):
                    return
            with ExitStack() as c:
                pl = ps("pl1", [P, RING, 512], c)
                block = c.enter_context(nc.Block())

                @block.sync
                def _(sp):
                    lin_loads(sp, 1)

                @block.tensor
                def _(pe):
                    lin_matmuls(pe, 1, pl, lambda k: mix[:, k, :], N2)

                @block.vector
                def _(dve):
                    lin_evac(dve, 1, residual_evac(1, pl, N2, 0, 2))
        cond.close()
        if done("l0mix"):
            return

        u_loaded = [sem(f"u_loaded{j}") for j in range(SLOTS)]
        v_loaded = [sem(f"v_loaded{j}") for j in range(SLOTS)]

        def peer_layer(l, cols):
            which = {0: 2, 1: 6}[l]
            peer_phase(nc, t, sem, sb, ps, xT, modT, cst, ident, l, cols, norm_phase, lin_loads, first[lin[which][0]],
                       w_loaded, wring, acc_ready, acc_free, which, u_loaded, v_loaded, l * HEADS * N2 // P)

        peer_layer(0, N2)
        if done("peer0"):
            return

        hgrn_phase(nc, t, sem, sb, ps, xT, modT, cst, vecs, ones, ident, norm_phase, lin_loads,
                   lin_matmuls, lin_evac, lin_done, residual_evac, V_HGN, done)
        if done("hgrn_p") or done("hgrn"):
            return
        peer_layer(1, T)

        s_out = sem("s_out")
        with ExitStack() as c:
            yT = sb("yT", [P, KT, T], ctx=c)
            norm_phase("nf", xT, yT, T, None, None)
            block = c.enter_context(nc.Block())

            @block.sync
            def _(sp):
                sp.dma_start(out, yT[:]).then_inc(s_out, 16)
                sp.wait_ge(s_out, 16)


def mla_phase(nc, t, sem, sb, ps, cT, mix, cst, vecs, ones, ident, cols, scT, mod_finish, done):
    V_QG, V_KVG, V_CB, V_LNG, V_LNB = cols
    rope_rows = slice(NOPE, QK)
    with ExitStack() as c:
        Q = sb("Q", [QK, HEADS, N2], ctx=c)
        K = sb("K", [QK, HEADS, N2], ctx=c)
        V = sb("V", [P, 4, HEADS * VDIM], ctx=c)
        gated = sb("gated", [P, CONV_T, 2, T + 2 * HALO], ctx=c)
        convw = sb("convw", [P, CONV_T, TAPS], ctx=c)
        GROUPS = 6 * D // 512
        aw = sb("aw1", [P, 2, KT * 512], ctx=c)
        rows = sb("rows1", [P, 2, 512], ctx=c)
        m1_loaded = [sem(f"m1_loaded{j}") for j in range(2)]
        m1_ready, m1_copied, m1_turned, m1_done = (sem(f"m1_{x}") for x in ("ready", "copied", "turned", "done"))
        s_w = sem("mla_w")
        s_act, s_pe, s_dve, s_pool = sem("mla_act"), sem("mla_pe"), sem("mla_dve"), sem("mla_pool")
        s_q, s_qe, s_k, s_ke, s_v, s_ve = (sem(f"mla_{x}") for x in ("q", "qe", "k", "ke", "v", "ve"))

        with ExitStack() as c2:
            wuq = sb("wuq", [P, 2, HEADS * P], ctx=c2)
            wuk = sb("wuk", [P, HEADS * NOPE], ctx=c2)
            wuv = sb("wuv", [P, HEADS * VDIM], ctx=c2)
            lat = sb("lat", [P, 3, N2], ctx=c2)
            rs = sb("lat_rs", [P, 2, N2], ctx=c2)
            QS = sb("QS", [QK, HEADS, T], ctx=c2)
            KS = sb("KS", [QK, N2], ctx=c2)
            KR = sb("KR", [QK, N2], ctx=c2)
            pn = ps("mla_pn", [P, 2, 512], c2)
            pq = ps("mla_pq", [P, 3, 512], c2)
            pk = ps("mla_pk", [P, 3, 512], c2)
            block = c2.enter_context(nc.Block())

            @block.sync
            def _(sp):
                sp.dma_start(wuq[:], t["w_uq"]).then_inc(s_w, 16)
                sp.dma_start(wuk[:], t["w_uk"]).then_inc(s_w, 16)
                sp.dma_start(wuv[:], t["w_uv"]).then_inc(s_w, 16)
                sp.dma_start(convw[:], t["conv_w"]).then_inc(s_w, 16)
                for j in range(2):
                    sp.dma_start(aw[:, j, :], t["ada_w"][GROUPS + j]).then_inc(m1_loaded[j], 16)

            @block.gpsimd
            def _(pool):
                nc.gpsimd.memset(rows[:], 0.0)
                nc.gpsimd.memset(gated[:], 0.0).then_inc(s_pool, 1)

            @block.scalar
            def _(act):
                nc.scalar.activation(lat[:], cT[:, 0:3, :], ACT.Square).then_inc(s_act, 1)
                nc.scalar.copy(KS[rope_rows, 0:T], cT[QK:P, 3, 0:T]).then_inc(s_act, 1)
                act.wait_ge(s_dve, 2)
                nc.scalar.activation(rs[:], rs[:], ACT.Sqrt).then_inc(s_act, 1)
                for h in range(HEADS):
                    act.wait_ge(s_q, h + 1)
                    nc.scalar.copy(Q[:, h, :], pq[0:QK, h % 3, :])
                    nc.scalar.copy(QS[rope_rows, h, :], pq[QK:P, h % 3, 0:T]).then_inc(s_qe, 1)
                for m in range(4):
                    act.wait_ge(s_v, m + 1)
                    nc.scalar.copy(V[:, m, :], pq[:, (HEADS + m) % 3, :]).then_inc(s_qe, 1)

            @block.tensor
            def _(pe):
                pe.wait_ge(s_act, 1)
                for k in range(2):
                    nc.tensor.matmul(pn[:, 0, :], ones[:], lat[:, k, :], start=(k == 0), stop=(k == 1))
                nc.tensor.matmul(pn[:, 1, :], ones[:], lat[:, 2, :], start=True, stop=True).then_inc(s_pe, 1)
                pe.wait_ge(s_w, 64)
                pe.wait_ge(s_dve, 6)
                for h in range(HEADS):
                    if h >= 3:
                        pe.wait_ge(s_qe, h - 2)
                    for k in range(2):
                        last = nc.tensor.matmul(pq[:, h % 3, :], wuq[:, k, h * P:(h + 1) * P], lat[:, k, :],
                                                start=(k == 0), stop=(k == 1))
                    last.then_inc(s_q, 1)
                    if h >= 3:
                        pe.wait_ge(s_ke, h - 2)
                    nc.tensor.matmul(pk[0:NOPE, h % 3, :], wuk[:, h * NOPE:(h + 1) * NOPE], lat[:, 2, :],
                                     start=True, stop=True).then_inc(s_k, 1)
                for m in range(4):
                    pe.wait_ge(s_qe, HEADS + m - 2)
                    nc.tensor.matmul(pq[:, (HEADS + m) % 3, :], lat[:, 2, m * P:(m + 1) * P], wuv[:],
                                     start=True, stop=True).then_inc(s_v, 1)

            @block.vector
            def _(dve):
                chain = Chain(dve, s_dve)
                dve.wait_ge(s_pe, 1)
                chain(nc.vector.tensor_scalar(rs[:, 0], pn[:, 0], 1.0 / 256, EPS, ALU.mult, ALU.add))
                chain(nc.vector.tensor_scalar(rs[:, 1], pn[:, 1], 1.0 / 128, EPS, ALU.mult, ALU.add))
                dve.wait_ge(s_act, 3)
                chain(nc.vector.reciprocal(rs[:], rs[:]))
                for k in range(3):
                    chain(nc.vector.scalar_tensor_tensor(
                        out=lat[:, k], in0=cT[:, k], scalar=vecs[:, V_QG + k:V_QG + k + 1],
                        in1=rs[:, k // 2], op0=ALU.mult, op1=ALU.mult))
                cos, sin = cst[rope_rows, C_COS:C_COS + T], cst[rope_rows, C_SIN:C_SIN + T]
                kr = cT[rope_rows, 3, 0:T]
                chain(nc.vector.tensor_tensor(KR[rope_rows, 0:T], kr, cos, ALU.mult))
                chain(nc.vector.tensor_tensor(KS[rope_rows, 0:T], KS[rope_rows, 0:T], sin, ALU.mult))
                chain(nc.vector.tensor_tensor(KR[rope_rows, 0:T], KR[rope_rows, 0:T], KS[rope_rows, 0:T], ALU.add))
                chain(nc.vector.tensor_copy(KR[rope_rows, T:N2], cT[rope_rows, 3, T:N2]))
                nc.vector.tensor_copy(K[rope_rows], KR[rope_rows, :].unsqueeze(1).broadcast_to([ROPE, HEADS, N2]))
                for h in range(HEADS):
                    dve.wait_ge(s_k, h + 1)
                    nc.vector.tensor_copy(K[0:NOPE, h, :], pk[0:NOPE, h % 3, :]).then_inc(s_ke, 1)
                dve.wait_ge(s_qe, HEADS)
                bc = [ROPE, HEADS, T]
                qx = Q[rope_rows, :, 0:T]
                chain(nc.vector.tensor_tensor(qx, qx, cos.unsqueeze(1).broadcast_to(bc), ALU.mult))
                chain(nc.vector.tensor_tensor(QS[rope_rows], QS[rope_rows], sin.unsqueeze(1).broadcast_to(bc), ALU.mult))
                chain(nc.vector.tensor_tensor(qx, qx, QS[rope_rows], ALU.add))
        if done("proj"):
            return

        O = sb("O", [P, 4, HEADS * VDIM], ctx=c)
        conv = sb("conv", [P, CONV_T, 2, T], ctx=c)
        with ExitStack() as c2:
            prob = sb("prob", [P, 2, N2], ctx=c2)
            probT = sb("probT", [P, 2, 4, P], ctx=c2)
            sg = sb("sg", [P, CONV_T, 2, T], ctx=c2)
            nmx = sb("nmx", [P, 2], ctx=c2)
            den = sb("den", [P, 2], ctx=c2)
            rden = sb("rden", [P, 2], ctx=c2)
            pS = ps("pS", [P, 2, 512], c2)
            pT = ps("pT", [P, 2, 4, P], c2)
            pO = ps("pO", [P, 2, 512], c2)
            pm = ps("pm1", [P, 2, 512], c2)
            turned = pO[:, 0, 256:256 + 8 * GROUPS].rearrange("p (n c) -> p n c", c=2)
            at = {x: sem(f"att_{x}") for x in ("s", "mx", "nmx", "exp", "t", "copied", "o", "rd", "norm", "sg", "gated", "conv")}
            block = c2.enter_context(nc.Block())
            units = [(m, h) for m in range(4) for h in range(HEADS)]
            copied_at = [-(-KT * (g + 1) // 3) for g in range(GROUPS)]
            turned_at = [u + 1 + (u + 1) % 2 for u in copied_at]

            def keys(m):
                return (0, 4) if m < 2 else (2, 4)

            @block.sync
            def _(sp):
                for g in range(2, GROUPS):
                    sp.wait_ge(m1_ready, g - 1)
                    sp.dma_start(aw[:, g % 2, :], t["ada_w"][GROUPS + g]).then_inc(m1_loaded[g % 2], 16)

            @block.tensor
            def _(pe):
                def modulation(x):
                    g, k = x // KT, x % KT
                    if g < GROUPS:
                        if k == 0:
                            pe.wait_ge(m1_loaded[g % 2], (g // 2 + 1) * 16)
                            if g >= 2:
                                pe.wait_ge(m1_copied, g - 1)
                        last = nc.tensor.matmul(pm[0:2, g % 2, :], scT[:, k, :], aw[:, g % 2, k * 512:(k + 1) * 512],
                                                start=(k == 0), stop=(k == KT - 1))
                        if k == KT - 1:
                            last.then_inc(m1_ready, 1)

                def turn(g):
                    pe.wait_ge(m1_copied, g + 1)
                    for q in range(4):
                        last = nc.tensor.matmul(turned[:, g * 4 + q, :], rows[:, g % 2, q * P:(q + 1) * P],
                                                ident[:, 0:2], start=True, stop=True)
                    last.then_inc(m1_turned, 1)

                for u in range(len(units) + 2):
                    modulation(3 * u)
                    if u < len(units):
                        m, h = units[u]
                        lo, hi = keys(m)
                        if u >= 2:
                            pe.wait_ge(at["exp"], u - 1)
                        nc.tensor.matmul(pS[:, u % 2, lo * P:hi * P], Q[:, h, m * P:(m + 1) * P],
                                         K[:, h, lo * P:hi * P], start=True, stop=True).then_inc(at["s"], 1)
                    modulation(3 * u + 1)
                    if 1 <= u <= len(units):
                        v = u - 1
                        lo, hi = keys(units[v][0])
                        pe.wait_ge(at["exp"], v + 1)
                        if v >= 2:
                            pe.wait_ge(at["copied"], v - 1)
                        for j in range(lo, hi):
                            last = nc.tensor.transpose(pT[:, v % 2, j, :], prob[:, v % 2, j * P:(j + 1) * P], ident)
                        last.then_inc(at["t"], 1)
                    modulation(3 * u + 2)
                    if u >= 2:
                        v = u - 2
                        m, h = units[v]
                        lo, hi = keys(m)
                        pe.wait_ge(at["copied"], v + 1)
                        if v >= 2:
                            pe.wait_ge(at["norm"], v - 1)
                        if u in turned_at:
                            turn(turned_at.index(u))
                        for j in range(lo, hi):
                            last = nc.tensor.matmul(pO[:, v % 2, 0:VDIM], probT[:, v % 2, j, :],
                                                    V[:, j, h * VDIM:(h + 1) * VDIM], start=(j == lo), stop=(j == hi - 1))
                        last.then_inc(at["o"], 1)
                pe.wait_ge(at["norm"], len(units))
                turn(GROUPS - 1)

            @block.scalar
            def _(act):
                nc.scalar.activation(sg[:].rearrange("p a b n -> p (a b n)"),
                                     cT[:, 8:12, :].rearrange("p a n -> p (a n)"), ACT.Sigmoid).then_inc(at["sg"], 1)
                for u in range(len(units) + 1):
                    if u < len(units):
                        lo, hi = keys(units[u][0])
                        act.wait_ge(at["nmx"], u + 1)
                        if u >= 2:
                            act.wait_ge(at["t"], u - 1)
                            act.wait_ge(at["rd"], u - 1)
                        nc.scalar.activation(prob[:, u % 2, lo * P:hi * P], pS[:, u % 2, lo * P:hi * P], ACT.Exp,
                                             bias=nmx[:, u % 2:u % 2 + 1], scale=MLA_SCALE,
                                             accum_out=den[:, u % 2:u % 2 + 1]).then_inc(at["exp"], 1)
                    if u >= 1:
                        v = u - 1
                        lo, hi = keys(units[v][0])
                        act.wait_ge(at["t"], v + 1)
                        if v >= 2:
                            act.wait_ge(at["o"], v - 1)
                        nc.scalar.copy(probT[:, v % 2, lo:hi, :], pT[:, v % 2, lo:hi, :]).then_inc(at["copied"], 1)
                    if u in copied_at:
                        g = copied_at.index(u)
                        act.wait_ge(m1_ready, g + 1)
                        if g >= 2:
                            act.wait_ge(m1_turned, g - 1)
                        nc.scalar.copy(rows[0:2, g % 2, :], pm[0:2, g % 2, :]).then_inc(m1_copied, 1)

            @block.vector
            def _(dve):
                dve.wait_ge(at["sg"], 1)
                for i in range(CONV_T):
                    nc.vector.tensor_tensor(gated[:, i, :, HALO:HALO + T],
                                            cT[:, 4 + i, :].rearrange("p (s n) -> p s n", s=2),
                                            sg[:, i], ALU.mult).then_inc(at["gated"], 1)
                dve.wait_ge(at["gated"], CONV_T)
                for u in range(len(units) + 2):
                    if u < len(units):
                        lo, hi = keys(units[u][0])
                        dve.wait_ge(at["s"], u + 1)
                        if u >= 2:
                            dve.wait_ge(at["exp"], u - 1)
                        nc.vector.reduce_max(nmx[:, u % 2:u % 2 + 1], pS[:, u % 2, lo * P:hi * P], AX).then_inc(at["mx"], 1)
                        dve.wait_ge(at["mx"], u + 1)
                        nc.vector.tensor_scalar(nmx[:, u % 2:u % 2 + 1], nmx[:, u % 2:u % 2 + 1],
                                                -MLA_SCALE, None, ALU.mult).then_inc(at["nmx"], 1)
                    if u < TAPS:
                        for i in range(CONV_T):
                            src, w = gated[:, i, :, u:u + T], convw[:, i, u:u + 1]
                            if u == 0:
                                nc.vector.tensor_scalar(conv[:, i], src, w, vecs[:, V_CB + i:V_CB + i + 1],
                                                        ALU.mult, ALU.add).then_inc(at["conv"], 1)
                            else:
                                dve.wait_ge(at["conv"], CONV_T * (u - 1) + i + 1)
                                nc.vector.scalar_tensor_tensor(out=conv[:, i], in0=src, scalar=w, in1=conv[:, i],
                                                               op0=ALU.mult, op1=ALU.add).then_inc(at["conv"], 1)
                    if u >= 2:
                        v = u - 2
                        m, h = units[v]
                        dve.wait_ge(at["exp"], v + 1)
                        nc.vector.reciprocal(rden[:, v % 2:v % 2 + 1], den[:, v % 2:v % 2 + 1]).then_inc(at["rd"], 1)
                        dve.wait_ge(at["o"], v + 1)
                        dve.wait_ge(at["rd"], v + 1)
                        nc.vector.tensor_scalar(O[:, m, h * VDIM:(h + 1) * VDIM], pO[:, v % 2, 0:VDIM],
                                                rden[:, v % 2:v % 2 + 1], None, ALU.mult).then_inc(at["norm"], 1)
                dve.wait_ge(m1_turned, GROUPS)
                mod_finish(Chain(dve, m1_done), 1, turned)
        if done("att"):
            return

        with ExitStack() as c2:
            sq = sb("conv_sq", [P, CONV_T, N2], ctx=c2)
            rs = sb("conv_rs", [P, N2], ctx=c2)
            pOT = ps("pOT", [P, 4, 512], c2)
            pL = ps("pL", [P, 2, 512], c2)
            ot, ln_pe, ln_dve, ln_act = sem("ot"), sem("ln_pe"), sem("ln_dve"), sem("ln_act")
            cv = conv[:].rearrange("p c s n -> p c (s n)")
            block = c2.enter_context(nc.Block())

            @block.tensor
            def _(pe):
                for i in range(CONV_T):
                    last = nc.tensor.matmul(pL[:, 0], ones[:], cv[:, i], start=(i == 0), stop=(i == CONV_T - 1))
                last.then_inc(ln_pe, 1)
                for k in range(4):
                    for m in range(4):
                        last = nc.tensor.transpose(pOT[:, k, m * P:(m + 1) * P], O[:, m, k * P:(k + 1) * P], ident)
                    last.then_inc(ot, 1)
                for i in range(CONV_T):
                    pe.wait_ge(ln_act, i + 1)
                    last = nc.tensor.matmul(pL[:, 1], ones[:], sq[:, i], start=(i == 0), stop=(i == CONV_T - 1))
                last.then_inc(ln_pe, 1)

            @block.vector
            def _(dve):
                chain = Chain(dve, ln_dve)
                dve.wait_ge(ln_pe, 1)
                for i in range(CONV_T):
                    chain(nc.vector.scalar_tensor_tensor(out=cv[:, i], in0=pL[:, 0], scalar=-1.0 / 512,
                                                         in1=cv[:, i], op0=ALU.mult, op1=ALU.add))
                dve.wait_ge(ln_pe, 2)
                chain(nc.vector.tensor_scalar(rs[:], pL[:, 1], 1.0 / 512, EPS, ALU.mult, ALU.add))
                dve.wait_ge(ln_act, CONV_T + 1)
                chain(nc.vector.reciprocal(rs[:], rs[:]))
                for i in range(CONV_T):
                    chain(nc.vector.tensor_tensor(cv[:, i], cv[:, i], rs[:], ALU.mult))
                for k in range(4):
                    dve.wait_ge(ot, k + 1)
                    nc.vector.tensor_copy(mix[:, k, :], pOT[:, k, :])

            @block.scalar
            def _(act):
                for i in range(CONV_T):
                    act.wait_ge(ln_dve, i + 1)
                    nc.scalar.activation(sq[:, i], cv[:, i], ACT.Square).then_inc(ln_act, 1)
                act.wait_ge(ln_dve, CONV_T + 1)
                nc.scalar.activation(rs[:], rs[:], ACT.Sqrt).then_inc(ln_act, 1)
                for i in range(CONV_T):
                    act.wait_ge(ln_dve, CONV_T + 3 + i)
                    nc.scalar.activation(mix[:, 4 + i, :], cv[:, i], ACT.Silu, scale=vecs[:, V_LNG + i:V_LNG + i + 1],
                                         bias=vecs[:, V_LNB + i:V_LNB + i + 1])


def peer_phase(nc, t, sem, sb, ps, xT, modT, cst, ident, l, cols, norm_phase, lin_loads, g0, w_loaded,
               wring, acc_ready, acc_free, which, u_loaded, v_loaded, steps_before):
    blocks = cols // P
    steps = blocks * HEADS
    TRIPS = HEADS // 2
    with ExitStack() as c:
        Y = sb(f"Y_{l}", [P, blocks, D], ctx=c)
        with ExitStack() as c2:
            hT = sb(f"h2T_{l}", [P, KT, cols], ctx=c2)
            norm_phase(f"np{l}", xT, hT, cols, l, 1)
            H2 = sb(f"H2_{l}", [P, blocks, D], ctx=c2)
            qT = sb(f"qT_{l}", [P, 2, cols], ctx=c2)
            keys = sb(f"keys_{l}", [P, 2 * HEADS, P], ctx=c2)
            S = [sb(f"S{l}_{e}", [P, blocks, 2, P], ctx=c2) for e in range(2)]
            U = [sb(f"U{l}_{j}", [P, D], ctx=c2) for j in range(SLOTS)]
            Vr = [sb(f"V{l}_{j}", [P, D], ctx=c2) for j in range(SLOTS)]
            diag = sb(f"diag{l}", [P, TOPK, P], ctx=c2)
            junk = sb(f"junk{l}", [P, 2, D], ctx=c2)
            rest = sb(f"rest{l}", [P, 2, P], ctx=c2)
            sv = sb(f"sv{l}", [P, 2, TOPK], ctx=c2)
            si = sb(f"si{l}", [P, 2, TOPK], U32, ctx=c2)
            sif = sb(f"sif{l}", [P, 2, TOPK], ctx=c2)
            cand = sb(f"cand{l}", [P, TOPK, TOPK], ctx=c2)
            cand2 = sb(f"cand2{l}", [P, TOPK, TOPK], ctx=c2)
            top = [sb(f"top{l}_{e}", [P, TOPK], ctx=c2) for e in range(2)]
            pos = sb(f"pos{l}", [P, TOPK], U32, ctx=c2)
            pij = sb(f"pij{l}", [P, 2, TOPK], U32, ctx=c2)
            pf = sb(f"pf{l}", [P, 2, TOPK], ctx=c2)
            hot = sb(f"hot{l}", [P, 2, TOPK, TOPK], ctx=c2)
            e2 = sb(f"e2{l}", [P, 2, TOPK], ctx=c2)
            idx = [sb(f"idx{l}_{e}", [P, TOPK], U32, ctx=c2) for e in range(2)]
            mine = [sb(f"mine{l}_{e}", [P, TOPK], U32, ctx=c2) for e in range(2)]
            nmax = [sb(f"nmax{l}_{e}", [P, 1], ctx=c2) for e in range(2)]
            ex = [sb(f"ex{l}_{e}", [P, TOPK], ctx=c2) for e in range(2)]
            den = [sb(f"pden{l}_{e}", [P, 1], ctx=c2) for e in range(2)]
            rden = sb(f"prden{l}", [P, 1], ctx=c2)
            dots = sb(f"dots{l}", [P, TOPK], ctx=c2)
            act_t = sb(f"actt{l}", [P, TOPK], ctx=c2)
            coef = sb(f"coef{l}", [P, TOPK], ctx=c2)
            pY = ps(f"pY{l}", [P, D], c2)
            pq = ps(f"pq{l}", [P, 2, 512], c2)
            psc = ps(f"psc{l}", [P, blocks, 2, P], c2)
            ptr = ps(f"ptr{l}", [P, 2, 512], c2)
            iota = cst[:, C_IOTA:C_IOTA + TOPK]
            s_keys, s_tr, s_tre, s_sc, s_sce, s_zero = (sem(f"p{l}_{x}") for x in ("keys", "tr", "tre", "sc", "sce", "zero"))
            s_idx, s_dot, s_gelu, s_coef, s_diag, s_y, s_u, s_v, s_exp, s_ch, s_taken = (
                sem(f"p{l}_{x}") for x in ("idx", "dot", "gelu", "coef", "diag", "y", "ufree", "vfree", "exp", "chain", "taken"))
            TOPK_LINKS, STEP_LINKS = 24, 26
            block = c2.enter_context(nc.Block())

            if blocks == 4:
                beside = {0: ("q0",), 1: ("q1",), 2: ("scores",), 3: ()}
            else:
                beside = {0: ("q0", "q1", "scores"), 1: ()}

            def trips(eng, body):
                with eng.Fori(0, TRIPS - 1) as p:
                    body(p, False)
                body(TRIPS - 1, True)

            def trip_steps(p, last):
                for hh in range(2):
                    for b in range(blocks):
                        yield p * (2 * blocks) + (hh * blocks + b), hh, b, last and hh == 1 and b == blocks - 1

            @block.sync
            def _(sp):
                sp.dma_start(keys[:], t[f"keys{l}"]).then_inc(s_keys, 16)
                lin_loads(sp, which)

            def pe_prepare(pe, part, p, n):
                if part == "scores":
                    pe.wait_ge(acc_free, p * RING + (RING + g0 + 2 * n + 2))
                    if not (isinstance(p, int) and p * 2 + n == 0):
                        pe.wait_ge(s_sce, p * 2 + n)
                    for b in range(blocks):
                        for i in range(2):
                            last = nc.tensor.matmul(psc[:, b, i, :], qT[:, i, b * P:(b + 1) * P],
                                                    keys[:, bass.ds(p * 4 + (2 * n + i), 1), :].rearrange("p a n -> p (a n)"),
                                                    start=True, stop=True)
                    last.then_inc(s_sc, 1)
                else:
                    i = ("q0", "q1").index(part)
                    j = 2 * n + i
                    pe.wait_ge(w_loaded[j % RING], p * 16 + (g0 // RING + j // RING + 1) * 16)
                    pe.wait_ge(acc_free, p * RING + (RING + g0 + j - 1))
                    for k in range(KT):
                        last = nc.tensor.matmul(pq[:, i, 0:cols], wring[:, j % RING, k * P:(k + 1) * P], hT[:, k, :],
                                                start=(k == 0), stop=(k == KT - 1))
                    last.then_inc(acc_ready, 1)

            def act_prepare(act, part, p, n):
                if part == "scores":
                    act.wait_ge(s_sc, p * 2 + (n + 1))
                    nc.scalar.copy(S[n % 2][:], psc[:]).then_inc(s_sce, 1)
                else:
                    i = ("q0", "q1").index(part)
                    act.wait_ge(acc_ready, p * RING + (g0 + 2 * n + i + 1))
                    nc.scalar.copy(qT[:, i, :], pq[:, i, 0:cols]).then_inc(acc_free, 1)

            def topk(chain, scores, e):
                v = nc.vector
                for h in range(2):
                    chain.apart(v.max(out=sv[:, h, 0:8], in_=scores[:, h]))
                    chain.apart(v.max_index(out=si[:, h, 0:8], in_max=sv[:, h, 0:8], in_values=scores[:, h]))
                    chain.apart(v.match_replace(out=rest[:, h], in_to_replace=sv[:, h, 0:8], in_values=scores[:, h], imm_value=NEG))
                    chain.apart(v.max(out=sv[:, h, 8:16], in_=rest[:, h]))
                    chain.apart(v.max_index(out=si[:, h, 8:16], in_max=sv[:, h, 8:16], in_values=rest[:, h]))
                chain.apart(v.tensor_tensor(cand[:], sv[:, 0, :].unsqueeze(2).broadcast_to([P, TOPK, TOPK]),
                                      sv[:, 1, :].unsqueeze(1).broadcast_to([P, TOPK, TOPK]), ALU.add))
                cf, cf2 = (x[:].rearrange("p a b -> p (a b)") for x in (cand, cand2))
                chain.apart(v.max(out=top[e][:, 0:8], in_=cf))
                chain.apart(v.max_index(out=pos[:, 0:8], in_max=top[e][:, 0:8], in_values=cf))
                chain.apart(v.match_replace(out=cf2, in_to_replace=top[e][:, 0:8], in_values=cf, imm_value=NEG))
                chain.apart(v.max(out=top[e][:, 8:16], in_=cf2))
                chain.apart(v.max_index(out=pos[:, 8:16], in_max=top[e][:, 8:16], in_values=cf2))
                chain(v.tensor_scalar(nmax[e][:], top[e][:, 0:1], -1.0, None, ALU.mult))
                chain(v.tensor_scalar(pij[:, 0], pos[:], 4, None, ALU.logical_shift_right))
                chain(v.tensor_scalar(pij[:, 1], pos[:], TOPK - 1, None, ALU.bitwise_and))
                chain(v.tensor_copy(pf[:], pij[:]))
                chain(v.tensor_copy(sif[:], si[:]))
                q4 = [P, 2, TOPK, TOPK]
                chain(v.tensor_tensor(hot[:], pf[:].unsqueeze(3).broadcast_to(q4),
                                      iota.unsqueeze(1).unsqueeze(1).broadcast_to(q4), ALU.is_equal))
                chain(v.tensor_tensor(hot[:], hot[:], sif[:].unsqueeze(2).broadcast_to(q4), ALU.mult))
                chain(v.tensor_reduce(e2[:], hot[:], AX, ALU.add))
                v.scalar_tensor_tensor(out=idx[e][:], in0=e2[:, 0], scalar=float(P), in1=e2[:, 1],
                                       op0=ALU.mult, op1=ALU.add).then_inc(s_idx, 1)

            def dots_of(dve, b, s):
                for k in range(TOPK):
                    j = k % SLOTS
                    dve.wait_ge(u_loaded[j], s * 32 + (steps_before * 32 + (k // SLOTS + 1) * 16))
                    dve.wait_ge(s_u, s * TOPK + (SLOTS + k - 1))
                    nc.vector.scalar_tensor_tensor(
                        out=junk[:, k % 2], in0=U[j][:], scalar=1.0, in1=H2[:, b, :],
                        op0=ALU.mult, op1=ALU.mult, accum_out=dots[:, k:k + 1]).then_inc(s_u, 1)

            @block.vector
            def _(dve):
                chain = Chain(dve, s_ch)
                dve.sem_inc(s_u, SLOTS)
                chain(nc.vector.memset(pY[:, 0:512], 0.0))
                chain(nc.vector.memset(pY[:, 512:D], 0.0))
                dve.sem_inc(s_y, 1)
                dve.wait_ge(s_sce, 1)
                topk(chain, S[0][:, 0], 0)
                assert chain.n == 2 + TOPK_LINKS, chain.n
                dve.wait_ge(s_zero, 1)
                dve.wait_ge(s_tre, 2 * blocks)

                def trip(p, last):
                    for s, hh, b, final in trip_steps(p, last):
                        e = b % 2
                        chain = Chain(dve, s_ch, s * STEP_LINKS + (2 + TOPK_LINKS))
                        if not final:
                            if b == blocks - 1:
                                wait_apart(dve, s_sce, p * 2 + (hh + 2))
                            wait_apart(dve, s_taken, s + 1)
                            topk(chain, S[(hh + (b + 1) // blocks) % 2][:, (b + 1) % blocks], 1 - e)
                        dots_of(dve, b, s)
                        dve.wait_ge(s_y, s + 1)
                        yb = Y[:, (b - 1) % blocks, :]
                        chain(nc.vector.tensor_tensor(yb, yb, pY[:], ALU.add))
                        dve.wait_ge(s_exp, s + 1)
                        chain(nc.vector.reciprocal(rden[:], den[e][:]))
                        assert final or chain.n == STEP_LINKS, chain.n
                        dve.wait_ge(s_gelu, s + 1)
                        nc.vector.scalar_tensor_tensor(out=coef[:], in0=act_t[:], scalar=rden[:, 0:1], in1=ex[e][:],
                                                       op0=ALU.mult, op1=ALU.mult).then_inc(s_coef, 1)

                trips(dve, trip)
                dve.wait_ge(s_y, steps + 1)
                nc.vector.tensor_tensor(Y[:, blocks - 1, :], Y[:, blocks - 1, :], pY[:], ALU.add)

            @block.gpsimd
            def _(pool):
                nc.gpsimd.memset(Y[:], 0.0).then_inc(s_zero, 1)
                pool.sem_inc(s_taken, 1)
                with pool.Fori(0, steps // 2) as p:
                    for e in range(2):
                        s = p * 2 + e
                        wait_apart(pool, s_idx, s + 1)
                        nc.gpsimd.tensor_copy(mine[e][:], idx[e][:]).then_inc(s_taken, 1)
                        wait_apart(pool, s_taken, s + 2)
                        for k in range(TOPK):
                            wait_apart(pool, s_u, s * TOPK + (k + 1))
                            nc.gpsimd.indirect_dma_start(
                                out=U[k % SLOTS][:], out_offset=None, in_=t[f"u{l}"],
                                in_offset=bass.IndirectOffsetOnAxis(ap=mine[e][:, k:k + 1], axis=0)
                            ).then_inc(u_loaded[k % SLOTS], 16)
                        for k in range(TOPK):
                            wait_apart(pool, s_v, s * TOPK + (k + 1))
                            nc.gpsimd.indirect_dma_start(
                                out=Vr[k % SLOTS][:], out_offset=None, in_=t[f"v{l}"],
                                in_offset=bass.IndirectOffsetOnAxis(ap=mine[e][:, k:k + 1], axis=0)
                            ).then_inc(v_loaded[k % SLOTS], 16)

            @block.scalar
            def _(act):
                def exponentials(s, e):
                    act.wait_ge(s_idx, s + 1)
                    nc.scalar.activation(ex[e][:], top[e][:], ACT.Exp, bias=nmax[e][:], accum_out=den[e][:]).then_inc(s_exp, 1)

                for part in ("q0", "q1", "scores"):
                    act_prepare(act, part, 0, 0)
                for n in range(2 * blocks):
                    act.wait_ge(s_tr, n + 1)
                    nc.scalar.copy(H2[:, n // 2, (n % 2) * 512:(n % 2 + 1) * 512], ptr[:, n % 2, :]).then_inc(s_tre, 1)
                exponentials(0, 0)

                def trip(p, last):
                    for s, hh, b, final in trip_steps(p, last):
                        if not final:
                            exponentials(s + 1, 1 - b % 2)
                        if not (last and hh == 1):
                            for part in beside[b]:
                                act_prepare(act, part, p, hh + 1)
                        act.wait_ge(s_u, s * TOPK + (TOPK + SLOTS))
                        nc.scalar.activation(act_t[:], dots[:], ACT.Gelu).then_inc(s_gelu, 1)
                        act.wait_ge(s_coef, s + 1)
                        for k in range(TOPK):
                            nc.scalar.activation(diag[:, k, :], ident, ACT.Copy, scale=coef[:, k:k + 1]).then_inc(s_diag, 1)

                trips(act, trip)

            @block.tensor
            def _(pe):
                pe.sem_inc(s_v, SLOTS)
                pe_prepare(pe, "q0", 0, 0)
                pe_prepare(pe, "q1", 0, 0)
                pe.wait_ge(s_keys, 16)
                pe_prepare(pe, "scores", 0, 0)
                for n in range(2 * blocks):
                    if n >= 2:
                        pe.wait_ge(s_tre, n - 1)
                    for k in range(4):
                        last = nc.tensor.transpose(ptr[:, n % 2, k * P:(k + 1) * P],
                                                   hT[:, 4 * (n % 2) + k, (n // 2) * P:(n // 2 + 1) * P], ident)
                    last.then_inc(s_tr, 1)

                def trip(p, last_trip):
                    for s, hh, b, final in trip_steps(p, last_trip):
                        if not (last_trip and hh == 1):
                            for part in beside[b]:
                                pe_prepare(pe, part, p, hh + 1)
                        for k in range(TOPK):
                            j = k % SLOTS
                            pe.wait_ge(s_diag, s * TOPK + (k + 1))
                            pe.wait_ge(v_loaded[j], s * 32 + (steps_before * 32 + (k // SLOTS + 1) * 16))
                            for half in range(2):
                                last = nc.tensor.matmul(pY[:, half * 512:(half + 1) * 512], diag[:, k, :],
                                                        Vr[j][:, half * 512:(half + 1) * 512],
                                                        start=(k == 0), stop=(k == TOPK - 1))
                            last.then_inc(s_v, 1)
                        pe.wait_ge(s_v, s * TOPK + (TOPK + SLOTS))
                        pe.sem_inc(s_y, 1)

                trips(pe, trip)

        with ExitStack() as c2:
            pt = ps(f"pt{l}", [P, 4, 512], c2)
            s_t, s_r = sem(f"p{l}_t"), sem(f"p{l}_r")
            block = c2.enter_context(nc.Block())

            @block.tensor
            def _(pe):
                for k in range(KT):
                    if k >= 4:
                        pe.wait_ge(s_r, k - 3)
                    for b in range(blocks):
                        last = nc.tensor.transpose(pt[:, k % 4, b * P:(b + 1) * P], Y[:, b, k * P:(k + 1) * P], ident)
                    last.then_inc(s_t, 1)

            @block.vector
            def _(dve):
                for k in range(KT):
                    dve.wait_ge(s_t, k + 1)
                    for c2_ in range(cols // T):
                        span = slice(c2_ * T, (c2_ + 1) * T)
                        last = nc.vector.scalar_tensor_tensor(out=xT[:, k, span], in0=pt[:, k % 4, span],
                                                              scalar=modT[:, l, 5, k, c2_:c2_ + 1], in1=xT[:, k, span],
                                                              op0=ALU.mult, op1=ALU.add)
                    last.then_inc(s_r, 1)


def hgrn_phase(nc, t, sem, sb, ps, xT, modT, cst, vecs, ones, ident, norm_phase, lin_loads, lin_matmuls,
               lin_evac, lin_done, residual_evac, V_HGN, done):
    CTX_CHUNKS = N2 // CHUNK // 2
    ORDER = ([4, 5, 6, 7, 0, 1, 2, 3], [7, 6, 5, 4, 3, 2, 1, 0])
    with ExitStack() as c:
        QG = sb("QG", [P, 2 * HEADS, T], ctx=c)
        OT = sb("OT", [P, HEADS, T], ctx=c)
        with ExitStack() as c1:
            F = sb("F", [P, 2 * HEADS, N2], ctx=c1)
            KK = sb("KK", [P, 2 * HEADS, N2], ctx=c1)
            VI = sb("VI", [P, 4, D], ctx=c1)

            with ExitStack() as c2:
                hT = sb("h1T", [P, KT, N2], ctx=c2)
                norm_phase("n1", xT, hT, N2, 1, 0)
                wi = sb("wi", [P, KT, D], ctx=c2)
                lb = sb("lb", [P, 2, 2 * KT], ctx=c2)
                mx = sb("lbmx", [P, 2 * KT], ctx=c2)
                low = sb("low", [P, 2 * KT], ctx=c2)
                room = sb("room", [P, 2 * KT], ctx=c2)
                pl = ps("plh", [P, RING, 512], c2)
                pi = ps("pi", [P, 2, 512], c2)
                s_w, s_lb, s_e, s_i, s_ie = (sem(f"hg_{x}") for x in ("w", "lb", "e", "i", "ie"))
                block = c2.enter_context(nc.Block())

                @block.sync
                def _(sp):
                    sp.dma_start(lb[:].rearrange("p l k -> p (l k)"),
                                 t["hg_lb"].rearrange("p l d k -> p (l d k)")).then_inc(s_w, 16)
                    sp.dma_start(wi[:], t["hg_i"]).then_inc(s_w, 16)
                    lin_loads(sp, 3)
                    lin_loads(sp, 4)

                @block.tensor
                def _(pe):
                    lin_matmuls(pe, 3, pl, lambda k: hT[:, k, :], N2)
                    lin_matmuls(pe, 4, pl, lambda k: hT[:, k, 0:T], T)
                    pe.wait_ge(s_w, 32)
                    for n in range(8):
                        if n >= 2:
                            pe.wait_ge(s_ie, n - 1)
                        for k in range(KT):
                            last = nc.tensor.matmul(pi[:, n % 2, :], hT[:, k, (n // 2) * P:(n // 2 + 1) * P],
                                                    wi[:, k, (n % 2) * 512:(n % 2 + 1) * 512],
                                                    start=(k == 0), stop=(k == KT - 1))
                        last.then_inc(s_i, 1)

                @block.scalar
                def _(act):
                    act.wait_ge(s_lb, 2)
                    nc.scalar.activation(lb[:], lb[:], ACT.Exp).then_inc(s_e, 1)
                    lin_evac(act, 3, lambda i, j: nc.scalar.activation(F[:, bass.ds(i, 1), :], pl[:, j:j + 1, :], ACT.Sigmoid))
                    lin_evac(act, 4, lambda i, j: nc.scalar.copy(QG[:, bass.ds(i, 1), :], pl[:, j:j + 1, 0:T]))

                @block.vector
                def _(dve):
                    chain = Chain(dve, s_lb)
                    v = nc.vector
                    dve.wait_ge(s_w, 32)
                    chain(v.tensor_tensor(mx[:], lb[:, 0], lb[:, 1], ALU.max))
                    chain(v.tensor_tensor(lb[:], lb[:], mx[:].unsqueeze(1).broadcast_to([P, 2, 2 * KT]), ALU.subtract))
                    dve.wait_ge(s_e, 1)
                    chain(v.tensor_tensor(mx[:], lb[:, 0], lb[:, 1], ALU.add))
                    chain(v.reciprocal(mx[:], mx[:]))
                    chain(v.tensor_tensor(lb[:], lb[:], mx[:].unsqueeze(1).broadcast_to([P, 2, 2 * KT]), ALU.mult))
                    chain(v.tensor_tensor(low[:], lb[:, 0], lb[:, 1], ALU.add))
                    chain(v.tensor_tensor(low[:], low[:], lb[:, 0], ALU.subtract))
                    chain(v.tensor_scalar(room[:], low[:], -1.0, 1.0, ALU.mult, ALU.add))
                    for i in range(2 * HEADS):
                        lin_done(dve, 3, i + 1)
                        chain(v.tensor_scalar(F[:, i], F[:, i], room[:, i:i + 1], low[:, i:i + 1], ALU.mult, ALU.add))
                        v.tensor_scalar(KK[:, i], F[:, i], -1.0, 1.0, ALU.mult, ALU.add)
                    for n in range(8):
                        dve.wait_ge(s_i, n + 1)
                        v.tensor_copy(VI[:, n // 2, (n % 2) * 512:(n % 2 + 1) * 512], pi[:, n % 2, :]).then_inc(s_ie, 1)
            if done("hgrn_p"):
                return

            with ExitStack() as c2:
                two = range(2)
                qin = sb("qin", [P, 2 * HEADS, T], ctx=c2)
                kin = sb("kin", [P, 2 * HEADS, T], ctx=c2)
                dec = sb("dec", [P, 2 * HEADS, 8], ctx=c2)
                kout = F
                halves = [slice(d * HEADS, (d + 1) * HEADS) for d in two]

                def flat(x, d):
                    return x[:, halves[d], :].rearrange("p h n -> p (h n)")

                def chunks(x, d):
                    return x[:, halves[d], :].rearrange("p h (c n) -> p (h c) n", n=CHUNK)

                with ExitStack() as c3:
                    starts = sb("starts", [P, N2], mybir.dt.bfloat16, ctx=c3)
                    bs = sb("bs", [P, 2 * HEADS, N2], ctx=c3)
                    def last_col(d):
                        at = (CHUNK - 1) * (1 - d)
                        return bs[:, halves[d], :].rearrange("p h (c n) -> p (h c) n", n=CHUNK)[:, :, at:at + 1]

                    g_ln, g_dve, g_ex = sem("g_ln"), sem("g_dve"), sem("g_ex")
                    block = c3.enter_context(nc.Block())

                    @block.scalar
                    def _(act):
                        for d in two:
                            nc.scalar.activation(flat(F, d), flat(F, d), ACT.Ln).then_inc(g_ln, 1)
                        for d in two:
                            act.wait_ge(g_dve, 4 + 2 * d)
                            nc.scalar.activation(dec[:, halves[d], :].rearrange("p h c -> p (h c)").unsqueeze(2),
                                                 last_col(d), ACT.Exp)
                            nc.scalar.activation(qin[:, halves[d], :], bs[:, halves[d], 0:T], ACT.Exp)
                            nc.scalar.activation(kin[:, halves[d], :], bs[:, halves[d], 0:T], ACT.Exp, scale=-1.0)
                            nc.scalar.activation(flat(F, d), flat(F, d), ACT.Exp).then_inc(g_ex, 1)

                    @block.vector
                    def _(dve):
                        v = nc.vector
                        chain = Chain(dve, g_dve)
                        chain(v.memset(starts[:], 1.0))
                        chain(v.memset(starts[:].rearrange("p (c n) -> p c n", n=CHUNK)[:, :, 0:1], 0.0))
                        for d in two:
                            dve.wait_ge(g_ln, d + 1)
                            way = slice(None) if d == 0 else slice(None, None, -1)
                            for i in range(d * HEADS, (d + 1) * HEADS):
                                last = v.tensor_tensor_scan(bs[:, i, way], starts[:], F[:, i, way], 0.0, ALU.mult, ALU.add)
                            chain(last)
                            chain(v.tensor_tensor(chunks(F, d), last_col(d).broadcast_to([P, HEADS * 8, CHUNK]),
                                                  chunks(bs, d), ALU.subtract))
                        for d in two:
                            dve.wait_ge(g_ex, d + 1)
                            v.tensor_tensor(flat(F, d), flat(F, d), flat(KK, d), ALU.mult)
                            v.tensor_tensor(qin[:, halves[d], :], qin[:, halves[d], :], QG[:, 0:HEADS, :], ALU.mult)

                    @block.gpsimd
                    def _(pool):
                        for d in two:
                            pool.wait_ge(g_ex, d + 1)
                            nc.gpsimd.tensor_tensor(kin[:, halves[d], :], kin[:, halves[d], :],
                                                    KK[:, halves[d], 0:T], ALU.mult)
                if done("decays"):
                    return

                koT = [[sb(f"koT{e}{d}", [P, 4, P], ctx=c2) for d in two] for e in two]
                AM = [[sb(f"AM{e}{d}", [P, 2, P], ctx=c2) for d in two] for e in two]
                ST = [[sb(f"ST{e}{d}", [P, 7, P], ctx=c2) for d in two] for e in two]
                pK = [ps(f"pK{d}", [P, 4, P], c2) for d in two]
                pA = ps("pA", [P, 2, 2, P], c2)
                pD = [[ps(f"pD{d}{x}", [P, 4, P], c2) for x in two] for d in two]
                pO = ps("pOh", [P, 512], c2)
                s = {x: sem(f"gla_{x}") for x in ("zero", "pt", "kot", "pa", "am", "ds", "st", "c", "o", "oc")}
                block = c2.enter_context(nc.Block())

                @block.gpsimd
                def _(pool):
                    for e in two:
                        for d in two:
                            nc.gpsimd.memset(AM[e][d][:], 0.0).then_inc(s["zero"], 1)

                @block.scalar
                def _(act):
                    for h in range(HEADS + 1):
                        if h < HEADS:
                            for d in two:
                                act.wait_ge(s["pt"], 2 * h + d + 1)
                                if h >= 2:
                                    act.wait_ge(s["ds"], 2 * (h - 2) + d + 1)
                                nc.scalar.copy(koT[h % 2][d][:], pK[d][:]).then_inc(s["kot"], 1)
                        if h >= 1:
                            act.wait_ge(s["o"], h)
                            nc.scalar.copy(OT[:, h - 1], pO[:, 0:T]).then_inc(s["oc"], 1)

                @block.vector
                def _(dve):
                    v = nc.vector
                    chain = Chain(dve, s["c"])
                    masks = cst[:, C_MASK:C_MASK + 2 * P].rearrange("p (d n) -> p d n", d=2).bitcast(U32)
                    dve.wait_ge(s["zero"], 4)
                    for h in range(HEADS):
                        e = h % 2
                        dve.wait_ge(s["pa"], h + 1)
                        if h >= 2:
                            dve.wait_ge(s["o"], h - 1)
                        for d in two:
                            v.copy_predicated(AM[e][d][:], masks[:, d, :].unsqueeze(1).broadcast_to([P, 2, P]),
                                              pA[:, d]).then_inc(s["am"], 1)
                        for i in range(7):
                            for d in two:
                                ch = ORDER[d][i]
                                own = pD[d][ch % 2][:, ch // 2, :]
                                if i == 0:
                                    dve.wait_ge(s["ds"], 2 * h + d + 1)
                                    ins = v.tensor_copy(ST[e][d][:, 0], own)
                                else:
                                    dve.wait_ge(s["c"], 14 * h + 2 * (i - 1) + d + 1)
                                    ins = v.scalar_tensor_tensor(out=ST[e][d][:, i], in0=ST[e][d][:, i - 1],
                                                                 scalar=dec[:, d * HEADS + h, ch:ch + 1], in1=own,
                                                                 op0=ALU.mult, op1=ALU.add)
                                ins.then_inc(s["c"], 1)

                @block.tensor
                def _(pe):
                    def turn(h):
                        for d in two:
                            if h >= 1:
                                pe.wait_ge(s["kot"], 2 * (h - 1) + d + 1)
                            for m in range(4):
                                last = nc.tensor.transpose(pK[d][:, m, :], kout[:, d * HEADS + h, m * P:(m + 1) * P], ident)
                            last.then_inc(s["pt"], 1)

                    def output(h):
                        e = h % 2
                        if h >= 1:
                            pe.wait_ge(s["oc"], h)
                        pe.wait_ge(s["am"], 2 * h + 2)
                        for d in two:
                            for m in two:
                                nc.tensor.matmul(pO[:, m * P:(m + 1) * P], VI[:, m, h * P:(h + 1) * P], AM[e][d][:, m, :],
                                                 start=(d == 0 and m == 0), stop=False, skip_group_check=True)
                        pe.wait_ge(s["c"], 14 * (h + 1))
                        for d in two:
                            for i in range(4):
                                ch = ORDER[d][CTX_CHUNKS + i]
                                cols = slice(ch * CHUNK, (ch + 1) * CHUNK)
                                last = nc.tensor.matmul(pO[:, cols], ST[e][d][:, 3 + i, :], qin[:, d * HEADS + h, cols],
                                                        start=False, stop=(d == 1 and i == 3), skip_group_check=True)
                        last.then_inc(s["o"], 1)

                    turn(0)
                    for h in range(HEADS):
                        if h + 1 < HEADS:
                            turn(h + 1)
                        if h >= 1:
                            pe.wait_ge(s["am"], 2 * h)
                        for d in two:
                            for m in two:
                                last = nc.tensor.matmul(pA[:, d, m, :], kin[:, d * HEADS + h, m * P:(m + 1) * P],
                                                        qin[:, d * HEADS + h, m * P:(m + 1) * P], start=True, stop=True)
                        last.then_inc(s["pa"], 1)
                        if h >= 1:
                            pe.wait_ge(s["c"], 14 * h)
                        for d in two:
                            pe.wait_ge(s["kot"], 2 * h + d + 1)
                            for i in range(7):
                                ch = ORDER[d][i]
                                rows = slice(CHUNK * (ch % 2), CHUNK * (ch % 2 + 1))
                                last = nc.tensor.matmul(pD[d][ch % 2][:, ch // 2, :], koT[h % 2][d][rows, ch // 2, :],
                                                        VI[rows, ch // 2, h * P:(h + 1) * P], start=True, stop=True)
                            last.then_inc(s["ds"], 1)
                        if h >= 1:
                            output(h - 1)
                    output(HEADS - 1)
        if done("gla"):
            return

        with ExitStack() as c1:
            sq = sb("osq", [P, HEADS, T], ctx=c1)
            rs = sb("ors", [P, HEADS, T], ctx=c1)
            pR = ps("pR", [P, HEADS, T], c1)
            pl = ps("plo", [P, RING, 512], c1)
            r_act, r_pe, r_dve = sem("r_act"), sem("r_pe"), sem("r_dve")
            block = c1.enter_context(nc.Block())

            @block.sync
            def _(sp):
                lin_loads(sp, 5)

            @block.scalar
            def _(act):
                for h in range(HEADS):
                    nc.scalar.activation(sq[:, h], OT[:, h], ACT.Square).then_inc(r_act, 1)
                nc.scalar.activation(QG[:, HEADS:], QG[:, HEADS:], ACT.Silu).then_inc(r_act, 1)
                act.wait_ge(r_dve, 1)
                nc.scalar.activation(rs[:], rs[:], ACT.Sqrt).then_inc(r_act, 1)

            @block.vector
            def _(dve):
                chain = Chain(dve, r_dve)
                dve.wait_ge(r_pe, 1)
                chain(nc.vector.tensor_scalar(rs[:], pR[:], 1.0 / P, EPS, ALU.mult, ALU.add))
                dve.wait_ge(r_act, HEADS + 2)
                chain(nc.vector.reciprocal(rs[:], rs[:]))
                chain(nc.vector.tensor_tensor(rs[:], rs[:], OT[:], ALU.mult))
                for h in range(HEADS):
                    chain(nc.vector.scalar_tensor_tensor(out=OT[:, h], in0=rs[:, h], scalar=vecs[:, V_HGN + h:V_HGN + h + 1],
                                                         in1=QG[:, HEADS + h], op0=ALU.mult, op1=ALU.mult))
                lin_evac(dve, 5, residual_evac(5, pl, T, 1, 2))

            @block.tensor
            def _(pe):
                for h in range(HEADS):
                    pe.wait_ge(r_act, h + 1)
                    last = nc.tensor.matmul(pR[:, h], ones[:], sq[:, h], start=True, stop=True)
                last.then_inc(r_pe, 1)
                pe.wait_ge(r_dve, 3 + HEADS)
                lin_matmuls(pe, 5, pl, lambda k: OT[:, k, :], T)

def host_arrays(a):
    import numpy as np
    f = {k: np.asarray(v) for k, v in a.items()}

    def tiles(w):
        K, N = w.shape
        return np.ascontiguousarray(w.reshape(K // P, P, N // P, P).transpose(2, 1, 0, 3).reshape(N // P, P, -1))

    def cols(v):
        return v.reshape(-1, P).T

    def swapped(w):
        return w.reshape(w.shape[0], -1, 2)[:, :, ::-1].reshape(w.shape)

    o = {}
    o["xT"] = np.concatenate([f["x"][0], f["ctx"][0]], axis=0).T.reshape(KT, P, N2).transpose(1, 0, 2)
    o["cT"] = np.stack([f["c"][0], f["c_ctx"]], axis=1).reshape(KT, P, 2).transpose(1, 0, 2)
    o["ada_w"] = f["ada_w"].reshape(2, KT, P, 12, 512).transpose(0, 3, 2, 1, 4).reshape(24, P, KT * 512)
    o["ada_b"] = cols(f["ada_b"].reshape(-1))
    w = f["ab_w_in"][0]
    kr = w[:, 384:416]
    o["w_in"] = tiles(np.concatenate([w[:, :384], w[:, 320:384], kr, swapped(kr), w[:, 416:]], axis=1))
    wq = f["mla_w_uq"][0].reshape(256, HEADS, QK)
    rope = wq[:, :, NOPE:]
    wq = np.concatenate([wq, rope.reshape(256, HEADS, ROPE // 2, 2)[..., ::-1].reshape(256, HEADS, ROPE)], axis=2)
    o["w_uq"] = wq.reshape(2, P, HEADS * P).transpose(1, 0, 2)
    wkv = f["mla_w_ukv"][0].reshape(P, HEADS, NOPE + VDIM)
    o["w_uk"] = wkv[:, :, :NOPE].reshape(P, -1)
    o["w_uv"] = wkv[:, :, NOPE:].reshape(P, -1)
    o["conv_w"] = f["conv_w"][0].reshape(TAPS, CONV_T, P).transpose(2, 1, 0)
    o["w_out"] = tiles(f["ab_w_out"][0])
    hg = f["hg_w_in"][0]
    o["hg_zz"] = tiles(hg[:, 1024:3072])
    o["hg_qg"] = tiles(np.concatenate([hg[:, 0:1024], hg[:, 4096:5120]], axis=1))
    o["hg_i"] = hg[:, 3072:4096].reshape(KT, P, D).transpose(1, 0, 2)
    o["hg_out"] = tiles(f["hg_w_out"][0])
    o["hg_lb"] = f["hg_lower_bound"].reshape(2, 2, KT, P).transpose(3, 0, 1, 2)
    for l in range(2):
        o[f"peer_q{l}"] = tiles(f["peer_w_q"][l])
        o[f"keys{l}"] = f["peer_sub_keys"][l].reshape(16, P, P).transpose(2, 0, 1)
        o[f"u{l}"] = f["peer_u"][l]
        o[f"v{l}"] = f["peer_v"][l]
    o["vecs"] = np.concatenate([cols(f[k].reshape(-1)) for k in (
        "norm1_g", "norm2_g", "final_norm_g", "mla_q_norm_g", "mla_kv_norm_g", "conv_b",
        "conv_ln_g", "conv_ln_b", "hg_norm_g")], axis=1)

    cst = np.zeros((P, C_END), np.float32)
    cst[:, C_ID:C_ID + P] = np.eye(P)
    s, q = np.arange(P)[:, None], np.arange(P)[None, :]
    same = s // CHUNK == q // CHUNK
    cst[:, C_MASK:C_MASK + P] = same & (s <= q)
    cst[:, C_MASK + P:C_MASK + 2 * P] = same & (s >= q)
    cst[:, C_IOTA:C_IOTA + TOPK] = np.arange(TOPK)
    tok = np.arange(T)
    inv = 10000.0 ** (-np.arange(0, ROPE // 2, 2, dtype=np.float64) / (ROPE // 2))
    ang = np.concatenate([(tok // 64)[:, None] * inv, (tok % 64)[:, None] * inv], axis=1).T
    cst[NOPE:QK, C_COS:C_COS + T] = np.repeat(np.cos(ang), 2, axis=0)
    sign = np.tile([-1.0, 1.0], ROPE // 2)[:, None]
    cst[NOPE:QK, C_SIN:C_SIN + T] = np.repeat(np.sin(ang), 2, axis=0) * sign
    o["consts"] = cst
    return {k: np.ascontiguousarray(v) for k, v in o.items()}


def kernel(**inputs):
    import numpy as np
    import concourse.bacc as bacc
    from concourse.bass_utils import run_bass_kernel_spmd

    arrays = host_arrays(inputs)
    nc = bacc.Bacc("TRN2", target_bir_lowering=False, num_devices=1)
    t = {k: nc.dram_tensor(k + "_dram", v.shape, mybir.dt.from_np(v.dtype), kind="ExternalInput").ap()
         for k, v in arrays.items()}
    out = nc.dram_tensor("out_dram", (P, KT, T), FP32, kind="ExternalOutput").ap()
    build(nc, t, out)
    r = run_bass_kernel_spmd(nc, [{k + "_dram": v for k, v in arrays.items()}], core_ids=[0])
    y = r.results[0]["out_dram"]
    return np.ascontiguousarray(np.asarray(y).transpose(2, 1, 0).reshape(1, T, D))
```

```python
import concourse.bass as bass
from concourse import mybir
from contextlib import ExitStack

FP32 = mybir.dt.float32
U32 = mybir.dt.uint32
ALU = mybir.AluOpType
ACT = mybir.ActivationFunctionType
AX = mybir.AxisListType.X

P = 128
D = 1024
KT = D // P
T = 256
N2 = 2 * T
EPS = 1e-6
MOD_TILES = 6 * KT
HEADS = 8
NOPE, ROPE, VDIM = 64, 32, 64
QK = NOPE + ROPE
MLA_SCALE = QK ** -0.5
CONV_T = 4
TAPS = 31
HALO = TAPS // 2
CHUNK = 64
TOPK = 16
RING = 4
SLOTS = 8
NEG = -3.0e38

C_ID, C_MASK, C_IOTA, C_COS, C_SIN, C_END = 0, 128, 384, 400, 656, 912


def wait_apart(eng, sem, value):
    if not isinstance(value, int):
        value = eng.to_reg(value)
        eng.wait_ge(sem, 1)
    eng.wait_ge(sem, value)


class Chain:

    def __init__(self, eng, sem, base=0):
        self.eng, self.sem, self.base, self.n = eng, sem, base, 0

    def __call__(self, ins):
        self.n += 1
        ins.then_inc(self.sem, 1)
        self.eng.wait_ge(self.sem, self.base + self.n)

    def apart(self, ins):
        self.n += 1
        ins.then_inc(self.sem, 1)
        wait_apart(self.eng, self.sem, self.base + self.n)


def build(nc, t, out, stop=None):
    with ExitStack() as whole:
        def sem(name):
            return whole.enter_context(nc.semaphore(name))

        def sb(name, shape, dt=FP32, ctx=whole):
            return ctx.enter_context(nc.sbuf_tensor(name, shape, dt))

        def ps(name, shape, ctx):
            return ctx.enter_context(nc.psum_tensor(name, shape, FP32))

        xT = sb("xT", [P, KT, N2])
        cst = sb("cst", [P, C_END])
        ones = sb("ones", [P, P])
        vecs = sb("vecs", [P, 128])
        modT = sb("modT", [P, 2, 6, KT, 2])
        gainT = sb("gainT", [P, 2, 2, KT, 2])
        wring = sb("wring", [P, RING, KT * P])
        ident = cst[:, C_ID:C_ID + P]

        V_N1, V_N2, V_FIN, V_QG, V_KVG, V_CB, V_LNG, V_LNB, V_HGN = 0, 16, 32, 40, 42, 43, 47, 51, 55

        w_loaded = [sem(f"w_loaded{j}") for j in range(RING)]
        acc_ready = sem("acc_ready")
        acc_free = sem("acc_free")
        lin = [("w_in", 12), ("w_out", 8), ("peer_q0", 16),
               ("hg_zz", 16), ("hg_qg", 16), ("hg_out", 8), ("peer_q1", 16)]
        first = {}
        g = 0
        for name, n in lin:
            first[name] = g
            g += n
        total_tiles = g

        def load_tile(sp, name, i, j, g):
            if not (isinstance(g, int) and g < RING):
                sp.wait_ge(acc_ready, g - (RING - 1))
            src = t[name][i] if isinstance(i, int) else \
                t[name][bass.ds(i, 1), :, :].rearrange("a p n -> p (a n)")
            sp.dma_start(wring[:, j, :], src).then_inc(w_loaded[j], 16)

        state = {"which": -1}

        def lin_loads(sp, which):
            name, n = lin[which]
            state["which"] = which
            g0 = first[name]
            if n > RING:
                with sp.Fori(0, n // RING - 1) as it:
                    for j in range(RING):
                        load_tile(sp, name, it * RING + (RING + j), j, it * RING + (g0 + RING + j))
            if which + 1 < len(lin):
                for j in range(RING):
                    load_tile(sp, lin[which + 1][0], j, j, g0 + n + j)

        def lin_matmuls(pe, which, psum, rhs, n_cols, after=None):
            name, n = lin[which]
            g0 = first[name]

            def trip(it):
                for j in range(RING):
                    pe.wait_ge(w_loaded[j], it * 16 + (g0 // RING + 1) * 16)
                    pe.wait_ge(acc_free, it * RING + (g0 + j + 1))
                    for k in range(KT):
                        last = nc.tensor.matmul(psum[:, j, 0:n_cols], wring[:, j, k * P:(k + 1) * P],
                                                rhs(k), start=(k == 0), stop=(k == KT - 1))
                    last.then_inc(acc_ready, 1)
                    if after:
                        after(it * RING + j)

            if after:
                for it in range(n // RING):
                    trip(it)
            else:
                with pe.Fori(0, n // RING) as it:
                    trip(it)

        def lin_evac(eng, which, one):
            name, n = lin[which]
            g0 = first[name]
            with eng.Fori(0, n // RING) as it:
                for j in range(RING):
                    eng.wait_ge(acc_ready, it * RING + (g0 + j + 1))
                    one(it * RING + j, j).then_inc(acc_free, 1)

        def lin_done(eng, which, tiles=None):
            name, n = lin[which]
            eng.wait_ge(acc_free, RING + first[name] + (tiles or n))

        s_xT, s_const, s_cond, s_sc, s_mod = sem("s_xT"), sem("s_const"), sem("s_cond"), sem("s_sc"), sem("s_mod")
        a_loaded = [sem(f"a_loaded{j}") for j in range(RING)]
        a_ready, a_copied, a_turned = sem("a_ready"), sem("a_copied"), sem("a_turned")
        GROUPS = 6 * D // 512
        FIRST = RING
        assert FIRST * 512 == 2 * D
        cond = ExitStack()
        scT = sb("scT", [P, KT, 2], ctx=cond)
        adab = sb("adab", [P, 2, MOD_TILES], ctx=cond)

        def mod_finish(chain, l, parts, columns):
            n0, n = parts[0] * KT, len(parts) * KT
            chain(nc.vector.tensor_tensor(modT[:, l].rearrange("p m k c -> p (m k) c")[:, n0:n0 + n], columns,
                                          adab[:, l, n0:n0 + n].unsqueeze(2).broadcast_to([P, n, 2]), ALU.add))
            for w in range(2):
                if 3 * w + 1 in parts:
                    gain = vecs[:, (V_N1, V_N2)[w] + 8 * l:][:, 0:8].unsqueeze(2).broadcast_to([P, KT, 2])
                    chain(nc.vector.scalar_tensor_tensor(
                        out=gainT[:, l, w], in0=modT[:, l, 3 * w + 1], scalar=1.0, in1=gain,
                        op0=ALU.add, op1=ALU.mult))

        def first_modulation(aw):
            with ExitStack() as c:
                rows = sb("rows", [P, FIRST, 512], ctx=c)
                pm = ps("pm", [P, FIRST, 512], c)
                pt = ps("pt", [P, 4 * FIRST, 2], c)
                block = c.enter_context(nc.Block())

                @block.sync
                def _(sp):
                    sp.dma_start(scT[:], t["cT"]).then_inc(s_cond, 16)
                    sp.dma_start(aw[:, 0, :], t["ada_w"][0]).then_inc(a_loaded[0], 16)
                    sp.dma_start(cst[:], t["consts"]).then_inc(s_const, 16)
                    sp.dma_start(vecs[:, 0:63], t["vecs"]).then_inc(s_const, 16)
                    sp.dma_start(adab[:].rearrange("p l n -> p (l n)"), t["ada_b"]).then_inc(s_const, 16)
                    for j in range(1, FIRST):
                        sp.dma_start(aw[:, j, :], t["ada_w"][j]).then_inc(a_loaded[j], 16)
                    sp.dma_start(xT[:], t["xT"]).then_inc(s_xT, 16)
                    for j in range(RING):
                        load_tile(sp, lin[0][0], j, j, j)
                    for j in range(FIRST):
                        sp.wait_ge(a_ready, j + 1)
                        sp.dma_start(aw[:, j, :], t["ada_w"][FIRST + j]).then_inc(a_loaded[j], 16)
                    sp.wait_ge(s_xT, 16)

                @block.gpsimd
                def _(pool):
                    nc.gpsimd.memset(ones[:], 1.0)

                @block.scalar
                def _(act):
                    act.wait_ge(s_cond, 16)
                    nc.scalar.activation(scT[:], scT[:], ACT.Silu).then_inc(s_sc, 1)

                @block.tensor
                def _(pe):
                    def turn(g):
                        pe.wait_ge(a_copied, g + 1)
                        for q in range(4):
                            last = nc.tensor.matmul(pt[:, 4 * g + q, :], rows[:, g, q * P:(q + 1) * P],
                                                    ident[:, 0:2], start=True, stop=True)
                        last.then_inc(a_turned, 1)

                    pe.wait_ge(s_sc, 1)
                    for g in range(FIRST):
                        pe.wait_ge(a_loaded[g], 16)
                        for k in range(KT):
                            last = nc.tensor.matmul(pm[0:2, g, :], scT[:, k, :], aw[:, g, k * 512:(k + 1) * 512],
                                                    start=(k == 0), stop=(k == KT - 1))
                        last.then_inc(a_ready, 1)
                        if g == 1:
                            pe.wait_ge(s_const, 48)
                        if g >= 1:
                            turn(g - 1)
                    turn(FIRST - 1)

                @block.vector
                def _(dve):
                    chain = Chain(dve, s_mod)
                    chain(nc.vector.memset(rows[:], 0.0))
                    dve.sem_inc(acc_free, RING)
                    for g in range(FIRST):
                        dve.wait_ge(a_ready, g + 1)
                        nc.vector.tensor_copy(rows[0:2, g, :], pm[0:2, g, :]).then_inc(a_copied, 1)
                    dve.wait_ge(a_turned, FIRST)
                    dve.wait_ge(s_const, 48)
                    mod_finish(chain, 0, (0, 1), pt[:])

        def done(name):
            if stop == name:
                with nc.Block() as block:
                    @block.sync
                    def _(sp):
                        nxt = lin[state["which"]] if state["which"] >= 0 else ("w_in", -0)
                        if state["which"] < 0:
                            nxt = ("w_in", 0)
                        for j in range(RING):
                            sp.wait_ge(w_loaded[j], (first[nxt[0]] + nxt[1] + RING) // RING * 16)
            return stop == name

        norms = {"done": 0}
        sq_ready, sum_ready, rs_ready, y_ready, root_ready = (sem(f"norm_{x}") for x in ("sq", "sum", "rs", "y", "root"))

        def norm_phase(tag, src, dst, cols, l, w):
            n = norms["done"]
            norms["done"] += 1
            with ExitStack() as c:
                sq = sb(f"{tag}_sqb", [P, KT, cols], ctx=c)
                rs = sb(f"{tag}_rsb", [P, cols], ctx=c)
                pn = ps(f"{tag}_pn", [P, 512], c)
                block = c.enter_context(nc.Block())

                def affine(eng, k):
                    for c2 in range(cols // T):
                        part = dst[:, k, c2 * T:(c2 + 1) * T]
                        if l is None:
                            a, b = vecs[:, V_FIN + k:V_FIN + k + 1], 0.0
                        else:
                            a, b = gainT[:, l, w, k, c2:c2 + 1], modT[:, l, 3 * w, k, c2:c2 + 1]
                        if eng is nc.scalar:
                            last = eng.activation(part, part, ACT.Identity, scale=a, bias=b)
                        elif l is None:
                            last = eng.tensor_scalar(part, part, a, None, ALU.mult)
                        else:
                            last = eng.tensor_scalar(part, part, a, b, ALU.mult, ALU.add)
                    return last

                @block.scalar
                def _(act):
                    for k in range(KT):
                        nc.scalar.activation(sq[:, k], src[:, k, 0:cols], ACT.Square).then_inc(sq_ready, 1)
                    act.wait_ge(rs_ready, 2 * n + 1)
                    nc.scalar.activation(rs[:], rs[:], ACT.Sqrt).then_inc(root_ready, 1)
                    for k in range(0, KT, 2):
                        act.wait_ge(y_ready, KT * n + k + 1)
                        affine(nc.scalar, k)

                @block.tensor
                def _(pe):
                    for k in range(KT):
                        pe.wait_ge(sq_ready, KT * n + k + 1)
                        last = nc.tensor.matmul(pn[:, 0:cols], ones[:], sq[:, k], start=(k == 0), stop=(k == KT - 1))
                    last.then_inc(sum_ready, 1)

                @block.vector
                def _(dve):
                    dve.wait_ge(sum_ready, n + 1)
                    nc.vector.tensor_scalar(rs[:], pn[:, 0:cols], 1.0 / D, EPS, ALU.mult, ALU.add).then_inc(rs_ready, 1)
                    dve.wait_ge(root_ready, n + 1)
                    nc.vector.reciprocal(rs[:], rs[:]).then_inc(rs_ready, 1)
                    dve.wait_ge(rs_ready, 2 * n + 2)
                    for k in range(KT):
                        nc.vector.tensor_tensor(dst[:, k, 0:cols], src[:, k, 0:cols], rs[:], ALU.mult).then_inc(y_ready, 1)
                        if k >= 1 and (k - 1) % 2 == 1:
                            dve.wait_ge(y_ready, KT * n + k)
                            affine(nc.vector, k - 1)
                    dve.wait_ge(y_ready, KT * (n + 1))
                    affine(nc.vector, KT - 1)

        def residual_evac(which, psum, cols, l, part):
            def one(i, j):
                for c2 in range(cols // T):
                    span = slice(c2 * T, (c2 + 1) * T)
                    last = nc.vector.scalar_tensor_tensor(
                        out=xT[:, bass.ds(i, 1), span], in0=psum[:, j:j + 1, span],
                        scalar=modT[:, l, part, bass.ds(i, 1), c2:c2 + 1].rearrange("p a c -> p (a c)"),
                        in1=xT[:, bass.ds(i, 1), span], op0=ALU.mult, op1=ALU.add)
                return last
            return one

        with ExitStack() as c0:
            mix = sb("mix", [P, KT, N2], ctx=c0)
            with ExitStack() as c1:
                cT = sb("cT", [P, 12, N2], ctx=c1)
                with ExitStack() as c:
                    hT = sb("hT0", [P, KT, N2], ctx=c)
                    aw = sb("aw", [P, RING, KT * 512], ctx=c)
                    first_modulation(aw)
                    if done("mod"):
                        return
                    norm_phase("n0", xT, hT, N2, 0, 0)
                    if done("n0"):
                        return
                    part = sb("mod_part", [P, RING, 2, 512], ctx=c)
                    pl = ps("pl0", [P, RING, 512], c)
                    pc = ps("pc0", [P, 4 * (GROUPS - FIRST), 2], c)
                    m_part, m_used, m_turned, m_fin = (sem(f"mod0_{x}") for x in ("part", "used", "turned", "fin"))
                    m_loaded = [sem(f"mod0_loaded{j}") for j in range(RING)]
                    later = range(FIRST, GROUPS)
                    block = c.enter_context(nc.Block())

                    @block.sync
                    def _(sp):
                        lin_loads(sp, 0)

                    @block.gpsimd
                    def _(pool):
                        for n, g in enumerate(later):
                            if n >= RING:
                                pool.wait_ge(m_used, n - RING + 1)
                                pool.dma_start(aw[:, n % RING, :], t["ada_w"][g]).then_inc(m_loaded[n % RING], 16)

                    @block.vector
                    def _(dve):
                        for n in range(len(later)):
                            if n < RING:
                                dve.wait_ge(a_loaded[n], 32)
                            else:
                                dve.wait_ge(m_loaded[n % RING], 16)
                            if n >= RING:
                                dve.wait_ge(m_turned, n - RING + 1)
                            for k in range(KT):
                                for x in range(2):
                                    w, to = aw[:, n % RING, k * 512:(k + 1) * 512], part[:, n % RING, x, :]
                                    if k == 0:
                                        ins = nc.vector.tensor_scalar(to, w, scT[:, k, x:x + 1], None, ALU.mult)
                                    else:
                                        dve.wait_ge(m_part, (n * KT + k - 1) * 2 + x + 1)
                                        ins = nc.vector.scalar_tensor_tensor(out=to, in0=w, scalar=scT[:, k, x:x + 1],
                                                                             in1=to, op0=ALU.mult, op1=ALU.add)
                                    ins.then_inc(m_part, 1)
                            dve.wait_ge(m_part, (n + 1) * KT * 2)
                            dve.sem_inc(m_used, 1)
                        dve.wait_ge(m_turned, len(later))
                        mod_finish(Chain(dve, m_fin), 0, (2, 3, 4, 5), pc[:])

                    @block.tensor
                    def _(pe):
                        def turn(i):
                            n = i - 3
                            if 0 <= n < len(later):
                                pe.wait_ge(m_used, n + 1)
                                for q in range(4):
                                    for x in range(2):
                                        last = nc.tensor.matmul(pc[:, 4 * n + q, x:x + 1],
                                                                part[:, n % RING, x, q * P:(q + 1) * P],
                                                                ones[:, 0:1], start=True, stop=True)
                                last.then_inc(m_turned, 1)

                        lin_matmuls(pe, 0, pl, lambda k: hT[:, k, :], N2, after=turn)

                    @block.scalar
                    def _(act):
                        lin_evac(act, 0, lambda i, j: nc.scalar.copy(cT[:, bass.ds(i, 1), :], pl[:, j:j + 1, :]))
                if done("w_in"):
                    return
                mla_phase(nc, t, sem, sb, ps, cT, mix, cst, vecs, ones, ident,
                          (V_QG, V_KVG, V_CB, V_LNG, V_LNB), scT, mod_finish, done)
                if done("mla") or done("proj"):
                    return
            with ExitStack() as c:
                pl = ps("pl1", [P, RING, 512], c)
                block = c.enter_context(nc.Block())

                @block.sync
                def _(sp):
                    lin_loads(sp, 1)

                @block.tensor
                def _(pe):
                    lin_matmuls(pe, 1, pl, lambda k: mix[:, k, :], N2)

                @block.vector
                def _(dve):
                    lin_evac(dve, 1, residual_evac(1, pl, N2, 0, 2))
        cond.close()
        if done("l0mix"):
            return

        u_loaded = [sem(f"u_loaded{j}") for j in range(SLOTS)]
        v_loaded = [sem(f"v_loaded{j}") for j in range(SLOTS)]

        def peer_layer(l, cols):
            which = {0: 2, 1: 6}[l]
            peer_phase(nc, t, sem, sb, ps, xT, modT, cst, ident, l, cols, norm_phase, lin_loads, first[lin[which][0]],
                       w_loaded, wring, acc_ready, acc_free, which, u_loaded, v_loaded, l * HEADS * N2 // P)

        peer_layer(0, N2)
        if done("peer0"):
            return

        hgrn_phase(nc, t, sem, sb, ps, xT, modT, cst, vecs, ones, ident, norm_phase, lin_loads,
                   lin_matmuls, lin_evac, lin_done, residual_evac, V_HGN, done)
        if done("hgrn_p") or done("hgrn"):
            return
        peer_layer(1, T)

        s_out = sem("s_out")
        with ExitStack() as c:
            yT = sb("yT", [P, KT, T], ctx=c)
            norm_phase("nf", xT, yT, T, None, None)
            block = c.enter_context(nc.Block())

            @block.sync
            def _(sp):
                sp.dma_start(out, yT[:]).then_inc(s_out, 16)
                sp.wait_ge(s_out, 16)


def mla_phase(nc, t, sem, sb, ps, cT, mix, cst, vecs, ones, ident, cols, scT, mod_finish, done):
    V_QG, V_KVG, V_CB, V_LNG, V_LNB = cols
    rope_rows = slice(NOPE, QK)
    with ExitStack() as c:
        Q = sb("Q", [QK, HEADS, N2], ctx=c)
        K = sb("K", [QK, HEADS, N2], ctx=c)
        V = sb("V", [P, 4, HEADS * VDIM], ctx=c)
        gated = sb("gated", [P, CONV_T, 2, T + 2 * HALO], ctx=c)
        convw = sb("convw", [P, CONV_T, TAPS], ctx=c)
        GROUPS = 6 * D // 512
        aw = sb("aw1", [P, 2, KT * 512], ctx=c)
        rows = sb("rows1", [P, 2, 512], ctx=c)
        m1_loaded = [sem(f"m1_loaded{j}") for j in range(2)]
        m1_ready, m1_copied, m1_turned, m1_done = (sem(f"m1_{x}") for x in ("ready", "copied", "turned", "done"))
        s_w = sem("mla_w")
        s_act, s_pe, s_dve, s_pool = sem("mla_act"), sem("mla_pe"), sem("mla_dve"), sem("mla_pool")
        s_q, s_qe, s_k, s_ke, s_v, s_ve = (sem(f"mla_{x}") for x in ("q", "qe", "k", "ke", "v", "ve"))

        with ExitStack() as c2:
            wuq = sb("wuq", [P, 2, HEADS * P], ctx=c2)
            wuk = sb("wuk", [P, HEADS * NOPE], ctx=c2)
            wuv = sb("wuv", [P, HEADS * VDIM], ctx=c2)
            lat = sb("lat", [P, 3, N2], ctx=c2)
            rs = sb("lat_rs", [P, 2, N2], ctx=c2)
            QS = sb("QS", [QK, HEADS, T], ctx=c2)
            KS = sb("KS", [QK, N2], ctx=c2)
            KR = sb("KR", [QK, N2], ctx=c2)
            pn = ps("mla_pn", [P, 2, 512], c2)
            pq = ps("mla_pq", [P, 3, 512], c2)
            pk = ps("mla_pk", [P, 3, 512], c2)
            block = c2.enter_context(nc.Block())

            @block.sync
            def _(sp):
                sp.dma_start(wuq[:], t["w_uq"]).then_inc(s_w, 16)
                sp.dma_start(wuk[:], t["w_uk"]).then_inc(s_w, 16)
                sp.dma_start(wuv[:], t["w_uv"]).then_inc(s_w, 16)
                sp.dma_start(convw[:], t["conv_w"]).then_inc(s_w, 16)
                for j in range(2):
                    sp.dma_start(aw[:, j, :], t["ada_w"][GROUPS + j]).then_inc(m1_loaded[j], 16)

            @block.gpsimd
            def _(pool):
                nc.gpsimd.memset(rows[:], 0.0)
                nc.gpsimd.memset(gated[:], 0.0).then_inc(s_pool, 1)

            @block.scalar
            def _(act):
                nc.scalar.activation(lat[:], cT[:, 0:3, :], ACT.Square).then_inc(s_act, 1)
                nc.scalar.copy(KS[rope_rows, 0:T], cT[QK:P, 3, 0:T]).then_inc(s_act, 1)
                act.wait_ge(s_dve, 2)
                nc.scalar.activation(rs[:], rs[:], ACT.Sqrt).then_inc(s_act, 1)
                for h in range(HEADS):
                    act.wait_ge(s_q, h + 1)
                    nc.scalar.copy(Q[:, h, :], pq[0:QK, h % 3, :])
                    nc.scalar.copy(QS[rope_rows, h, :], pq[QK:P, h % 3, 0:T]).then_inc(s_qe, 1)
                for m in range(4):
                    act.wait_ge(s_v, m + 1)
                    nc.scalar.copy(V[:, m, :], pq[:, (HEADS + m) % 3, :]).then_inc(s_qe, 1)

            @block.tensor
            def _(pe):
                pe.wait_ge(s_act, 1)
                for k in range(2):
                    nc.tensor.matmul(pn[:, 0, :], ones[:], lat[:, k, :], start=(k == 0), stop=(k == 1))
                nc.tensor.matmul(pn[:, 1, :], ones[:], lat[:, 2, :], start=True, stop=True).then_inc(s_pe, 1)
                pe.wait_ge(s_w, 64)
                pe.wait_ge(s_dve, 6)
                for h in range(HEADS):
                    if h >= 3:
                        pe.wait_ge(s_qe, h - 2)
                    for k in range(2):
                        last = nc.tensor.matmul(pq[:, h % 3, :], wuq[:, k, h * P:(h + 1) * P], lat[:, k, :],
                                                start=(k == 0), stop=(k == 1))
                    last.then_inc(s_q, 1)
                    if h >= 3:
                        pe.wait_ge(s_ke, h - 2)
                    nc.tensor.matmul(pk[0:NOPE, h % 3, :], wuk[:, h * NOPE:(h + 1) * NOPE], lat[:, 2, :],
                                     start=True, stop=True).then_inc(s_k, 1)
                for m in range(4):
                    pe.wait_ge(s_qe, HEADS + m - 2)
                    nc.tensor.matmul(pq[:, (HEADS + m) % 3, :], lat[:, 2, m * P:(m + 1) * P], wuv[:],
                                     start=True, stop=True).then_inc(s_v, 1)

            @block.vector
            def _(dve):
                chain = Chain(dve, s_dve)
                dve.wait_ge(s_pe, 1)
                chain(nc.vector.tensor_scalar(rs[:, 0], pn[:, 0], 1.0 / 256, EPS, ALU.mult, ALU.add))
                chain(nc.vector.tensor_scalar(rs[:, 1], pn[:, 1], 1.0 / 128, EPS, ALU.mult, ALU.add))
                dve.wait_ge(s_act, 3)
                chain(nc.vector.reciprocal(rs[:], rs[:]))
                for k in range(3):
                    chain(nc.vector.scalar_tensor_tensor(
                        out=lat[:, k], in0=cT[:, k], scalar=vecs[:, V_QG + k:V_QG + k + 1],
                        in1=rs[:, k // 2], op0=ALU.mult, op1=ALU.mult))
                cos, sin = cst[rope_rows, C_COS:C_COS + T], cst[rope_rows, C_SIN:C_SIN + T]
                kr = cT[rope_rows, 3, 0:T]
                chain(nc.vector.tensor_tensor(KR[rope_rows, 0:T], kr, cos, ALU.mult))
                chain(nc.vector.tensor_tensor(KS[rope_rows, 0:T], KS[rope_rows, 0:T], sin, ALU.mult))
                chain(nc.vector.tensor_tensor(KR[rope_rows, 0:T], KR[rope_rows, 0:T], KS[rope_rows, 0:T], ALU.add))
                chain(nc.vector.tensor_copy(KR[rope_rows, T:N2], cT[rope_rows, 3, T:N2]))
                nc.vector.tensor_copy(K[rope_rows], KR[rope_rows, :].unsqueeze(1).broadcast_to([ROPE, HEADS, N2]))
                for h in range(HEADS):
                    dve.wait_ge(s_k, h + 1)
                    nc.vector.tensor_copy(K[0:NOPE, h, :], pk[0:NOPE, h % 3, :]).then_inc(s_ke, 1)
                dve.wait_ge(s_qe, HEADS)
                bc = [ROPE, HEADS, T]
                qx = Q[rope_rows, :, 0:T]
                chain(nc.vector.tensor_tensor(qx, qx, cos.unsqueeze(1).broadcast_to(bc), ALU.mult))
                chain(nc.vector.tensor_tensor(QS[rope_rows], QS[rope_rows], sin.unsqueeze(1).broadcast_to(bc), ALU.mult))
                chain(nc.vector.tensor_tensor(qx, qx, QS[rope_rows], ALU.add))
        if done("proj"):
            return

        O = sb("O", [P, 4, HEADS * VDIM], ctx=c)
        conv = sb("conv", [P, CONV_T, 2, T], ctx=c)
        with ExitStack() as c2:
            prob = sb("prob", [P, 2, N2], ctx=c2)
            probT = sb("probT", [P, 2, 4, P], ctx=c2)
            sg = sb("sg", [P, CONV_T, 2, T], ctx=c2)
            nmx = sb("nmx", [P, 2], ctx=c2)
            den = sb("den", [P, 2], ctx=c2)
            rden = sb("rden", [P, 2], ctx=c2)
            pS = ps("pS", [P, 2, 512], c2)
            pT = ps("pT", [P, 2, 4, P], c2)
            pO = ps("pO", [P, 2, 512], c2)
            pm = ps("pm1", [P, 2, 512], c2)
            turned = pO[:, 0, 256:256 + 8 * GROUPS].rearrange("p (n c) -> p n c", c=2)
            at = {x: sem(f"att_{x}") for x in ("s", "mx", "nmx", "exp", "t", "copied", "o", "rd", "norm", "sg", "gated", "conv")}
            block = c2.enter_context(nc.Block())
            units = [(m, h) for m in range(4) for h in range(HEADS)]
            copied_at = [-(-KT * (g + 1) // 3) for g in range(GROUPS)]
            turned_at = [u + 1 + (u + 1) % 2 for u in copied_at]

            def keys(m):
                return (0, 4) if m < 2 else (2, 4)

            @block.sync
            def _(sp):
                for g in range(2, GROUPS):
                    sp.wait_ge(m1_ready, g - 1)
                    sp.dma_start(aw[:, g % 2, :], t["ada_w"][GROUPS + g]).then_inc(m1_loaded[g % 2], 16)

            @block.tensor
            def _(pe):
                def modulation(x):
                    g, k = x // KT, x % KT
                    if g < GROUPS:
                        if k == 0:
                            pe.wait_ge(m1_loaded[g % 2], (g // 2 + 1) * 16)
                            if g >= 2:
                                pe.wait_ge(m1_copied, g - 1)
                        last = nc.tensor.matmul(pm[0:2, g % 2, :], scT[:, k, :], aw[:, g % 2, k * 512:(k + 1) * 512],
                                                start=(k == 0), stop=(k == KT - 1))
                        if k == KT - 1:
                            last.then_inc(m1_ready, 1)

                def turn(g):
                    pe.wait_ge(m1_copied, g + 1)
                    for q in range(4):
                        last = nc.tensor.matmul(turned[:, g * 4 + q, :], rows[:, g % 2, q * P:(q + 1) * P],
                                                ident[:, 0:2], start=True, stop=True)
                    last.then_inc(m1_turned, 1)

                for u in range(len(units) + 2):
                    modulation(3 * u)
                    if u < len(units):
                        m, h = units[u]
                        lo, hi = keys(m)
                        if u >= 2:
                            pe.wait_ge(at["exp"], u - 1)
                        nc.tensor.matmul(pS[:, u % 2, lo * P:hi * P], Q[:, h, m * P:(m + 1) * P],
                                         K[:, h, lo * P:hi * P], start=True, stop=True).then_inc(at["s"], 1)
                    modulation(3 * u + 1)
                    if 1 <= u <= len(units):
                        v = u - 1
                        lo, hi = keys(units[v][0])
                        pe.wait_ge(at["exp"], v + 1)
                        if v >= 2:
                            pe.wait_ge(at["copied"], v - 1)
                        for j in range(lo, hi):
                            last = nc.tensor.transpose(pT[:, v % 2, j, :], prob[:, v % 2, j * P:(j + 1) * P], ident)
                        last.then_inc(at["t"], 1)
                    modulation(3 * u + 2)
                    if u >= 2:
                        v = u - 2
                        m, h = units[v]
                        lo, hi = keys(m)
                        pe.wait_ge(at["copied"], v + 1)
                        if v >= 2:
                            pe.wait_ge(at["norm"], v - 1)
                        if u in turned_at:
                            turn(turned_at.index(u))
                        for j in range(lo, hi):
                            last = nc.tensor.matmul(pO[:, v % 2, 0:VDIM], probT[:, v % 2, j, :],
                                                    V[:, j, h * VDIM:(h + 1) * VDIM], start=(j == lo), stop=(j == hi - 1))
                        last.then_inc(at["o"], 1)
                pe.wait_ge(at["norm"], len(units))
                turn(GROUPS - 1)

            @block.scalar
            def _(act):
                nc.scalar.activation(sg[:].rearrange("p a b n -> p (a b n)"),
                                     cT[:, 8:12, :].rearrange("p a n -> p (a n)"), ACT.Sigmoid).then_inc(at["sg"], 1)
                for u in range(len(units) + 1):
                    if u < len(units):
                        lo, hi = keys(units[u][0])
                        act.wait_ge(at["nmx"], u + 1)
                        if u >= 2:
                            act.wait_ge(at["t"], u - 1)
                            act.wait_ge(at["rd"], u - 1)
                        nc.scalar.activation(prob[:, u % 2, lo * P:hi * P], pS[:, u % 2, lo * P:hi * P], ACT.Exp,
                                             bias=nmx[:, u % 2:u % 2 + 1], scale=MLA_SCALE,
                                             accum_out=den[:, u % 2:u % 2 + 1]).then_inc(at["exp"], 1)
                    if u >= 1:
                        v = u - 1
                        lo, hi = keys(units[v][0])
                        act.wait_ge(at["t"], v + 1)
                        if v >= 2:
                            act.wait_ge(at["o"], v - 1)
                        nc.scalar.copy(probT[:, v % 2, lo:hi, :], pT[:, v % 2, lo:hi, :]).then_inc(at["copied"], 1)
                    if u in copied_at:
                        g = copied_at.index(u)
                        act.wait_ge(m1_ready, g + 1)
                        if g >= 2:
                            act.wait_ge(m1_turned, g - 1)
                        nc.scalar.copy(rows[0:2, g % 2, :], pm[0:2, g % 2, :]).then_inc(m1_copied, 1)

            @block.vector
            def _(dve):
                dve.wait_ge(at["sg"], 1)
                for i in range(CONV_T):
                    nc.vector.tensor_tensor(gated[:, i, :, HALO:HALO + T],
                                            cT[:, 4 + i, :].rearrange("p (s n) -> p s n", s=2),
                                            sg[:, i], ALU.mult).then_inc(at["gated"], 1)
                dve.wait_ge(at["gated"], CONV_T)
                for u in range(len(units) + 2):
                    if u < len(units):
                        lo, hi = keys(units[u][0])
                        dve.wait_ge(at["s"], u + 1)
                        if u >= 2:
                            dve.wait_ge(at["exp"], u - 1)
                        nc.vector.reduce_max(nmx[:, u % 2:u % 2 + 1], pS[:, u % 2, lo * P:hi * P], AX).then_inc(at["mx"], 1)
                        dve.wait_ge(at["mx"], u + 1)
                        nc.vector.tensor_scalar(nmx[:, u % 2:u % 2 + 1], nmx[:, u % 2:u % 2 + 1],
                                                -MLA_SCALE, None, ALU.mult).then_inc(at["nmx"], 1)
                    if u < TAPS:
                        for i in range(CONV_T):
                            src, w = gated[:, i, :, u:u + T], convw[:, i, u:u + 1]
                            if u == 0:
                                nc.vector.tensor_scalar(conv[:, i], src, w, vecs[:, V_CB + i:V_CB + i + 1],
                                                        ALU.mult, ALU.add).then_inc(at["conv"], 1)
                            else:
                                dve.wait_ge(at["conv"], CONV_T * (u - 1) + i + 1)
                                nc.vector.scalar_tensor_tensor(out=conv[:, i], in0=src, scalar=w, in1=conv[:, i],
                                                               op0=ALU.mult, op1=ALU.add).then_inc(at["conv"], 1)
                    if u >= 2:
                        v = u - 2
                        m, h = units[v]
                        dve.wait_ge(at["exp"], v + 1)
                        nc.vector.reciprocal(rden[:, v % 2:v % 2 + 1], den[:, v % 2:v % 2 + 1]).then_inc(at["rd"], 1)
                        dve.wait_ge(at["o"], v + 1)
                        dve.wait_ge(at["rd"], v + 1)
                        nc.vector.tensor_scalar(O[:, m, h * VDIM:(h + 1) * VDIM], pO[:, v % 2, 0:VDIM],
                                                rden[:, v % 2:v % 2 + 1], None, ALU.mult).then_inc(at["norm"], 1)
                dve.wait_ge(m1_turned, GROUPS)
                mod_finish(Chain(dve, m1_done), 1, range(6), turned)
        if done("att"):
            return

        with ExitStack() as c2:
            sq = sb("conv_sq", [P, CONV_T, N2], ctx=c2)
            rs = sb("conv_rs", [P, N2], ctx=c2)
            pOT = ps("pOT", [P, 4, 512], c2)
            pL = ps("pL", [P, 2, 512], c2)
            ot, ln_pe, ln_dve, ln_act = sem("ot"), sem("ln_pe"), sem("ln_dve"), sem("ln_act")
            cv = conv[:].rearrange("p c s n -> p c (s n)")
            block = c2.enter_context(nc.Block())

            @block.tensor
            def _(pe):
                for i in range(CONV_T):
                    last = nc.tensor.matmul(pL[:, 0], ones[:], cv[:, i], start=(i == 0), stop=(i == CONV_T - 1))
                last.then_inc(ln_pe, 1)
                for k in range(4):
                    for m in range(4):
                        last = nc.tensor.transpose(pOT[:, k, m * P:(m + 1) * P], O[:, m, k * P:(k + 1) * P], ident)
                    last.then_inc(ot, 1)
                for i in range(CONV_T):
                    pe.wait_ge(ln_act, i + 1)
                    last = nc.tensor.matmul(pL[:, 1], ones[:], sq[:, i], start=(i == 0), stop=(i == CONV_T - 1))
                last.then_inc(ln_pe, 1)

            @block.vector
            def _(dve):
                chain = Chain(dve, ln_dve)
                dve.wait_ge(ln_pe, 1)
                for i in range(CONV_T):
                    chain(nc.vector.scalar_tensor_tensor(out=cv[:, i], in0=pL[:, 0], scalar=-1.0 / 512,
                                                         in1=cv[:, i], op0=ALU.mult, op1=ALU.add))
                dve.wait_ge(ln_pe, 2)
                chain(nc.vector.tensor_scalar(rs[:], pL[:, 1], 1.0 / 512, EPS, ALU.mult, ALU.add))
                dve.wait_ge(ln_act, CONV_T + 1)
                chain(nc.vector.reciprocal(rs[:], rs[:]))
                for i in range(CONV_T):
                    chain(nc.vector.tensor_tensor(cv[:, i], cv[:, i], rs[:], ALU.mult))
                for k in range(4):
                    dve.wait_ge(ot, k + 1)
                    nc.vector.tensor_copy(mix[:, k, :], pOT[:, k, :])

            @block.scalar
            def _(act):
                for i in range(CONV_T):
                    act.wait_ge(ln_dve, i + 1)
                    nc.scalar.activation(sq[:, i], cv[:, i], ACT.Square).then_inc(ln_act, 1)
                act.wait_ge(ln_dve, CONV_T + 1)
                nc.scalar.activation(rs[:], rs[:], ACT.Sqrt).then_inc(ln_act, 1)
                for i in range(CONV_T):
                    act.wait_ge(ln_dve, CONV_T + 3 + i)
                    nc.scalar.activation(mix[:, 4 + i, :], cv[:, i], ACT.Silu, scale=vecs[:, V_LNG + i:V_LNG + i + 1],
                                         bias=vecs[:, V_LNB + i:V_LNB + i + 1])


def peer_phase(nc, t, sem, sb, ps, xT, modT, cst, ident, l, cols, norm_phase, lin_loads, g0, w_loaded,
               wring, acc_ready, acc_free, which, u_loaded, v_loaded, steps_before):
    blocks = cols // P
    steps = blocks * HEADS
    TRIPS = HEADS // 2
    with ExitStack() as c:
        Y = sb(f"Y_{l}", [P, blocks, D], ctx=c)
        with ExitStack() as c2:
            hT = sb(f"h2T_{l}", [P, KT, cols], ctx=c2)
            norm_phase(f"np{l}", xT, hT, cols, l, 1)
            H2 = sb(f"H2_{l}", [P, blocks, D], ctx=c2)
            qT = sb(f"qT_{l}", [P, 2, cols], ctx=c2)
            keys = sb(f"keys_{l}", [P, 2 * HEADS, P], ctx=c2)
            S = [sb(f"S{l}_{e}", [P, blocks, 2, P], ctx=c2) for e in range(2)]
            U = [sb(f"U{l}_{j}", [P, D], ctx=c2) for j in range(SLOTS)]
            Vr = [sb(f"V{l}_{j}", [P, D], ctx=c2) for j in range(SLOTS)]
            diag = sb(f"diag{l}", [P, TOPK, P], ctx=c2)
            junk = sb(f"junk{l}", [P, 2, D], ctx=c2)
            rest = sb(f"rest{l}", [P, 2, P], ctx=c2)
            sv = sb(f"sv{l}", [P, 2, TOPK], ctx=c2)
            si = sb(f"si{l}", [P, 2, TOPK], U32, ctx=c2)
            sif = sb(f"sif{l}", [P, 2, TOPK], ctx=c2)
            cand = sb(f"cand{l}", [P, TOPK, TOPK], ctx=c2)
            cand2 = sb(f"cand2{l}", [P, TOPK, TOPK], ctx=c2)
            top = [sb(f"top{l}_{e}", [P, TOPK], ctx=c2) for e in range(2)]
            pos = sb(f"pos{l}", [P, TOPK], U32, ctx=c2)
            pij = sb(f"pij{l}", [P, 2, TOPK], U32, ctx=c2)
            pf = sb(f"pf{l}", [P, 2, TOPK], ctx=c2)
            hot = sb(f"hot{l}", [P, 2, TOPK, TOPK], ctx=c2)
            e2 = sb(f"e2{l}", [P, 2, TOPK], ctx=c2)
            idx = [sb(f"idx{l}_{e}", [P, TOPK], U32, ctx=c2) for e in range(2)]
            mine = [sb(f"mine{l}_{e}", [P, TOPK], U32, ctx=c2) for e in range(2)]
            nmax = [sb(f"nmax{l}_{e}", [P, 1], ctx=c2) for e in range(2)]
            ex = [sb(f"ex{l}_{e}", [P, TOPK], ctx=c2) for e in range(2)]
            den = [sb(f"pden{l}_{e}", [P, 1], ctx=c2) for e in range(2)]
            rden = sb(f"prden{l}", [P, 1], ctx=c2)
            dots = sb(f"dots{l}", [P, TOPK], ctx=c2)
            act_t = sb(f"actt{l}", [P, TOPK], ctx=c2)
            coef = sb(f"coef{l}", [P, TOPK], ctx=c2)
            pY = ps(f"pY{l}", [P, D], c2)
            pq = ps(f"pq{l}", [P, 2, 512], c2)
            psc = ps(f"psc{l}", [P, blocks, 2, P], c2)
            ptr = ps(f"ptr{l}", [P, 2, 512], c2)
            iota = cst[:, C_IOTA:C_IOTA + TOPK]
            s_keys, s_tr, s_tre, s_sc, s_sce, s_zero = (sem(f"p{l}_{x}") for x in ("keys", "tr", "tre", "sc", "sce", "zero"))
            s_idx, s_gelu, s_coef, s_diag, s_y, s_u, s_v, s_exp, s_ch, s_taken = (
                sem(f"p{l}_{x}") for x in ("idx", "gelu", "coef", "diag", "y", "ufree", "vfree", "exp", "chain", "taken"))
            TOPK_LINKS, STEP_LINKS = 24, 26
            block = c2.enter_context(nc.Block())

            if blocks == 4:
                beside = {0: ("q0",), 1: ("q1",), 2: ("scores",), 3: ()}
            else:
                beside = {0: ("q0", "q1", "scores"), 1: ()}

            def trips(eng, body):
                with eng.Fori(0, TRIPS - 1) as p:
                    body(p, False)
                body(TRIPS - 1, True)

            def trip_steps(p, last):
                for hh in range(2):
                    for b in range(blocks):
                        yield p * (2 * blocks) + (hh * blocks + b), hh, b, last and hh == 1 and b == blocks - 1

            @block.sync
            def _(sp):
                sp.dma_start(keys[:], t[f"keys{l}"]).then_inc(s_keys, 16)
                lin_loads(sp, which)

            def pe_prepare(pe, part, p, n):
                if part == "scores":
                    pe.wait_ge(acc_free, p * RING + (RING + g0 + 2 * n + 2))
                    if not (isinstance(p, int) and p * 2 + n == 0):
                        pe.wait_ge(s_sce, p * 2 + n)
                    for b in range(blocks):
                        for i in range(2):
                            last = nc.tensor.matmul(psc[:, b, i, :], qT[:, i, b * P:(b + 1) * P],
                                                    keys[:, bass.ds(p * 4 + (2 * n + i), 1), :].rearrange("p a n -> p (a n)"),
                                                    start=True, stop=True)
                    last.then_inc(s_sc, 1)
                else:
                    i = ("q0", "q1").index(part)
                    j = 2 * n + i
                    pe.wait_ge(w_loaded[j % RING], p * 16 + (g0 // RING + j // RING + 1) * 16)
                    pe.wait_ge(acc_free, p * RING + (RING + g0 + j - 1))
                    for k in range(KT):
                        last = nc.tensor.matmul(pq[:, i, 0:cols], wring[:, j % RING, k * P:(k + 1) * P], hT[:, k, :],
                                                start=(k == 0), stop=(k == KT - 1))
                    last.then_inc(acc_ready, 1)

            def act_prepare(act, part, p, n):
                if part == "scores":
                    act.wait_ge(s_sc, p * 2 + (n + 1))
                    nc.scalar.copy(S[n % 2][:], psc[:]).then_inc(s_sce, 1)
                else:
                    i = ("q0", "q1").index(part)
                    act.wait_ge(acc_ready, p * RING + (g0 + 2 * n + i + 1))
                    nc.scalar.copy(qT[:, i, :], pq[:, i, 0:cols]).then_inc(acc_free, 1)

            def topk(chain, scores, e):
                v = nc.vector
                for h in range(2):
                    chain.apart(v.max(out=sv[:, h, 0:8], in_=scores[:, h]))
                    chain.apart(v.max_index(out=si[:, h, 0:8], in_max=sv[:, h, 0:8], in_values=scores[:, h]))
                    chain.apart(v.match_replace(out=rest[:, h], in_to_replace=sv[:, h, 0:8], in_values=scores[:, h], imm_value=NEG))
                    chain.apart(v.max(out=sv[:, h, 8:16], in_=rest[:, h]))
                    chain.apart(v.max_index(out=si[:, h, 8:16], in_max=sv[:, h, 8:16], in_values=rest[:, h]))
                chain.apart(v.tensor_tensor(cand[:], sv[:, 0, :].unsqueeze(2).broadcast_to([P, TOPK, TOPK]),
                                      sv[:, 1, :].unsqueeze(1).broadcast_to([P, TOPK, TOPK]), ALU.add))
                cf, cf2 = (x[:].rearrange("p a b -> p (a b)") for x in (cand, cand2))
                chain.apart(v.max(out=top[e][:, 0:8], in_=cf))
                chain.apart(v.max_index(out=pos[:, 0:8], in_max=top[e][:, 0:8], in_values=cf))
                chain.apart(v.match_replace(out=cf2, in_to_replace=top[e][:, 0:8], in_values=cf, imm_value=NEG))
                chain.apart(v.max(out=top[e][:, 8:16], in_=cf2))
                chain.apart(v.max_index(out=pos[:, 8:16], in_max=top[e][:, 8:16], in_values=cf2))
                chain(v.tensor_scalar(nmax[e][:], top[e][:, 0:1], -1.0, None, ALU.mult))
                chain(v.tensor_scalar(pij[:, 0], pos[:], 4, None, ALU.logical_shift_right))
                chain(v.tensor_scalar(pij[:, 1], pos[:], TOPK - 1, None, ALU.bitwise_and))
                chain(v.tensor_copy(pf[:], pij[:]))
                chain(v.tensor_copy(sif[:], si[:]))
                q4 = [P, 2, TOPK, TOPK]
                chain(v.tensor_tensor(hot[:], pf[:].unsqueeze(3).broadcast_to(q4),
                                      iota.unsqueeze(1).unsqueeze(1).broadcast_to(q4), ALU.is_equal))
                chain(v.tensor_tensor(hot[:], hot[:], sif[:].unsqueeze(2).broadcast_to(q4), ALU.mult))
                chain(v.tensor_reduce(e2[:], hot[:], AX, ALU.add))
                v.scalar_tensor_tensor(out=idx[e][:], in0=e2[:, 0], scalar=float(P), in1=e2[:, 1],
                                       op0=ALU.mult, op1=ALU.add).then_inc(s_idx, 1)

            def dots_of(dve, b, s):
                for k in range(TOPK):
                    j = k % SLOTS
                    dve.wait_ge(u_loaded[j], s * 32 + (steps_before * 32 + (k // SLOTS + 1) * 16))
                    dve.wait_ge(s_u, s * TOPK + (SLOTS + k - 1))
                    nc.vector.scalar_tensor_tensor(
                        out=junk[:, k % 2], in0=U[j][:], scalar=1.0, in1=H2[:, b, :],
                        op0=ALU.mult, op1=ALU.mult, accum_out=dots[:, k:k + 1]).then_inc(s_u, 1)

            @block.vector
            def _(dve):
                chain = Chain(dve, s_ch)
                dve.sem_inc(s_u, SLOTS)
                chain(nc.vector.memset(pY[:, 0:512], 0.0))
                chain(nc.vector.memset(pY[:, 512:D], 0.0))
                dve.sem_inc(s_y, 1)
                dve.wait_ge(s_sce, 1)
                topk(chain, S[0][:, 0], 0)
                assert chain.n == 2 + TOPK_LINKS, chain.n
                dve.wait_ge(s_zero, 1)
                dve.wait_ge(s_tre, 2 * blocks)

                def trip(p, last):
                    for s, hh, b, final in trip_steps(p, last):
                        e = b % 2
                        chain = Chain(dve, s_ch, s * STEP_LINKS + (2 + TOPK_LINKS))
                        if not final:
                            if b == blocks - 1:
                                wait_apart(dve, s_sce, p * 2 + (hh + 2))
                            wait_apart(dve, s_taken, s + 1)
                            topk(chain, S[(hh + (b + 1) // blocks) % 2][:, (b + 1) % blocks], 1 - e)
                        dots_of(dve, b, s)
                        dve.wait_ge(s_y, s + 1)
                        yb = Y[:, (b - 1) % blocks, :]
                        chain(nc.vector.tensor_tensor(yb, yb, pY[:], ALU.add))
                        dve.wait_ge(s_exp, s + 1)
                        chain(nc.vector.reciprocal(rden[:], den[e][:]))
                        assert final or chain.n == STEP_LINKS, chain.n
                        dve.wait_ge(s_gelu, s + 1)
                        nc.vector.scalar_tensor_tensor(out=coef[:], in0=act_t[:], scalar=rden[:, 0:1], in1=ex[e][:],
                                                       op0=ALU.mult, op1=ALU.mult).then_inc(s_coef, 1)

                trips(dve, trip)
                dve.wait_ge(s_y, steps + 1)
                nc.vector.tensor_tensor(Y[:, blocks - 1, :], Y[:, blocks - 1, :], pY[:], ALU.add)

            @block.gpsimd
            def _(pool):
                nc.gpsimd.memset(Y[:], 0.0).then_inc(s_zero, 1)
                pool.sem_inc(s_taken, 1)
                with pool.Fori(0, steps // 2) as p:
                    for e in range(2):
                        s = p * 2 + e
                        wait_apart(pool, s_idx, s + 1)
                        nc.gpsimd.tensor_copy(mine[e][:], idx[e][:]).then_inc(s_taken, 1)
                        wait_apart(pool, s_taken, s + 2)
                        for k in range(TOPK):
                            wait_apart(pool, s_u, s * TOPK + (k + 1))
                            nc.gpsimd.indirect_dma_start(
                                out=U[k % SLOTS][:], out_offset=None, in_=t[f"u{l}"],
                                in_offset=bass.IndirectOffsetOnAxis(ap=mine[e][:, k:k + 1], axis=0)
                            ).then_inc(u_loaded[k % SLOTS], 16)
                        for k in range(TOPK):
                            wait_apart(pool, s_v, s * TOPK + (k + 1))
                            nc.gpsimd.indirect_dma_start(
                                out=Vr[k % SLOTS][:], out_offset=None, in_=t[f"v{l}"],
                                in_offset=bass.IndirectOffsetOnAxis(ap=mine[e][:, k:k + 1], axis=0)
                            ).then_inc(v_loaded[k % SLOTS], 16)

            @block.scalar
            def _(act):
                def exponentials(s, e):
                    act.wait_ge(s_idx, s + 1)
                    nc.scalar.activation(ex[e][:], top[e][:], ACT.Exp, bias=nmax[e][:], accum_out=den[e][:]).then_inc(s_exp, 1)

                for part in ("q0", "q1", "scores"):
                    act_prepare(act, part, 0, 0)
                for n in range(2 * blocks):
                    act.wait_ge(s_tr, n + 1)
                    nc.scalar.copy(H2[:, n // 2, (n % 2) * 512:(n % 2 + 1) * 512], ptr[:, n % 2, :]).then_inc(s_tre, 1)
                exponentials(0, 0)

                def trip(p, last):
                    for s, hh, b, final in trip_steps(p, last):
                        if not final:
                            exponentials(s + 1, 1 - b % 2)
                        if not (last and hh == 1):
                            for part in beside[b]:
                                act_prepare(act, part, p, hh + 1)
                        act.wait_ge(s_u, s * TOPK + (TOPK + SLOTS))
                        nc.scalar.activation(act_t[:], dots[:], ACT.Gelu).then_inc(s_gelu, 1)
                        act.wait_ge(s_coef, s + 1)
                        for k in range(TOPK):
                            nc.scalar.activation(diag[:, k, :], ident, ACT.Copy, scale=coef[:, k:k + 1]).then_inc(s_diag, 1)

                trips(act, trip)

            @block.tensor
            def _(pe):
                pe.sem_inc(s_v, SLOTS)
                pe_prepare(pe, "q0", 0, 0)
                pe_prepare(pe, "q1", 0, 0)
                pe.wait_ge(s_keys, 16)
                pe_prepare(pe, "scores", 0, 0)
                for n in range(2 * blocks):
                    if n >= 2:
                        pe.wait_ge(s_tre, n - 1)
                    for k in range(4):
                        last = nc.tensor.transpose(ptr[:, n % 2, k * P:(k + 1) * P],
                                                   hT[:, 4 * (n % 2) + k, (n // 2) * P:(n // 2 + 1) * P], ident)
                    last.then_inc(s_tr, 1)

                def trip(p, last_trip):
                    for s, hh, b, final in trip_steps(p, last_trip):
                        if not (last_trip and hh == 1):
                            for part in beside[b]:
                                pe_prepare(pe, part, p, hh + 1)
                        for k in range(TOPK):
                            j = k % SLOTS
                            pe.wait_ge(s_diag, s * TOPK + (k + 1))
                            pe.wait_ge(v_loaded[j], s * 32 + (steps_before * 32 + (k // SLOTS + 1) * 16))
                            for half in range(2):
                                last = nc.tensor.matmul(pY[:, half * 512:(half + 1) * 512], diag[:, k, :],
                                                        Vr[j][:, half * 512:(half + 1) * 512],
                                                        start=(k == 0), stop=(k == TOPK - 1))
                            last.then_inc(s_v, 1)
                        pe.wait_ge(s_v, s * TOPK + (TOPK + SLOTS))
                        pe.sem_inc(s_y, 1)

                trips(pe, trip)

        with ExitStack() as c2:
            pt = ps(f"pt{l}", [P, 4, 512], c2)
            s_t, s_r = sem(f"p{l}_t"), sem(f"p{l}_r")
            block = c2.enter_context(nc.Block())

            @block.tensor
            def _(pe):
                for k in range(KT):
                    if k >= 4:
                        pe.wait_ge(s_r, k - 3)
                    for b in range(blocks):
                        last = nc.tensor.transpose(pt[:, k % 4, b * P:(b + 1) * P], Y[:, b, k * P:(k + 1) * P], ident)
                    last.then_inc(s_t, 1)

            @block.vector
            def _(dve):
                for k in range(KT):
                    dve.wait_ge(s_t, k + 1)
                    for c2_ in range(cols // T):
                        span = slice(c2_ * T, (c2_ + 1) * T)
                        last = nc.vector.scalar_tensor_tensor(out=xT[:, k, span], in0=pt[:, k % 4, span],
                                                              scalar=modT[:, l, 5, k, c2_:c2_ + 1], in1=xT[:, k, span],
                                                              op0=ALU.mult, op1=ALU.add)
                    last.then_inc(s_r, 1)


def hgrn_phase(nc, t, sem, sb, ps, xT, modT, cst, vecs, ones, ident, norm_phase, lin_loads, lin_matmuls,
               lin_evac, lin_done, residual_evac, V_HGN, done):
    CTX_CHUNKS = N2 // CHUNK // 2
    ORDER = ([4, 5, 6, 7, 0, 1, 2, 3], [7, 6, 5, 4, 3, 2, 1, 0])
    with ExitStack() as c:
        QG = sb("QG", [P, 2 * HEADS, T], ctx=c)
        OT = QG[:, 0:HEADS, :]
        with ExitStack() as c1:
            F = sb("F", [P, 2 * HEADS, N2], ctx=c1)
            KK = sb("KK", [P, 2 * HEADS, N2], ctx=c1)
            VI = sb("VI", [P, 4, D], ctx=c1)
            bs = sb("bs", [P, 2 * HEADS, N2], ctx=c1)
            kout = F
            two = range(2)
            halves = [slice(d * HEADS, (d + 1) * HEADS) for d in two]

            def flat(x, d):
                return x[:, halves[d], :].rearrange("p h n -> p (h n)")

            def chunks(x, d):
                return x[:, halves[d], :].rearrange("p h (c n) -> p (h c) n", n=CHUNK)

            def last_col(d):
                at = (CHUNK - 1) * (1 - d)
                return chunks(bs, d)[:, :, at:at + 1]

            with ExitStack() as c2:
                hT = sb("h1T", [P, KT, N2], ctx=c2)
                norm_phase("n1", xT, hT, N2, 1, 0)
                wi = sb("wi", [P, KT, 512], ctx=c2)
                starts = sb("starts", [P, N2], mybir.dt.bfloat16, ctx=c2)
                lb = sb("lb", [P, 2, 2 * KT], ctx=c2)
                mx = sb("lbmx", [P, 2 * KT], ctx=c2)
                low = sb("low", [P, 2 * KT], ctx=c2)
                room = sb("room", [P, 2 * KT], ctx=c2)
                pl = ps("plh", [P, RING, 512], c2)
                pi = ps("pi", [P, 2, 512], c2)
                s_w, s_wi, s_lb, s_e, s_i, s_ie, s_ln = (sem(f"hg_{x}") for x in ("w", "wi", "lb", "e", "i", "ie", "ln"))
                block = c2.enter_context(nc.Block())

                @block.sync
                def _(sp):
                    sp.dma_start(lb[:].rearrange("p l k -> p (l k)"),
                                 t["hg_lb"].rearrange("p l d k -> p (l d k)")).then_inc(s_w, 16)
                    sp.dma_start(wi[:], t["hg_i"][:, :, 0:512]).then_inc(s_wi, 16)
                    lin_loads(sp, 3)
                    sp.wait_ge(s_i, 4)
                    sp.dma_start(wi[:], t["hg_i"][:, :, 512:D]).then_inc(s_wi, 16)
                    lin_loads(sp, 4)

                @block.tensor
                def _(pe):
                    def values(half):
                        pe.wait_ge(s_wi, 16 * (half + 1))
                        for m in range(4):
                            n = 4 * half + m
                            if n >= 2:
                                pe.wait_ge(s_ie, n - 1)
                            for k in range(KT):
                                last = nc.tensor.matmul(pi[:, n % 2, :], hT[:, k, m * P:(m + 1) * P], wi[:, k, :],
                                                        start=(k == 0), stop=(k == KT - 1))
                            last.then_inc(s_i, 1)

                    lin_matmuls(pe, 3, pl, lambda k: hT[:, k, :], N2)
                    values(0)
                    lin_matmuls(pe, 4, pl, lambda k: hT[:, k, 0:T], T)
                    values(1)

                @block.scalar
                def _(act):
                    act.wait_ge(s_lb, 2)
                    nc.scalar.activation(lb[:], lb[:], ACT.Exp).then_inc(s_e, 1)
                    lin_evac(act, 3, lambda i, j: nc.scalar.activation(F[:, bass.ds(i, 1), :], pl[:, j:j + 1, :], ACT.Sigmoid))
                    for d in two:
                        act.wait_ge(s_lb, 8 + 2 * HEADS * (d + 1))
                        nc.scalar.activation(flat(F, d), flat(F, d), ACT.Ln).then_inc(s_ln, 1)

                    def values_evac(half):
                        for m in range(4):
                            act.wait_ge(s_i, 4 * half + m + 1)
                            nc.scalar.copy(VI[:, m, half * 512:(half + 1) * 512],
                                           pi[:, m % 2, :]).then_inc(s_ie, 1)

                    values_evac(0)
                    lin_evac(act, 4, lambda i, j: nc.scalar.copy(QG[:, bass.ds(i, 1), :], pl[:, j:j + 1, 0:T]))
                    lin_done(act, 4)
                    nc.scalar.activation(QG[:, HEADS:], QG[:, HEADS:], ACT.Silu)
                    values_evac(1)

                @block.vector
                def _(dve):
                    chain = Chain(dve, s_lb)
                    v = nc.vector
                    dve.wait_ge(s_w, 16)
                    chain(v.tensor_tensor(mx[:], lb[:, 0], lb[:, 1], ALU.max))
                    chain(v.tensor_tensor(lb[:], lb[:], mx[:].unsqueeze(1).broadcast_to([P, 2, 2 * KT]), ALU.subtract))
                    dve.wait_ge(s_e, 1)
                    chain(v.tensor_tensor(mx[:], lb[:, 0], lb[:, 1], ALU.add))
                    chain(v.reciprocal(mx[:], mx[:]))
                    chain(v.tensor_tensor(lb[:], lb[:], mx[:].unsqueeze(1).broadcast_to([P, 2, 2 * KT]), ALU.mult))
                    chain(v.tensor_tensor(low[:], lb[:, 0], lb[:, 1], ALU.add))
                    chain(v.tensor_tensor(low[:], low[:], lb[:, 0], ALU.subtract))
                    chain(v.tensor_scalar(room[:], low[:], -1.0, 1.0, ALU.mult, ALU.add))
                    for i in range(2 * HEADS):
                        lin_done(dve, 3, i + 1)
                        chain(v.tensor_scalar(F[:, i], F[:, i], room[:, i:i + 1], low[:, i:i + 1], ALU.mult, ALU.add))
                        chain(v.tensor_scalar(KK[:, i], F[:, i], -1.0, 1.0, ALU.mult, ALU.add))
                    chain(v.memset(starts[:], 1.0))
                    chain(v.memset(starts[:].rearrange("p (c n) -> p c n", n=CHUNK)[:, :, 0:1], 0.0))
                    for d in two:
                        dve.wait_ge(s_ln, d + 1)
                        way = slice(None) if d == 0 else slice(None, None, -1)
                        for i in range(d * HEADS, (d + 1) * HEADS):
                            last = v.tensor_tensor_scan(bs[:, i, way], starts[:], F[:, i, way], 0.0, ALU.mult, ALU.add)
                        chain(last)
                        chain(v.tensor_tensor(chunks(F, d), last_col(d).broadcast_to([P, HEADS * 8, CHUNK]),
                                              chunks(bs, d), ALU.subtract))
            if done("hgrn_p"):
                return

            with ExitStack() as c2:
                AHEAD = 2
                qin = sb("qin", [P, 2 + AHEAD, 2, T], ctx=c2)
                kin = sb("kin", [P, 1 + AHEAD, 2, T], ctx=c2)
                dec = sb("dec", [P, 2 * HEADS, 8], ctx=c2)
                koT = [[sb(f"koT{e}{d}", [P, 4, P], ctx=c2) for d in two] for e in two]
                AM = [[sb(f"AM{e}{d}", [P, 2, P], ctx=c2) for d in two] for e in two]
                ST = [[sb(f"ST{e}{d}", [P, 7, P], ctx=c2) for d in two] for e in two]
                pK = [ps(f"pK{d}", [P, 4, P], c2) for d in two]
                pA = ps("pA", [P, 2, 2, P], c2)
                pD = [[ps(f"pD{d}{x}", [P, 4, P], c2) for x in two] for d in two]
                pO = ps("pOh", [P, 512], c2)
                s = {x: sem(f"gla_{x}") for x in ("zero", "pt", "kot", "pa", "am", "ds", "c", "o", "oc", "ex", "qk", "kin", "dec")}
                block = c2.enter_context(nc.Block())

                @block.gpsimd
                def _(pool):
                    for e in two:
                        for d in two:
                            nc.gpsimd.memset(AM[e][d][:], 0.0).then_inc(s["zero"], 1)
                    for h in range(HEADS):
                        x = h % (1 + AHEAD)
                        pool.wait_ge(s["ex"], h + 1)
                        nc.gpsimd.tensor_tensor(kin[:, x], kin[:, x], KK[:, h::HEADS, 0:T], ALU.mult).then_inc(s["kin"], 1)

                @block.scalar
                def _(act):
                    def exponentials(h):
                        x = h % (2 + AHEAD)
                        if h >= 2 + AHEAD:
                            act.wait_ge(s["o"], h - AHEAD - 1)
                        nc.scalar.activation(qin[:, x], bs[:, h::HEADS, 0:T], ACT.Exp)
                        if h >= 1 + AHEAD:
                            act.wait_ge(s["pa"], h - AHEAD)
                        nc.scalar.activation(kin[:, h % (1 + AHEAD)], bs[:, h::HEADS, 0:T], ACT.Exp, scale=-1.0)
                        nc.scalar.activation(F[:, h::HEADS, :], F[:, h::HEADS, :], ACT.Exp).then_inc(s["ex"], 1)

                    for h in range(AHEAD):
                        exponentials(h)
                    for d in two:
                        nc.scalar.activation(dec[:, halves[d], :].rearrange("p h c -> p (h c)").unsqueeze(2),
                                             last_col(d), ACT.Exp).then_inc(s["dec"], 1)
                    for h in range(HEADS + 1):
                        if h + AHEAD < HEADS:
                            exponentials(h + AHEAD)
                        if h < HEADS:
                            for d in two:
                                act.wait_ge(s["pt"], 2 * h + d + 1)
                                if h >= 2:
                                    act.wait_ge(s["ds"], 2 * (h - 2) + d + 1)
                                nc.scalar.copy(koT[h % 2][d][:], pK[d][:]).then_inc(s["kot"], 1)
                        if h >= 1:
                            act.wait_ge(s["o"], h)
                            nc.scalar.copy(OT[:, h - 1], pO[:, 0:T]).then_inc(s["oc"], 1)

                @block.vector
                def _(dve):
                    v = nc.vector
                    chain = Chain(dve, s["c"])
                    masks = cst[:, C_MASK:C_MASK + 2 * P].rearrange("p (d n) -> p d n", d=2).bitcast(U32)

                    def queries_keys(h):
                        dve.wait_ge(s["ex"], h + 1)
                        x = h % (2 + AHEAD)
                        v.tensor_tensor(F[:, h::HEADS, :], F[:, h::HEADS, :], KK[:, h::HEADS, :], ALU.mult)
                        v.tensor_tensor(qin[:, x], qin[:, x], QG[:, h, :].unsqueeze(1).broadcast_to([P, 2, T]),
                                        ALU.mult).then_inc(s["qk"], 1)

                    for h in range(AHEAD):
                        queries_keys(h)
                    dve.wait_ge(s["zero"], 4)
                    dve.wait_ge(s["dec"], 2)
                    for h in range(HEADS):
                        e = h % 2
                        dve.wait_ge(s["pa"], h + 1)
                        if h >= 2:
                            dve.wait_ge(s["o"], h - 1)
                        for d in two:
                            v.copy_predicated(AM[e][d][:], masks[:, d, :].unsqueeze(1).broadcast_to([P, 2, P]),
                                              pA[:, d]).then_inc(s["am"], 1)
                        if h + AHEAD < HEADS:
                            queries_keys(h + AHEAD)
                        for i in range(7):
                            for d in two:
                                ch = ORDER[d][i]
                                own = pD[d][ch % 2][:, ch // 2, :]
                                if i == 0:
                                    dve.wait_ge(s["ds"], 2 * h + d + 1)
                                    ins = v.tensor_copy(ST[e][d][:, 0], own)
                                else:
                                    dve.wait_ge(s["c"], 14 * h + 2 * (i - 1) + d + 1)
                                    ins = v.scalar_tensor_tensor(out=ST[e][d][:, i], in0=ST[e][d][:, i - 1],
                                                                 scalar=dec[:, d * HEADS + h, ch:ch + 1], in1=own,
                                                                 op0=ALU.mult, op1=ALU.add)
                                ins.then_inc(s["c"], 1)

                @block.tensor
                def _(pe):
                    def turn(h):
                        pe.wait_ge(s["qk"], h + 1)
                        for d in two:
                            if h >= 1:
                                pe.wait_ge(s["kot"], 2 * (h - 1) + d + 1)
                            for m in range(4):
                                last = nc.tensor.transpose(pK[d][:, m, :], kout[:, d * HEADS + h, m * P:(m + 1) * P], ident)
                            last.then_inc(s["pt"], 1)

                    def output(h):
                        e = h % 2
                        if h >= 1:
                            pe.wait_ge(s["oc"], h)
                        pe.wait_ge(s["am"], 2 * h + 2)
                        for d in two:
                            for m in two:
                                nc.tensor.matmul(pO[:, m * P:(m + 1) * P], VI[:, m, h * P:(h + 1) * P], AM[e][d][:, m, :],
                                                 start=(d == 0 and m == 0), stop=False, skip_group_check=True)
                        pe.wait_ge(s["c"], 14 * (h + 1))
                        for d in two:
                            for i in range(4):
                                ch = ORDER[d][CTX_CHUNKS + i]
                                cols = slice(ch * CHUNK, (ch + 1) * CHUNK)
                                last = nc.tensor.matmul(pO[:, cols], ST[e][d][:, 3 + i, :], qin[:, h % (2 + AHEAD), d, cols],
                                                        start=False, stop=(d == 1 and i == 3), skip_group_check=True)
                        last.then_inc(s["o"], 1)

                    turn(0)
                    for h in range(HEADS):
                        pe.wait_ge(s["kin"], h + 1)
                        if h >= 1:
                            pe.wait_ge(s["am"], 2 * h)
                        for d in two:
                            for m in two:
                                last = nc.tensor.matmul(pA[:, d, m, :], kin[:, h % (1 + AHEAD), d, m * P:(m + 1) * P],
                                                        qin[:, h % (2 + AHEAD), d, m * P:(m + 1) * P], start=True, stop=True)
                        last.then_inc(s["pa"], 1)
                        if h >= 1:
                            pe.wait_ge(s["c"], 14 * h)
                        for d in two:
                            pe.wait_ge(s["kot"], 2 * h + d + 1)
                            for i in range(7):
                                ch = ORDER[d][i]
                                rows = slice(CHUNK * (ch % 2), CHUNK * (ch % 2 + 1))
                                last = nc.tensor.matmul(pD[d][ch % 2][:, ch // 2, :], koT[h % 2][d][rows, ch // 2, :],
                                                        VI[rows, ch // 2, h * P:(h + 1) * P], start=True, stop=True)
                            last.then_inc(s["ds"], 1)
                        if h + 1 < HEADS:
                            turn(h + 1)
                        if h >= 1:
                            output(h - 1)
                    output(HEADS - 1)
        if done("gla"):
            return

        with ExitStack() as c1:
            sq = sb("osq", [P, HEADS, T], ctx=c1)
            rs = sb("ors", [P, HEADS, T], ctx=c1)
            pR = ps("pR", [P, HEADS, T], c1)
            pl = ps("plo", [P, RING, 512], c1)
            r_act, r_pe, r_dve = sem("r_act"), sem("r_pe"), sem("r_dve")
            block = c1.enter_context(nc.Block())

            @block.sync
            def _(sp):
                lin_loads(sp, 5)

            @block.scalar
            def _(act):
                for h in range(HEADS):
                    nc.scalar.activation(sq[:, h], OT[:, h], ACT.Square).then_inc(r_act, 1)
                act.wait_ge(r_dve, 1)
                nc.scalar.activation(rs[:], rs[:], ACT.Sqrt).then_inc(r_act, 1)

            @block.vector
            def _(dve):
                chain = Chain(dve, r_dve)
                dve.wait_ge(r_pe, 1)
                chain(nc.vector.tensor_scalar(rs[:], pR[:], 1.0 / P, EPS, ALU.mult, ALU.add))
                dve.wait_ge(r_act, HEADS + 1)
                chain(nc.vector.reciprocal(rs[:], rs[:]))
                chain(nc.vector.tensor_tensor(rs[:], rs[:], OT, ALU.mult))
                for h in range(HEADS):
                    chain(nc.vector.scalar_tensor_tensor(out=OT[:, h], in0=rs[:, h], scalar=vecs[:, V_HGN + h:V_HGN + h + 1],
                                                         in1=QG[:, HEADS + h], op0=ALU.mult, op1=ALU.mult))
                lin_evac(dve, 5, residual_evac(5, pl, T, 1, 2))

            @block.tensor
            def _(pe):
                for h in range(HEADS):
                    pe.wait_ge(r_act, h + 1)
                    last = nc.tensor.matmul(pR[:, h], ones[:], sq[:, h], start=True, stop=True)
                last.then_inc(r_pe, 1)
                pe.wait_ge(r_dve, 3 + HEADS)
                lin_matmuls(pe, 5, pl, lambda k: OT[:, k, :], T)

def host_arrays(a):
    import numpy as np
    f = {k: np.asarray(v) for k, v in a.items()}

    def tiles(w):
        K, N = w.shape
        return np.ascontiguousarray(w.reshape(K // P, P, N // P, P).transpose(2, 1, 0, 3).reshape(N // P, P, -1))

    def cols(v):
        return v.reshape(-1, P).T

    def swapped(w):
        return w.reshape(w.shape[0], -1, 2)[:, :, ::-1].reshape(w.shape)

    o = {}
    o["xT"] = np.concatenate([f["x"][0], f["ctx"][0]], axis=0).T.reshape(KT, P, N2).transpose(1, 0, 2)
    o["cT"] = np.stack([f["c"][0], f["c_ctx"]], axis=1).reshape(KT, P, 2).transpose(1, 0, 2)
    o["ada_w"] = f["ada_w"].reshape(2, KT, P, 12, 512).transpose(0, 3, 2, 1, 4).reshape(24, P, KT * 512)
    o["ada_b"] = cols(f["ada_b"].reshape(-1))
    w = f["ab_w_in"][0]
    kr = w[:, 384:416]
    o["w_in"] = tiles(np.concatenate([w[:, :384], w[:, 320:384], kr, swapped(kr), w[:, 416:]], axis=1))
    wq = f["mla_w_uq"][0].reshape(256, HEADS, QK)
    rope = wq[:, :, NOPE:]
    wq = np.concatenate([wq, rope.reshape(256, HEADS, ROPE // 2, 2)[..., ::-1].reshape(256, HEADS, ROPE)], axis=2)
    o["w_uq"] = wq.reshape(2, P, HEADS * P).transpose(1, 0, 2)
    wkv = f["mla_w_ukv"][0].reshape(P, HEADS, NOPE + VDIM)
    o["w_uk"] = wkv[:, :, :NOPE].reshape(P, -1)
    o["w_uv"] = wkv[:, :, NOPE:].reshape(P, -1)
    o["conv_w"] = f["conv_w"][0].reshape(TAPS, CONV_T, P).transpose(2, 1, 0)
    o["w_out"] = tiles(f["ab_w_out"][0])
    hg = f["hg_w_in"][0]
    o["hg_zz"] = tiles(hg[:, 1024:3072])
    o["hg_qg"] = tiles(np.concatenate([hg[:, 0:1024], hg[:, 4096:5120]], axis=1))
    o["hg_i"] = hg[:, 3072:4096].reshape(KT, P, D).transpose(1, 0, 2)
    o["hg_out"] = tiles(f["hg_w_out"][0])
    o["hg_lb"] = f["hg_lower_bound"].reshape(2, 2, KT, P).transpose(3, 0, 1, 2)
    for l in range(2):
        o[f"peer_q{l}"] = tiles(f["peer_w_q"][l])
        o[f"keys{l}"] = f["peer_sub_keys"][l].reshape(16, P, P).transpose(2, 0, 1)
        o[f"u{l}"] = f["peer_u"][l]
        o[f"v{l}"] = f["peer_v"][l]
    o["vecs"] = np.concatenate([cols(f[k].reshape(-1)) for k in (
        "norm1_g", "norm2_g", "final_norm_g", "mla_q_norm_g", "mla_kv_norm_g", "conv_b",
        "conv_ln_g", "conv_ln_b", "hg_norm_g")], axis=1)

    cst = np.zeros((P, C_END), np.float32)
    cst[:, C_ID:C_ID + P] = np.eye(P)
    s, q = np.arange(P)[:, None], np.arange(P)[None, :]
    same = s // CHUNK == q // CHUNK
    cst[:, C_MASK:C_MASK + P] = same & (s <= q)
    cst[:, C_MASK + P:C_MASK + 2 * P] = same & (s >= q)
    cst[:, C_IOTA:C_IOTA + TOPK] = np.arange(TOPK)
    tok = np.arange(T)
    inv = 10000.0 ** (-np.arange(0, ROPE // 2, 2, dtype=np.float64) / (ROPE // 2))
    ang = np.concatenate([(tok // 64)[:, None] * inv, (tok % 64)[:, None] * inv], axis=1).T
    cst[NOPE:QK, C_COS:C_COS + T] = np.repeat(np.cos(ang), 2, axis=0)
    sign = np.tile([-1.0, 1.0], ROPE // 2)[:, None]
    cst[NOPE:QK, C_SIN:C_SIN + T] = np.repeat(np.sin(ang), 2, axis=0) * sign
    o["consts"] = cst
    return {k: np.ascontiguousarray(v) for k, v in o.items()}


def kernel(**inputs):
    import numpy as np
    import concourse.bacc as bacc
    from concourse.bass_utils import run_bass_kernel_spmd

    arrays = host_arrays(inputs)
    nc = bacc.Bacc("TRN2", target_bir_lowering=False, num_devices=1)
    t = {k: nc.dram_tensor(k + "_dram", v.shape, mybir.dt.from_np(v.dtype), kind="ExternalInput").ap()
         for k, v in arrays.items()}
    out = nc.dram_tensor("out_dram", (P, KT, T), FP32, kind="ExternalOutput").ap()
    build(nc, t, out)
    r = run_bass_kernel_spmd(nc, [{k + "_dram": v for k, v in arrays.items()}], core_ids=[0])
    y = r.results[0]["out_dram"]
    return np.ascontiguousarray(np.asarray(y).transpose(2, 1, 0).reshape(1, T, D))
```
